# Optimizing a Trainium2 kernel written in Bass

```python
import math
import jax, jax.numpy as jnp
from jax import lax
import numpy as np

D_MODEL = 1024
BATCH = 1
SEQ = 2048
DEPTH = 1

CONV_WIDTH = D_MODEL // 2
CONV_KERNEL = 31
SSM_WIDTH = D_MODEL // 2
SSM_GROUP = 16
SSM_GROUPS = SSM_WIDTH // SSM_GROUP
SSM_STATE = 64
FFN_HIDDEN = ((8 * D_MODEL + 3 * 256 - 1) // (3 * 256)) * 256
IN_COLS = 2 * CONV_WIDTH + SSM_WIDTH + 2 * D_MODEL
N_MOD = 6
EPS = 1e-6
DT_MIN = 1e-3
DT_MAX = 1e-1

kernel_name = "hybrid_conv_s5_gated_block"

def rmsnorm(x, g):
    x32 = x.astype(jnp.float32)
    y = x32 * lax.rsqrt(jnp.mean(x32 * x32, axis=-1, keepdims=True) + EPS)
    return (y * g.astype(jnp.float32)).astype(x.dtype)

def layernorm(x, g, b):
    x32 = x.astype(jnp.float32)
    mu = jnp.mean(x32, axis=-1, keepdims=True)
    var = jnp.mean(jnp.square(x32 - mu), axis=-1, keepdims=True)
    y = (x32 - mu) * lax.rsqrt(var + EPS)
    return (y * g.astype(jnp.float32) + b.astype(jnp.float32)).astype(x.dtype)

def conformer_conv(u_glu, conv_w, conv_b, ln_g, ln_b, w_proj):
    a, gate = jnp.split(u_glu, 2, axis=-1)
    u = a * jax.nn.sigmoid(gate)
    y = lax.conv_general_dilated(
        u, conv_w[:, None, :].astype(u.dtype), window_strides=(1,),
        padding=[(CONV_KERNEL - 1, 0)],
        dimension_numbers=("NWC", "WIO", "NWC"),
        feature_group_count=CONV_WIDTH) + conv_b
    y = jax.nn.silu(layernorm(y, ln_g, ln_b))
    return y @ w_proj

def _scan_combine(e1, e2):
    a1r, a1i, b1r, b1i = e1
    a2r, a2i, b2r, b2i = e2
    ar = a2r * a1r - a2i * a1i
    ai = a2r * a1i + a2i * a1r
    br = a2r * b1r - a2i * b1i + b2r
    bi = a2r * b1i + a2i * b1r + b2i
    return (ar, ai, br, bi)

def s5_mixer(u, a_re, a_im, b_re, b_im, c_re, c_im, d, log_dt, w_glu):
    bsz, seq, _ = u.shape
    f32 = jnp.float32
    u32 = u.astype(f32).reshape(bsz, seq, SSM_GROUPS, SSM_GROUP)
    ar, ai = a_re.astype(f32), a_im.astype(f32)
    dt = jnp.exp(log_dt.astype(f32))[:, None]
    mag = jnp.exp(dt * ar)
    e_re, e_im = mag * jnp.cos(dt * ai), mag * jnp.sin(dt * ai)
    n_re, n_im = e_re - 1.0, e_im
    den = ar * ar + ai * ai
    q_re = (n_re * ar + n_im * ai) / den
    q_im = (n_im * ar - n_re * ai) / den
    br32, bi32 = b_re.astype(f32), b_im.astype(f32)
    bb_re = q_re[..., None] * br32 - q_im[..., None] * bi32
    bb_im = q_re[..., None] * bi32 + q_im[..., None] * br32
    bu_re = jnp.einsum("bsgh,gph->bsgp", u32, bb_re)
    bu_im = jnp.einsum("bsgh,gph->bsgp", u32, bb_im)
    abar_re = jnp.broadcast_to(e_re, bu_re.shape)
    abar_im = jnp.broadcast_to(e_im, bu_re.shape)
    _, _, x_re, x_im = lax.associative_scan(
        _scan_combine, (abar_re, abar_im, bu_re, bu_im), axis=1)
    y = (jnp.einsum("bsgp,ghp->bsgh", x_re, c_re.astype(f32))
         - jnp.einsum("bsgp,ghp->bsgh", x_im, c_im.astype(f32)))
    y = y.reshape(bsz, seq, SSM_WIDTH) + d.astype(f32) * u.astype(f32)
    y = jax.nn.gelu(y).astype(u.dtype)
    za, zb = jnp.split(y @ w_glu, 2, axis=-1)
    return za * jax.nn.sigmoid(zb)

def setup_inputs(seed: int = 0) -> dict:
    key = jax.random.key(seed)
    ks = jax.random.split(key, 32)
    f32 = jnp.float32
    L, D, G, P, H = DEPTH, D_MODEL, SSM_GROUPS, SSM_STATE, SSM_GROUP

    def nrm(k, shape, fan_in):
        return jax.random.normal(k, shape, f32) * fan_in ** -0.5

    def gain(k, shape):
        return 1.0 + 0.05 * jax.random.normal(k, shape, f32)

    n_idx = jnp.arange(P, dtype=f32)
    a_re = -0.5 + 0.01 * jax.random.normal(ks[8], (L, G, P), f32)
    a_im = math.pi * n_idx[None, None, :] + 0.01 * jax.random.normal(ks[9], (L, G, P), f32)
    log_dt = jax.random.uniform(ks[10], (L, G), f32, math.log(DT_MIN), math.log(DT_MAX))
    return {
        "x": jax.random.normal(ks[0], (BATCH, SEQ, D), f32),
        "c": jax.random.normal(ks[1], (BATCH, D), f32),
        "w_ada": nrm(ks[2], (L, D, N_MOD * D), D) * 0.5,
        "b_ada": 0.02 * jax.random.normal(ks[3], (L, N_MOD * D), f32),
        "norm1_g": gain(ks[4], (L, D)),
        "w_in": nrm(ks[5], (L, D, IN_COLS), D),
        "conv_w": nrm(ks[6], (L, CONV_KERNEL, CONV_WIDTH), CONV_KERNEL),
        "conv_b": 0.02 * jax.random.normal(ks[7], (L, CONV_WIDTH), f32),
        "conv_ln_g": gain(ks[11], (L, CONV_WIDTH)),
        "conv_ln_b": 0.02 * jax.random.normal(ks[12], (L, CONV_WIDTH), f32),
        "conv_proj": nrm(ks[13], (L, CONV_WIDTH, D), CONV_WIDTH),
        "ssm_a_re": a_re,
        "ssm_a_im": a_im,
        "ssm_b_re": nrm(ks[14], (L, G, P, H), 2 * H),
        "ssm_b_im": nrm(ks[15], (L, G, P, H), 2 * H),
        "ssm_c_re": nrm(ks[16], (L, G, H, P), P),
        "ssm_c_im": nrm(ks[17], (L, G, H, P), P),
        "ssm_d": jax.random.normal(ks[18], (L, SSM_WIDTH), f32),
        "ssm_log_dt": log_dt,
        "ssm_glu": nrm(ks[19], (L, SSM_WIDTH, 2 * D), SSM_WIDTH),
        "w_out": nrm(ks[20], (L, D, D), D),
        "norm2_g": gain(ks[21], (L, D)),
        "w_ffn_in": nrm(ks[22], (L, D, 2 * FFN_HIDDEN), D),
        "w_ffn_out": nrm(ks[23], (L, FFN_HIDDEN, D), FFN_HIDDEN),
        "final_g": gain(ks[24], (D,)),
    }

def reference(x, c, w_ada, b_ada, norm1_g, w_in, conv_w, conv_b, conv_ln_g, conv_ln_b,
              conv_proj, ssm_a_re, ssm_a_im, ssm_b_re, ssm_b_im, ssm_c_re, ssm_c_im,
              ssm_d, ssm_log_dt, ssm_glu, w_out, norm2_g, w_ffn_in, w_ffn_out, final_g):
    c_act = jax.nn.silu(c)
    split_pts = [2 * CONV_WIDTH, 2 * CONV_WIDTH + SSM_WIDTH, 2 * CONV_WIDTH + SSM_WIDTH + D_MODEL]
    for l in range(DEPTH):
        mod = (c_act @ w_ada[l] + b_ada[l])[:, None, :]
        sh1, sc1, g1, sh2, sc2, g2 = jnp.split(mod, N_MOD, axis=-1)

        h = rmsnorm(x, norm1_g[l]) * (1.0 + sc1) + sh1
        z = h @ w_in[l]
        u_conv, u_ssm, gl_conv, gl_ssm = jnp.split(z, split_pts, axis=-1)
        y_conv = conformer_conv(u_conv, conv_w[l], conv_b[l], conv_ln_g[l],
                                conv_ln_b[l], conv_proj[l])
        y_ssm = s5_mixer(u_ssm, ssm_a_re[l], ssm_a_im[l], ssm_b_re[l], ssm_b_im[l],
                         ssm_c_re[l], ssm_c_im[l], ssm_d[l], ssm_log_dt[l], ssm_glu[l])
        merged = jax.nn.sigmoid(gl_conv) * y_conv + jax.nn.sigmoid(gl_ssm) * y_ssm
        x = x + g1 * (merged @ w_out[l])

        h = rmsnorm(x, norm2_g[l]) * (1.0 + sc2) + sh2
        f_gate, f_up = jnp.split(h @ w_ffn_in[l], 2, axis=-1)
        x = x + g2 * ((jax.nn.silu(f_gate) * f_up) @ w_ffn_out[l])
    return rmsnorm(x, final_g)


_drawn_inputs = setup_inputs


def setup_inputs(seed=0):
    import zlib

    import numpy as np

    out = dict(_drawn_inputs(seed))
    spreads = {}
    factors = {'b_ada': 3.234,
     'norm1_g': 8.0,
     'conv_b': 8.0,
     'conv_ln_g': 8.0,
     'conv_ln_b': 25.82,
     'ssm_a_re': 64.0,
     'ssm_a_im': 64.0,
     'ssm_b_re': 64.0,
     'ssm_b_im': 64.0,
     'ssm_c_re': 64.0,
     'ssm_c_im': 64.0,
     'ssm_log_dt': 64.0,
     'norm2_g': 3.82}
    for name, (base, spread) in spreads.items():
        noise = np.random.default_rng([zlib.crc32(name.encode()), seed]).standard_normal(out[name].shape)
        drawn = base * np.exp(spread * noise) if base else spread * noise
        out[name] = __import__('jax').numpy.asarray(drawn.astype(out[name].dtype))
    for name, factor in factors.items():
        out[name] = (out[name] * factor).astype(out[name].dtype)
    return out
```

```python
from contextlib import ExitStack

import numpy as np

import concourse.bass as bass
from concourse import mybir

ALU = mybir.AluOpType
ACT = mybir.ActivationFunctionType
F32 = mybir.dt.float32
F32R = mybir.dt.float32r
BF16 = mybir.dt.bfloat16
I32 = mybir.dt.int32

P = 128
EPS = 1e-6


class Steps:

    def __init__(self, sem, phases):
        self.sem, self.at, self.base, self.per, self.names = sem, {}, {}, {}, {}
        total = 0
        for phase, times, segments in phases:
            n = 0
            names = []
            for seg, rep in segments:
                for j, name in enumerate(seg):
                    assert (phase, name) not in self.at, name
                    self.at[phase, name] = (n + j + 1, len(seg))
                names += seg
                n += len(seg) * rep
            self.base[phase], self.per[phase], self.names[phase] = total, n, names
            total += n * times
        self.next = {phase: 0 for phase, _, _ in phases}

    def step(self, phase, name):
        want = self.names[phase][self.next[phase]]
        assert want == name, f"{phase}: {name} where {want} stands"
        self.next[phase] += 1
        return self.sem, 1

    def after(self, phase, b, name, it=0):
        at, width = self.at[phase, name]
        return self.sem, self.base[phase] + at + b * self.per[phase] + it * width

    def before(self, phase, b, name, it=0):
        at, width = self.at[phase, name]
        round_ = self.per[phase] if it is None else width
        v = self.base[phase] + at - round_
        assert v >= 0, (phase, name, v)
        return self.sem, v + b * self.per[phase] + (0 if it is None else it * width)

    def start(self, phase, b):
        return self.sem, self.base[phase] + b * self.per[phase]

    def finished(self):
        for phase, n in self.next.items():
            assert n == len(self.names[phase]), (phase, self.names[phase][n])


def build(nc, x, c, w_ada, b_ada, norm1_g, w_in, conv_w, conv_b, conv_ln_g, conv_ln_b, conv_proj,
          ssm_a_re, ssm_a_im, ssm_b_re, ssm_b_im, ssm_c_re, ssm_c_im, ssm_d, ssm_log_dt, ssm_glu,
          w_out, norm2_g, w_ffn_in, w_ffn_out, final_g, out):
    SEQ, D = x.shape[1], x.shape[2]
    TAPS, CW = conv_w.shape[1], conv_w.shape[2]
    G, NST, HG = ssm_b_re.shape[1:]
    FF = w_ffn_out.shape[1]
    SW = G * HG
    TB = 512
    NB = SEQ // TB
    TT = TB // P
    KD = D // P
    KC = CW // P
    KS = SW // P
    KF = FF // P
    T = P // HG
    NC = TB // T
    GQ = 512 // NC
    NQ = G // GQ
    GT = P // HG
    HALO = TAPS - 1
    CH = 1024
    HALF = D // 2
    RAW, SPL = 3, 2
    assert 2 * NST == P and KC == 4 and KS == 4 and KD == 8 and NQ == 4 and x.shape[0] == 1
    assert KF % 2 == 0 and GT == T

    o_ssm, o_gl = 2 * CW, 2 * CW + SW
    MIX_CHUNKS = [("in", o_ssm + m * P) for m in range(KS)]
    for m in range(KC):
        MIX_CHUNKS += [("in", m * P), ("in", CW + m * P)]
    MIX_CHUNKS += [("in", o_gl + i * P) for i in range(2 * KD)]
    for p in range(KD // 2):
        MIX_CHUNKS += [("proj", 2 * p * P), ("glu", 2 * p * P), ("glu", D + 2 * p * P)]
    MIX_CHUNKS += [("out", h, j) for h in range(2) for j in range(KD // 2)]
    NMIX = len(MIX_CHUNKS)
    FI = KF // 2
    NFFN = 2 * KF + 2 * (KF // 2)
    assert NMIX % (RAW * SPL) == 0 and NFFN % (RAW * SPL) == 0

    x2_d = nc.dram_tensor("x2_scratch", (SEQ, D), F32).ap()
    us_d = nc.dram_tensor("us_scratch", (SW, T, NC), F32).ap()
    ys_d = nc.dram_tensor("ys_scratch", (SW, T, NC), F32).ap()
    wt_d = nc.dram_tensor("wt_scratch", (P, G, P), F32).ap()
    vk_d = nc.dram_tensor("vk_scratch", (P, G, 2, P), F32).ap()

    x_d, out_d = x[0], out[0]
    win_d = w_in[0].rearrange("(k p) n -> p k n", p=P)
    proj_d = conv_proj[0].rearrange("(k p) n -> p k n", p=P)
    glu_d = ssm_glu[0].rearrange("(k p) n -> p k n", p=P)
    wout_d = w_out[0].rearrange("(k p) n -> p k n", p=P)
    fin_d = w_ffn_in[0].rearrange("(k p) n -> p k n", p=P)
    fout_d = w_ffn_out[0].rearrange("(k p) n -> p k n", p=P)
    ada_d = w_ada[0].rearrange("(k p) n -> p k n", p=P)

    with ExitStack() as ctx:
        cursor = [(nc.sbuf_base + 63) // 64 * 64]

        def place(name, shape, dtype=F32, at=None):
            size = int(np.prod(shape[1:])) * (2 if dtype == BF16 else 4)
            off = cursor[0] if at is None else at
            t = nc.alloc_sbuf_tensor_at(name, list(shape), dtype, offset=off)
            if at is None:
                cursor[0] = (off + size + 63) // 64 * 64
            return t

        raw_at = cursor[0]
        raw = [place(f"raw{s}", [P, CH]) for s in range(RAW)]
        w_hi = [place(f"w_hi{s}", [P, CH], F32R) for s in range(SPL)]
        w_lo = [place(f"w_lo{s}", [P, CH], F32R) for s in range(SPL)]
        h_at = cursor[0]
        h_hi = place("h_hi", [P, KD, TB], F32R)
        h_lo = place("h_lo", [P, KD, TB], F32R)
        tr_at = cursor[0]
        tr = [place(f"tr{s}", [P, TB]) for s in range(4)]
        dt_at = cursor[0]
        dt_ = [place(f"dt{s}", [P, TB]) for s in range(4)]
        junk = place("junk", [P, D], BF16)
        g2b = place("g2b", [P, D])
        ident = place("ident", [P, P])
        turn = place("turn", [P, P])
        mean_w = place("mean_w", [P, P])
        zero1 = place("zero1", [P, 1])
        eps1 = place("eps1", [P, 1])
        sign = place("sign", [P, 1])
        nsign = place("nsign", [P, 1])
        mod = place("mod", [P, 4 * KD])
        bmod = place("bmod", [P, 6 * KD])
        ng = place("ng", [P, 2 * KD])
        scale = [place(f"scale{n}", [P, KD]) for n in range(2)]
        cvec = place("cvec", [P, 3, KC])
        ss = place("ss", [P, TT])
        sd = place("sd", [P, TT])
        rs = place("rs", [P, TT])
        over = cursor[0]
        g1b = place("g1b", [P, D])
        uc = place("uc", [P, KC, HALO + TB])
        cwt = place("cwt", [P, KC, TAPS])
        carry = place("carry", [P, G])
        ctmp = place("ctmp", [P, G])
        mag_t = place("mag_t", [P, G])
        cos_t = place("cos_t", [P, NC + 1, G])
        sin_t = place("sin_t", [P, NC + 1, G])
        kept = cursor[0]
        ssm_m = [place(f"ssm_m{s}", [P, CH]) for s in range(3)]
        xr = [place(f"xr{s}", [P, HALF]) for s in range(4)]
        yn_at = cursor[0]
        yn_hi = place("yn_hi", [P, KC, TB], F32R)
        ync_at = cursor[0]
        yn_lo = place("yn_lo", [P, KC, TB], F32R)
        ys_hi = place("ys_hi", [P, KS, TB], F32R)
        yz_at = cursor[0]
        ys_lo = place("ys_lo", [P, KS, TB], F32R)
        mc_at = cursor[0]
        m_hi = place("m_hi", [P, KD, TB], F32R)
        ms_at = cursor[0]
        m_lo = place("m_lo", [P, KD, TB], F32R)
        end_kept = cursor[0]
        xs = place("xs", [P, TT, D])
        uz = place("uz", [P, KS, T, NC], at=yn_at)
        sq = place("sq", [P, KC, TB], at=yn_at)
        yc = place("yc", [P, KC, TB], at=ync_at)
        yz = place("yz", [P, KS, T, NC], at=yz_at)
        sg_c = place("sg_c", [P, KD, TB], at=mc_at)
        sg_s = place("sg_s", [P, KD, TB], at=ms_at)
        cursor[0] = end_kept
        u8 = place("u8", [P, G, NC])
        wst = place("wst", [P, G, NC + 1])
        cursor[0] = over
        hid_hi = place("hid_hi", [P, KF, TB], F32R)
        hid_lo = place("hid_lo", [P, KF, TB], F32R)
        x3 = place("x3", [P, TT, D])
        fgb = place("fgb", [P, D])
        assert cursor[0] <= end_kept
        cursor[0] = kept
        vm = place("vm", [P, G, T + 1, HG])
        wm = place("wm", [P, G, T, HG])
        kst = place("kst", [HG, G, T, HG])
        bx1 = place("bx1", [P, G, HG])
        bx2 = place("bx2", [P, G, HG])
        b1 = place("b1", [P, G, HG])
        b2 = place("b2", [P, G, HG])
        c1 = place("c1", [P, G, HG])
        c2 = place("c2", [P, G, HG])
        cx = place("cx", [P, 2, 4, P])
        ptmp = place("ptmp", [P, G, HG])
        jexp = place("jexp", [P, T + 1, G])
        jer = place("jer", [P, T + 1, G])
        jei = place("jei", [P, T + 1, G])
        sv = place("sv", [P, 12, G])
        iota_i = place("iota_i", [P, NC + 1], I32)
        iota_f = place("iota_f", [P, NC + 1])
        cact = place("cact", [P, 2, KD])
        dvec = place("dvec", [HG, G])
        zrow = place("zrow", [HG, P])
        assert cursor[0] <= end_kept, (cursor[0], end_kept)
        ada = [place(f"ada{s}", [P, KD, 256], at=raw_at + s * KD * 256 * 4) for s in range(2)]
        bg = place("bg", [P, 2, D], at=dt_at)
        cbc = place("cbc", [P, KD, P], at=tr_at)
        ddiag = place("ddiag", [HG, G, HG], at=tr_at + KD * P * 4)
        cursor[0] = h_at
        karg = place("karg", [P, 2, NC + 1, G])
        ktmp = place("ktmp", [P, NC + 1, G])
        jarg = place("jarg", [P, 2, T + 1, G])
        jtmp = place("jtmp", [P, T + 1, G])
        assert cursor[0] <= tr_at

        bank = [ctx.enter_context(nc.psum_tensor(f"bank{i}", [P, 512], F32)) for i in range(8)]
        Z, Q = [0, 1, 2, 3], [4, 5, 6, 7]

        def sem(name):
            return ctx.enter_context(nc.semaphore(name))

        R = range
        norm_act = ["ns0", "ns1", "ns2", "ns3", "nsd"]
        norm_dve = ["nms", "nr", "nx0", "nx1", "nx2", "nx3"]
        h_steps = [f"h{k}" for k in R(KD)]
        hh = lambda k: [f"hh{k}", f"hl{k}"]
        h_dve = [n for k in R(KD) for n in hh(k)]

        pe_mix = [f"us{m}" for m in R(KS)] + [f"u{a}{m}" for m in R(KC) for a in "ag"]
        pe_mix += [f"S{q}" for q in R(NQ)] + ["gl0", "gl1"] + [f"R{q}" for q in R(NQ)]
        pe_mix += [f"gl{i}" for i in R(2, 6)] + [f"D{q}" for q in R(NQ)] + ["dc"]
        pe_mix += [f"gl{i}" for i in R(6, 10)]
        for q in R(NQ):
            pe_mix += [f"Y{q}", f"gl{10 + q}"]
        pe_mix += ["ln1", "gl14", "ln2", "gl15"]
        for p in R(KD // 2):
            pe_mix += [f"{a}{m}" for a in ("cp", "za", "zb") for m in (2 * p, 2 * p + 1)]
            pe_mix += [f"h{2 * p}", f"h{2 * p + 1}"]
        for f in R(2):
            pe_mix += [f"oc{f}{j}" for j in R(KD // 2 - 1)] + [f"o{f}{i}" for i in R(TT)]
        pe_loop = ["fg0", "fu0", "fg1", "fu1"]
        pe_out = []
        for f in R(2):
            for j in R(KF // 2 - 1):
                pe_out += [f"fc{f}_{j}"] + ([f"h{j - 1}"] if f == 0 and 1 <= j <= KD else [])
            pe_out += [f"p{f}{i}" for i in R(TT)]
        pe_pro = ["ct0", "ct1"] + [f"wt{n}" for n in R(8)] + [f"kk{n}" for n in R(8)]
        pe_pro += [f"ada{n}" for n in R(24)] + h_steps
        tensor = Steps(sem("tensor_done"), [
            ("pro", 1, [(pe_pro, 1)]), ("mix", NB, [(pe_mix, 1)]), ("mid", 1, [(h_steps, 1)]),
            ("ffn", NB, [(pe_loop, FI), (pe_out, 1)])])

        act_mix = [f"us{m}" for m in R(KS)] + [f"ug{m}" for m in R(KC)] + [f"S{q}" for q in R(NQ)]
        act_mix += [f"gl{i}" for i in R(10)]
        for q in R(NQ):
            act_mix += [f"Y{q}", f"gl{10 + q}"]
        act_mix += [f"sq{m}" for m in R(KC)]
        act_mix += ["gl14", "lsd"] + [f"ge{m}" for m in R(KS)] + ["gl15"] + [f"si{m}" for m in R(KC)]
        act_mix += norm_act
        for p in R(KD // 2):
            act_mix += [f"zb{2 * p}", f"zb{2 * p + 1}", f"h{2 * p}", f"h{2 * p + 1}"]
        act_loop = ["fs0", "fs1"]
        act_out = norm_act + h_steps + [f"fq{i}" for i in R(TT)] + ["fsd"]
        act_pro = ["dt", "ej", "sj", "cj", "sk", "ck", "m8", "cs"]
        act_pro += [f"wt{n}" for n in R(8)] + [f"kk{n}" for n in R(8)] + norm_act + h_steps
        scal = Steps(sem("scalar_done"), [
            ("pro", 1, [(act_pro, 1)]), ("mix", NB, [(act_mix, 1)]), ("mid", 1, [(norm_act + h_steps, 1)]),
            ("ffn", NB, [(act_loop, FI), (act_out, 1)])])

        CUT = [0, 8, 16, 24, TAPS]
        taps = lambda n: [f"c{t}_{m}" for t in R(CUT[n], CUT[n + 1]) for m in R(KC)]
        dve_mix = [f"u{m}" for m in R(KC)] + taps(0)
        for q in R(NQ):
            dve_mix += [f"Rt{q}", f"Rc{q}"]
        dve_mix += [f"Rs{q}" for q in R(NQ)] + ["in"] + [f"sc{g}" for g in R(G)]
        dve_mix += taps(1)
        for q in R(NQ):
            dve_mix += [f"Dt{q}", f"Dc{q}"]
        dve_mix += ["dc1", "dc2"] + [f"Ds{q}" for q in R(NQ)] + ["dc3"]
        dve_mix += taps(2) + taps(3) + ["halo"]
        dve_mix += [f"cen{m}" for m in R(KC)] + ["rec"] + [f"nm{m}" for m in R(KC)]
        dve_mix += [f"{a}{m}" for m in R(KS) for a in ("ysh", "ysl")]
        dve_mix += [f"{a}{m}" for m in R(KC) for a in ("ynh", "ynl")] + norm_dve
        for p in R(KD // 2):
            for m in (2 * p, 2 * p + 1):
                dve_mix += [f"mc{m}", f"ms{m}", f"mt{m}", f"ma{m}", f"mh{m}", f"ml{m}"]
            dve_mix += hh(2 * p) + hh(2 * p + 1)
        for f in R(2):
            dve_mix += [n for i in R(TT) for n in (f"oa{f}{i}", f"ob{f}{i}")]
        dve_loop = [f"{a}{j}" for a in ("fm", "fh", "fl") for j in R(2)]
        dve_out = norm_dve + h_dve
        for f in R(2):
            dve_out += [n for i in R(TT) for n in (f"pa{f}{i}", f"pb{f}{i}")]
        dve_out += ["fms", "fr"] + [f"fx{i}" for i in R(TT)]
        vec = Steps(sem("vector_done"), [
            ("pro", 1, [(norm_dve + h_dve, 1)]), ("mix", NB, [(dve_mix, 1)]),
            ("mid", 1, [(norm_dve + h_dve, 1)]), ("ffn", NB, [(dve_loop, FI), (dve_out, 1)])])

        def is_z(n):
            return n[0] in "uzh" or n[:2] in ("gl", "cp") or n[:2] in ("fg", "fu")

        plan = {}
        for phase, names in (("pro", h_steps), ("mix", pe_mix), ("mid", h_steps), ("ffn", pe_loop + pe_out)):
            z = 0
            for n in names:
                if n[:2] in ("oc", "fc"):
                    continue
                if is_z(n) or n[:2] in ("o0", "p1"):
                    plan[phase, n] = z % 4
                    z += 1
            assert z % 4 == 0
        for q in R(NQ):
            plan["mix", f"S{q}"] = 4 + q % 2
            plan["mix", f"R{q}"] = 6 + q % 2
            plan["mix", f"D{q}"] = 4 + q % 2
            plan["mix", f"Y{q}"] = 6 + q % 2
        plan["mix", "dc"], plan["mix", "ln1"], plan["mix", "ln2"] = 6, 4, 5
        for i in R(TT):
            plan["mix", f"o1{i}"] = plan["ffn", f"p0{i}"] = 4 + i

        def reader(phase, n):
            if n[:2] in ("us", "gl", "zb", "ug") or n[0] in "hSY":
                return scal, n
            if n == "ln2":
                return scal, "lsd"
            if n[0] in "RD":
                return vec, n[0] + "t" + n[1]
            return vec, {"ua": "u" + n[2:], "dc": "dc1", "ln": "cen3", "cp": "mc" + n[2:], "za": "ms" + n[2:],
                         "o0": "oa" + n[1:], "o1": "oa" + n[1:], "p0": "pa" + n[1:], "p1": "pa" + n[1:],
                         "fu": "fm" + n[2:]}[n[:2]] if n[:2] != "fg" else None

        order = {"pro": h_steps, "mix": pe_mix, "mid": h_steps, "ffn": pe_loop + pe_out}

        def bank_free(phase, b, n, it=0):
            use = [m for m in order[phase] if plan.get((phase, m)) == plan[phase, n]]
            j = use.index(n)
            if j and not (n in pe_loop):
                who, step = reader(phase, use[j - 1]) if use[j - 1][:2] != "fg" else (scal, "fs" + use[j - 1][2])
                last = FI - 1 if use[j - 1] in pe_loop else 0
                return who.after(phase, b, step, last)
            if n in pe_loop:
                who, step = (scal, "fs" + n[2]) if n[:2] == "fg" else (vec, "fm" + n[2])
                return who.before(phase, b, step, it)
            who, step = reader(phase, use[-1])
            return who.before(phase, b, step, None)

        raw_in = [sem(f"raw_in{s}") for s in R(RAW)]
        hi_done = sem("hi_done")
        split_done = sem("split_done")
        ssm_in = [sem(f"ssm_in{s}") for s in R(3)]
        xs_in = sem("xs_in")
        uz_out, u8_in, y_out, yz_in = sem("uz_out"), sem("u8_in"), sem("y_out"), sem("yz_in")
        xr_in = [sem(f"xr_in{s}") for s in R(4)]
        x2_out = [sem(f"x2_out{s}") for s in R(4)]
        x3_in, final_out = sem("x3_in"), sem("final_out")
        small_in = sem("small_in")
        consts = sem("consts")
        ada_in = [sem("ada_in0"), sem("ada_in1")]
        ada_done = sem("ada_done")
        pro_v = sem("prologue_vector")
        mat_out = sem("mat_out")
        fg_in = sem("fg_in")
        mark = {}

        chunk_no = {}
        n = 0
        for s in pe_mix:
            if s[:2] in ("us", "gl", "ua", "ug", "oc") or s in ("o03", "o13") or (
                    s[:2] in ("cp", "za", "zb") and int(s[2]) % 2):
                n += 1
                chunk_no["mix", n] = s
        assert n == NMIX
        n = 2 * KF
        for s in pe_out:
            if s[:2] == "fc" or s in ("p03", "p13"):
                n += 1
                chunk_no["ffn", n] = s
        assert n == NFFN

        def chunk_used(phase, b, n, it=0):
            return tensor.after(phase, b, chunk_no[phase, n])

        block = ctx.enter_context(nc.Block())

        @block.vector
        def _(dve):
            v = nc.vector

            def link(ins, name=None):
                mark["n"] = mark.get("n", 0) + 1
                ins.then_inc(pro_v, 1)
                dve.wait_ge(pro_v, mark["n"])
                if name:
                    mark[name] = mark["n"]

            dve.wait_ge(consts, 9)
            TWO_PI = 2 * np.pi
            c1_ = float(np.float32(6.28125))
            c2_ = float(np.float32(TWO_PI - 6.28125))
            c3_ = float(np.float32(TWO_PI - 6.28125 - np.float64(np.float32(TWO_PI - 6.28125))))
            MAGIC = float(1.5 * 2 ** 23)
            PI_ = float(np.float32(3.1415925))

            def reduce_angle(dst, src, tmp):
                link(v.tensor_scalar(tmp, src, float(1 / TWO_PI), MAGIC, ALU.mult, ALU.add))
                link(v.tensor_scalar(tmp, tmp, MAGIC, None, ALU.subtract))
                link(v.scalar_tensor_tensor(out=dst, in0=tmp, scalar=-c1_, in1=src, op0=ALU.mult, op1=ALU.add))
                link(v.scalar_tensor_tensor(out=dst, in0=tmp, scalar=-c2_, in1=dst, op0=ALU.mult, op1=ALU.add))
                link(v.scalar_tensor_tensor(out=dst, in0=tmp, scalar=-c3_, in1=dst, op0=ALU.mult, op1=ALU.add))
                link(v.tensor_scalar(dst, dst, PI_, -PI_, ALU.min, ALU.max))

            ar, ai, dt, th, lg, ph, t0, t1 = (sv[:, n, :] for n in R(8))
            qr, qi, nr, den = (sv[:, n, :] for n in R(8, 12))
            dve.wait_ge(*scal.after("pro", 0, "dt"))
            link(v.tensor_tensor(th, dt, ai, ALU.mult))
            link(v.tensor_tensor(lg, dt, ar, ALU.mult))
            reduce_angle(th, th, t0)
            link(v.tensor_scalar(ph, th, float(T), None, ALU.mult))
            reduce_angle(ph, ph, t0)
            for table, angle, n in ((jarg, th, T + 1), (karg, ph, NC + 1)):
                tmp = jtmp if n == T + 1 else ktmp
                steps = iota_f[:, 0:n].unsqueeze(2).broadcast_to([P, n, G])
                link(v.tensor_tensor(table[:, 0, :, :], steps, angle.unsqueeze(1).broadcast_to([P, n, G]), ALU.mult))
                flat = lambda a: a.rearrange("p a b -> p (a b)")
                reduce_angle(flat(table[:, 0, :, :]), flat(table[:, 0, :, :]), flat(tmp[:, :, :]))
                link(v.tensor_scalar(flat(table[:, 1, :, :]), flat(table[:, 0, :, :]), float(np.pi / 2), None, ALU.add))
                reduce_angle(flat(table[:, 1, :, :]), flat(table[:, 1, :, :]), flat(tmp[:, :, :]))
            link(v.tensor_tensor(jexp[:], iota_f[:, 0:T + 1].unsqueeze(2).broadcast_to([P, T + 1, G]),
                                 lg.unsqueeze(1).broadcast_to([P, T + 1, G]), ALU.mult), "args")
            dve.wait_ge(*scal.after("pro", 0, "cj"))
            link(v.tensor_tensor(jer[:], jexp[:], jer[:], ALU.mult))
            link(v.tensor_tensor(jei[:], jexp[:], jei[:], ALU.mult))
            e_r, e_i = jer[:, 1, :], jei[:, 1, :]
            link(v.tensor_scalar(nr, e_r, -1.0, None, ALU.add))
            link(v.tensor_tensor(t0, ar, ar, ALU.mult))
            link(v.tensor_tensor(t1, ai, ai, ALU.mult))
            link(v.tensor_tensor(den, t0, t1, ALU.add))
            link(v.reciprocal(den, den))
            link(v.tensor_tensor(t0, nr, ar, ALU.mult))
            link(v.tensor_tensor(t1, e_i, ai, ALU.mult))
            link(v.tensor_tensor(qr, t0, t1, ALU.add))
            link(v.tensor_tensor(qr, qr, den, ALU.mult))
            link(v.tensor_tensor(t0, e_i, ar, ALU.mult))
            link(v.tensor_tensor(t1, nr, ai, ALU.mult))
            link(v.tensor_tensor(qi, t0, t1, ALU.subtract))
            link(v.tensor_tensor(qi, qi, den, ALU.mult))

            def by_h(a):
                return a.unsqueeze(2).broadcast_to([P, G, HG])

            link(v.tensor_tensor(b1[:], bx1[:], by_h(qr), ALU.mult))
            link(v.tensor_tensor(ptmp[:], bx2[:], by_h(qi), ALU.mult))
            flat2 = lambda a: a[:].rearrange("p a b -> p (a b)")
            link(v.scalar_tensor_tensor(out=flat2(b1), in0=flat2(ptmp), scalar=sign[:, 0:1], in1=flat2(b1),
                                        op0=ALU.mult, op1=ALU.add))
            link(v.tensor_tensor(b2[:], bx2[:], by_h(qr), ALU.mult))
            link(v.tensor_tensor(ptmp[:], bx1[:], by_h(qi), ALU.mult))
            link(v.scalar_tensor_tensor(out=flat2(b2), in0=flat2(b2), scalar=sign[:, 0:1], in1=flat2(ptmp),
                                        op0=ALU.mult, op1=ALU.subtract))
            for s in R(T):
                j = T - 1 - s
                link(v.tensor_tensor(wm[:, :, s, :], b1[:], by_h(jer[:, j, :]), ALU.mult))
                link(v.tensor_tensor(ptmp[:], b2[:], by_h(jei[:, j, :]), ALU.mult))
                link(v.tensor_tensor(wm[:, :, s, :], wm[:, :, s, :], ptmp[:], ALU.add), "wm" if s == T - 1 else None)
            dve.wait_ge(*tensor.after("pro", 0, "ct1"))
            flatg = lambda a: a[:].rearrange("p g h -> p (g h)")
            link(v.tensor_scalar(flatg(c1), bank[0][:], nsign[:, 0:1], None, ALU.mult))
            link(v.tensor_scalar(flatg(c2), bank[1][:], -1.0, None, ALU.mult), "cc")
            for j in R(T + 1):
                link(v.tensor_tensor(vm[:, :, j, :], c1[:], by_h(jer[:, j, :]), ALU.mult))
                link(v.tensor_tensor(ptmp[:], c2[:], by_h(jei[:, j, :]), ALU.mult))
                link(v.tensor_tensor(vm[:, :, j, :], vm[:, :, j, :], ptmp[:], ALU.add), "vm" if j == T else None)
            dve.wait_ge(*scal.after("pro", 0, "cs"))
            link(v.tensor_copy(cbc[:], cact[:, 1, :].unsqueeze(2).broadcast_to([P, KD, P])), "cbc")
            link(v.tensor_tensor(ddiag[:], ident[0:HG, 0:HG].unsqueeze(1).broadcast_to([HG, G, HG]),
                                 dvec[:].unsqueeze(2).broadcast_to([HG, G, HG]), ALU.mult))
            dve.wait_ge(*scal.after("pro", 0, "kk7"))
            link(v.tensor_tensor(kst[:, :, 0, :], kst[:, :, 0, :], ddiag[:], ALU.add), "kst")
            for n in R(24):
                kind = n // 4
                dve.wait_ge(*tensor.after("pro", 0, f"ada{n}"))
                if kind in (2, 5):
                    dst = (g1b if kind == 2 else g2b)[:, (n % 4) * 256:(n % 4 + 1) * 256]
                    v.tensor_tensor(dst, bank[2 + n % 2][:, 0:256], bg[:, kind // 3, (n % 4) * 256:(n % 4 + 1) * 256],
                                    ALU.add).then_inc(ada_done, 1)
                else:
                    col = (kind if kind < 2 else kind - 1) * KD + (n % 4) * 2
                    v.tensor_tensor(mod[:, col:col + 2], bank[2 + n % 2][:, 0:2],
                                    bmod[:, kind * KD + (n % 4) * 2:kind * KD + (n % 4) * 2 + 2],
                                    ALU.add).then_inc(ada_done, 1)
                    if n % 4 == 3 and kind in (1, 4):
                        which = kind // 4
                        dve.wait_ge(ada_done, n + 1)
                        link(v.tensor_scalar(scale[which][:], mod[:, (2 * which + 1) * KD:(2 * which + 2) * KD],
                                             1.0, None, ALU.add))
                        link(v.tensor_tensor(scale[which][:], scale[which][:], ng[:, which * KD:(which + 1) * KD],
                                             ALU.mult), f"scale{which}")

            def wait_self(phase, b, name, it=0):
                dve.wait_ge(*vec.after(phase, b, name, it))

            def split(hi, lo, src, steps, phase, b, it=0):
                v.tensor_copy(hi, src).then_inc(*vec.step(phase, steps[0]))
                wait_self(phase, b, steps[0], it)
                v.tensor_tensor(lo, src, hi.bitcast(F32), ALU.subtract).then_inc(*vec.step(phase, steps[1]))

            def norm_scale(phase, b):
                dve.wait_ge(*scal.after(phase, b, "ns3"))
                v.tensor_scalar(ss[:], ss[:], 1.0 / D, EPS, ALU.mult, ALU.add).then_inc(*vec.step(phase, "nms"))
                dve.wait_ge(*scal.after(phase, b, "nsd"))
                v.reciprocal(rs[:], sd[:]).then_inc(*vec.step(phase, "nr"))
                wait_self(phase, b, "nr")
                for i in R(TT):
                    v.tensor_scalar(xs[:, i, :], xs[:, i, :], rs[:, i:i + 1], None, ALU.mult)\
                        .then_inc(*vec.step(phase, f"nx{i}"))

            def h_split(phase, b, k):
                dve.wait_ge(*scal.after(phase, b, f"h{k}"))
                split(h_hi[:, k, :], h_lo[:, k, :], tr[k % 4][:], hh(k), phase, b)

            norm_scale("pro", 0)
            for k in R(KD):
                h_split("pro", 0, k)

            with dve.Fori(0, NB) as b:
                for m in R(KC):
                    dve.wait_ge(*scal.after("mix", b, f"ug{m}"))
                    v.tensor_tensor(uc[:, m, HALO:], bank[plan["mix", f"ua{m}"]][:], tr[m][:], ALU.mult)\
                        .then_inc(*vec.step("mix", f"u{m}"))

                def conv(part):
                    for t in R(CUT[part], CUT[part + 1]):
                        for m in R(KC):
                            src = uc[:, m, t:t + TB]
                            w = cwt[:, m, t:t + 1]
                            if t == 0:
                                wait_self("mix", b, f"u{m}")
                                ins = v.tensor_scalar(yc[:, m, :], src, w, cvec[:, 0, m:m + 1], ALU.mult, ALU.add)
                            else:
                                wait_self("mix", b, f"c{t - 1}_{m}")
                                ins = v.scalar_tensor_tensor(out=yc[:, m, :], in0=src, scalar=w, in1=yc[:, m, :],
                                                             op0=ALU.mult, op1=ALU.add)
                            ins.then_inc(*vec.step("mix", f"c{t}_{m}"))

                def quarter(a, q, lo, hi_):
                    return a[:, q * GQ:(q + 1) * GQ, lo:hi_]

                def table(t, q, lo, hi_):
                    return t[:, lo:hi_, q * GQ:(q + 1) * GQ].rearrange("p k g -> p g k")

                def by_g(a):
                    return a.rearrange("p (g k) -> p g k", g=GQ)

                conv(0)
                for q in R(NQ):
                    dve.wait_ge(*tensor.after("mix", b, f"R{q}"))
                    v.tensor_tensor(by_g(dt_[q][:]), by_g(bank[plan["mix", f"R{q}"]][:]), table(sin_t, q, 1, NC + 1),
                                    ALU.mult).then_inc(*vec.step("mix", f"Rt{q}"))
                    v.tensor_tensor(quarter(wst, q, 1, NC + 1), quarter(wst, q, 1, NC + 1), table(cos_t, q, 1, NC + 1),
                                    ALU.mult).then_inc(*vec.step("mix", f"Rc{q}"))
                for q in R(NQ):
                    wait_self("mix", b, f"Rc{q}")
                    v.tensor_tensor(quarter(wst, q, 1, NC + 1), quarter(wst, q, 1, NC + 1), by_g(dt_[q][:]),
                                    ALU.add).then_inc(*vec.step("mix", f"Rs{q}"))
                v.tensor_copy(wst[:, :, 0], carry[:]).then_inc(*vec.step("mix", "in"))
                for g in R(G):
                    if g == 0:
                        wait_self("mix", b, "in")
                    v.tensor_tensor_scan(wst[:, g, 1:], mag_t[:, g:g + 1].broadcast_to([P, NC]), wst[:, g, 1:],
                                         carry[:, g:g + 1], ALU.mult, ALU.add).then_inc(*vec.step("mix", f"sc{g}"))
                conv(1)
                for q in R(NQ):
                    dve.wait_ge(*tensor.after("mix", b, f"D{q}"))
                    v.tensor_tensor(by_g(dt_[q][:]), by_g(bank[plan["mix", f"D{q}"]][:]), table(sin_t, q, 0, NC),
                                    ALU.mult).then_inc(*vec.step("mix", f"Dt{q}"))
                    v.tensor_tensor(quarter(wst, q, 0, NC), quarter(wst, q, 0, NC), table(cos_t, q, 0, NC),
                                    ALU.mult).then_inc(*vec.step("mix", f"Dc{q}"))
                dve.wait_ge(*tensor.after("mix", b, "dc"))
                v.tensor_tensor(ctmp[:], bank[plan["mix", "dc"]][:, 0:G], sin_t[:, NC, :], ALU.mult)\
                    .then_inc(*vec.step("mix", "dc1"))
                v.tensor_tensor(carry[:], wst[:, :, NC], cos_t[:, NC, :], ALU.mult).then_inc(*vec.step("mix", "dc2"))
                for q in R(NQ):
                    wait_self("mix", b, f"Dc{q}")
                    v.tensor_tensor(quarter(wst, q, 0, NC), quarter(wst, q, 0, NC), by_g(dt_[q][:]),
                                    ALU.subtract).then_inc(*vec.step("mix", f"Ds{q}"))
                wait_self("mix", b, "dc2")
                v.tensor_tensor(carry[:], carry[:], ctmp[:], ALU.subtract).then_inc(*vec.step("mix", "dc3"))
                conv(2)
                conv(3)
                v.tensor_copy(uc[:, :, 0:HALO], uc[:, :, TB:]).then_inc(*vec.step("mix", "halo"))
                dve.wait_ge(*tensor.after("mix", b, "ln1"))
                for m in R(KC):
                    v.tensor_tensor(yc[:, m, :], yc[:, m, :], bank[plan["mix", "ln1"]][:], ALU.subtract)\
                        .then_inc(*vec.step("mix", f"cen{m}"))
                dve.wait_ge(*scal.after("mix", b, "lsd"))
                v.reciprocal(dt_[1][:], dt_[0][:]).then_inc(*vec.step("mix", "rec"))
                wait_self("mix", b, "rec")
                for m in R(KC):
                    v.tensor_tensor(yc[:, m, :], yc[:, m, :], dt_[1][:], ALU.mult).then_inc(*vec.step("mix", f"nm{m}"))
                for m in R(KS):
                    dve.wait_ge(*scal.after("mix", b, f"ge{KS - 1}"))
                    split(ys_hi[:, m, :], ys_lo[:, m, :], tr[m][:], (f"ysh{m}", f"ysl{m}"), "mix", b)
                for m in R(KC):
                    dve.wait_ge(*scal.after("mix", b, f"si{m}"))
                    split(yn_hi[:, m, :], yn_lo[:, m, :], tr[m][:], (f"ynh{m}", f"ynl{m}"), "mix", b)
                norm_scale("mix", b)
                for p in R(KD // 2):
                    for m in (2 * p, 2 * p + 1):
                        dve.wait_ge(*tensor.after("mix", b, f"cp{m}"))
                        v.tensor_tensor(dt_[0][:], bank[plan["mix", f"cp{m}"]][:], sg_c[:, m, :], ALU.mult)\
                            .then_inc(*vec.step("mix", f"mc{m}"))
                        dve.wait_ge(*scal.after("mix", b, f"zb{m}"))
                        v.tensor_tensor(dt_[1][:], bank[plan["mix", f"za{m}"]][:], tr[m % 2][:], ALU.mult)\
                            .then_inc(*vec.step("mix", f"ms{m}"))
                        wait_self("mix", b, f"ms{m}")
                        v.tensor_tensor(dt_[1][:], dt_[1][:], sg_s[:, m, :], ALU.mult).then_inc(*vec.step("mix", f"mt{m}"))
                        wait_self("mix", b, f"mt{m}")
                        v.tensor_tensor(dt_[2][:], dt_[0][:], dt_[1][:], ALU.add).then_inc(*vec.step("mix", f"ma{m}"))
                        wait_self("mix", b, f"ma{m}")
                        split(m_hi[:, m, :], m_lo[:, m, :], dt_[2][:], (f"mh{m}", f"ml{m}"), "mix", b)
                    for k in (2 * p, 2 * p + 1):
                        dve.wait_ge(*scal.after("mix", b, f"h{k}"))
                        split(h_hi[:, k, :], h_lo[:, k, :], tr[2 + k % 2][:], hh(k), "mix", b)
                for f in R(2):
                    for i in R(TT):
                        dve.wait_ge(*tensor.after("mix", b, f"o{f}{i}"))
                        v.tensor_tensor(dt_[i][:], bank[plan["mix", f"o{f}{i}"]][:], g1b[:, f * HALF:(f + 1) * HALF],
                                        ALU.mult).then_inc(*vec.step("mix", f"oa{f}{i}"))
                        dve.wait_ge(xr_in[i], 16 * (2 * b + f + 1))
                        wait_self("mix", b, f"oa{f}{i}")
                        v.tensor_tensor(xr[i][:], xr[i][:], dt_[i][:], ALU.add).then_inc(*vec.step("mix", f"ob{f}{i}"))

            norm_scale("mid", 0)
            for k in R(KD):
                h_split("mid", 0, k)

            with dve.Fori(0, NB) as b:
                with dve.Fori(0, FI) as it:
                    for j in R(2):
                        dve.wait_ge(*scal.after("ffn", b, f"fs{j}", it))
                        dve.wait_ge(*tensor.after("ffn", b, f"fu{j}", it))
                        dve.wait_ge(*vec.before("ffn", b, f"fl{j}", it))
                        v.tensor_tensor(dt_[j][:], bank[plan["ffn", f"fu{j}"]][:], tr[j][:], ALU.mult)\
                            .then_inc(*vec.step("ffn", f"fm{j}"))
                    hid = lambda t, j: t[:, bass.ds(2 * it + j, 1), :]
                    one = lambda a: a.unsqueeze(1)
                    for j in R(2):
                        wait_self("ffn", b, f"fm{j}", it)
                        v.tensor_copy(hid(hid_hi, j), one(dt_[j][:])).then_inc(*vec.step("ffn", f"fh{j}"))
                    for j in R(2):
                        wait_self("ffn", b, f"fh{j}", it)
                        v.tensor_tensor(hid(hid_lo, j), one(dt_[j][:]), hid(hid_hi, j).bitcast(F32), ALU.subtract)\
                            .then_inc(*vec.step("ffn", f"fl{j}"))
                norm_scale("ffn", b)
                for k in R(KD):
                    h_split("ffn", b, k)
                for f in R(2):
                    for i in R(TT):
                        dve.wait_ge(*tensor.after("ffn", b, f"p{f}{i}"))
                        v.tensor_tensor(dt_[i][:], bank[plan["ffn", f"p{f}{i}"]][:], g2b[:, f * HALF:(f + 1) * HALF],
                                        ALU.mult).then_inc(*vec.step("ffn", f"pa{f}{i}"))
                        if f == i == 0:
                            dve.wait_ge(x3_in, 16 * (b + 1))
                        wait_self("ffn", b, f"pa{f}{i}")
                        part = x3[:, i, f * HALF:(f + 1) * HALF]
                        v.tensor_tensor(part, part, dt_[i][:], ALU.add).then_inc(*vec.step("ffn", f"pb{f}{i}"))
                dve.wait_ge(*scal.after("ffn", b, f"fq{TT - 1}"))
                v.tensor_scalar(ss[:], ss[:], 1.0 / D, EPS, ALU.mult, ALU.add).then_inc(*vec.step("ffn", "fms"))
                dve.wait_ge(*scal.after("ffn", b, "fsd"))
                v.reciprocal(rs[:], sd[:]).then_inc(*vec.step("ffn", "fr"))
                wait_self("ffn", b, "fr")
                dve.wait_ge(fg_in, 16)
                for i in R(TT):
                    v.scalar_tensor_tensor(out=x3[:, i, :], in0=x3[:, i, :], scalar=rs[:, i:i + 1], in1=fgb[:],
                                           op0=ALU.mult, op1=ALU.mult).then_inc(*vec.step("ffn", f"fx{i}"))

        @block.scalar
        def _(act):
            s = nc.scalar

            def load_small():
                with nc.allow_non_contiguous_dma(reason="small per-channel vectors"):
                    yield act.dma_start(cact[:, 0, :], c[0].rearrange("(k p) -> p k", p=P))
                    yield act.dma_start(bmod[:], b_ada[0].rearrange("(k p) -> p k", p=P))
                    yield act.dma_start(ng[:, 0:KD], norm1_g[0].rearrange("(k p) -> p k", p=P))
                    yield act.dma_start(ng[:, KD:], norm2_g[0].rearrange("(k p) -> p k", p=P))
                    yield act.dma_start(cvec[:, 0, :], conv_b[0].rearrange("(k p) -> p k", p=P))
                    yield act.dma_start(cvec[:, 1, :], conv_ln_g[0].rearrange("(k p) -> p k", p=P))
                    yield act.dma_start(cvec[:, 2, :], conv_ln_b[0].rearrange("(k p) -> p k", p=P))
                    for m in R(KC):
                        yield act.dma_start(cwt[:, m, :], conv_w[0][:, m * P:(m + 1) * P].rearrange("t p -> p t"))
                    for half in R(2):
                        rows = slice(half * NST, (half + 1) * NST)
                        yield act.dma_start(sv[rows, 0, :], ssm_a_re[0].rearrange("g p -> p g"))
                        yield act.dma_start(sv[rows, 1, :], ssm_a_im[0].rearrange("g p -> p g"))
                        for dst, first in ((bx1, ssm_b_re), (bx2, ssm_b_im)):
                            src = first if half == 0 else (ssm_b_im if first is ssm_b_re else ssm_b_re)
                            yield act.dma_start(dst[rows, :, :], src[0].rearrange("g p h -> p g h"))
                    yield act.dma_start(sv[:, 2, :], ssm_log_dt[0].partition_broadcast(P))
                    for n, (re, im) in enumerate(((ssm_c_re, ssm_c_im), (ssm_c_im, ssm_c_re))):
                        flat = lambda a: a[0].rearrange("g h p -> (g h) p").rearrange("(t q) p -> q t p", q=P)
                        yield act.dma_start(cx[:, n, :, 0:NST], flat(re))
                        yield act.dma_start(cx[:, n, :, NST:], flat(im))
                    yield act.dma_start(dvec[:], ssm_d[0].rearrange("(g h) -> h g", h=HG))
                    for n, off in enumerate((2 * D, 5 * D)):
                        yield act.dma_start(bg[:, n, :], b_ada[0][off:off + D].partition_broadcast(P))

            n_small = 0
            for ins in load_small():
                ins.then_inc(small_in, 16)
                n_small += 1
            mark["small"] = 16 * n_small

            def load_xs(src, row):
                for i in R(TT):
                    act.dma_start(xs[:, i, :], src[bass.ds(row + i * P, P), :]).then_inc(xs_in, 16)

            load_xs(x_d, 0)
            act.wait_ge(consts, 9)
            act.wait_ge(small_in, mark["small"])
            s.activation(sv[:, 2, :], sv[:, 2, :], ACT.Exp).then_inc(*scal.step("pro", "dt"))
            act.wait_ge(pro_v, mark["args"])
            s.activation(jexp[:], jexp[:], ACT.Exp).then_inc(*scal.step("pro", "ej"))
            s.activation(jei[:], jarg[:, 0, :, :], ACT.Sin).then_inc(*scal.step("pro", "sj"))
            s.activation(jer[:], jarg[:, 1, :, :], ACT.Sin).then_inc(*scal.step("pro", "cj"))
            s.activation(sin_t[:], karg[:, 0, :, :], ACT.Sin).then_inc(*scal.step("pro", "sk"))
            s.activation(cos_t[:], karg[:, 1, :, :], ACT.Sin).then_inc(*scal.step("pro", "ck"))
            s.activation(mag_t[:], sv[:, 4, :], ACT.Exp, scale=float(T)).then_inc(*scal.step("pro", "m8"))
            s.activation(cact[:, 1, :], cact[:, 0, :], ACT.Silu).then_inc(*scal.step("pro", "cs"))
            for n in R(8):
                act.wait_ge(*tensor.after("pro", 0, f"wt{n}"))
                s.activation(wm[:, 4 * n:4 * n + 4, :, :].rearrange("p g s h -> p (g s h)"), bank[n][:], ACT.Copy)\
                    .then_inc(*scal.step("pro", f"wt{n}"))
            for n in R(8):
                act.wait_ge(*tensor.after("pro", 0, f"kk{n}"))
                s.activation(kst[:, 4 * n:4 * n + 4, :, :].rearrange("p g s h -> p (g s h)"), bank[n][0:HG, :],
                             ACT.Copy).then_inc(*scal.step("pro", f"kk{n}"))
            act.wait_ge(*scal.after("pro", 0, "wt7"))
            act.dma_start(wt_d, wm[:].rearrange("p g s h -> p g (s h)")).then_inc(mat_out, 16)
            act.wait_ge(pro_v, mark["vm"])
            act.dma_start(vk_d[:, :, 0, :], vm[:, :, 1:, :].rearrange("p g s h -> p g (s h)")).then_inc(mat_out, 16)
            act.wait_ge(pro_v, mark["kst"])
            for t in R(T):
                rows = vk_d[t * HG:(t + 1) * HG, :, 1, :]
                act.dma_start(rows[:, :, t * HG:], kst[:, :, 0:T - t, :].rearrange("p g s h -> p g (s h)"))\
                    .then_inc(mat_out, 16)
                if t:
                    act.dma_start(rows[:, :, 0:t * HG],
                                  zrow[:, 0:t * HG].unsqueeze(1).broadcast_to([HG, G, t * HG])).then_inc(mat_out, 16)

            def norm_stats(phase, b, n_loads):
                act.wait_ge(xs_in, n_loads)
                for i in R(TT):
                    if i:
                        act.wait_ge(*scal.after(phase, b, f"ns{i - 1}"))
                    s.activation(junk[:], xs[:, i, :], ACT.Square, accum_out=ss[:, i:i + 1])\
                        .then_inc(*scal.step(phase, f"ns{i}"))
                act.wait_ge(*vec.after(phase, b, "nms"))
                s.activation(sd[:], ss[:], ACT.Sqrt).then_inc(*scal.step(phase, "nsd"))

            def h_tile(phase, b, k, slot, which, free):
                act.wait_ge(*tensor.after(phase, b, f"h{k}"))
                if free:
                    act.wait_ge(*free)
                s.activation(tr[slot][:], bank[plan[phase, f"h{k}"]][:], ACT.Identity, scale=scale[which][:, k:k + 1],
                             bias=mod[:, 2 * which * KD + k:2 * which * KD + k + 1]).then_inc(*scal.step(phase, f"h{k}"))

            norm_stats("pro", 0, 64)
            act.wait_ge(pro_v, mark["scale1"])
            for k in R(KD):
                h_tile("pro", 0, k, k % 4, 0, vec.after("pro", 0, f"hl{k - 4}") if k >= 4 else None)

            with act.Fori(0, NB) as b:
                for m in R(KS):
                    act.wait_ge(*tensor.after("mix", b, f"us{m}"))
                    s.activation(uz[:, m, :, :].rearrange("p s c -> p c s"),
                                 bank[plan["mix", f"us{m}"]][:].rearrange("p (c s) -> p c s", s=T), ACT.Copy)\
                        .then_inc(*scal.step("mix", f"us{m}"))
                    act.wait_ge(*scal.after("mix", b, f"us{m}"))
                    act.dma_start(us_d[m * P:(m + 1) * P], uz[:, m, :, :]).then_inc(uz_out, 16)
                act.wait_ge(uz_out, 64 * (b + 1))
                for t in R(T):
                    act.dma_start(u8[t * HG:(t + 1) * HG, :, :], us_d[:, t, :].rearrange("(g h) c -> h g c", h=HG))\
                        .then_inc(u8_in, 16)
                for m in R(KC):
                    act.wait_ge(*tensor.after("mix", b, f"ug{m}"))
                    s.activation(tr[m][:], bank[plan["mix", f"ug{m}"]][:], ACT.Sigmoid)\
                        .then_inc(*scal.step("mix", f"ug{m}"))
                for q in R(NQ):
                    act.wait_ge(*tensor.after("mix", b, f"S{q}"))
                    s.activation(wst[:, q * GQ:(q + 1) * GQ, 1:], bank[plan["mix", f"S{q}"]][:]
                                 .rearrange("p (g k) -> p g k", g=GQ), ACT.Copy).then_inc(*scal.step("mix", f"S{q}"))

                def gate(i):
                    act.wait_ge(*tensor.after("mix", b, f"gl{i}"))
                    dst = (sg_c if i < KD else sg_s)[:, i % KD, :]
                    s.activation(dst, bank[plan["mix", f"gl{i}"]][:], ACT.Sigmoid).then_inc(*scal.step("mix", f"gl{i}"))

                for i in R(10):
                    gate(i)
                for q in R(NQ):
                    act.wait_ge(*tensor.after("mix", b, f"Y{q}"))
                    s.activation(u8[:, q * GQ:(q + 1) * GQ, :], bank[plan["mix", f"Y{q}"]][:]
                                 .rearrange("p (g k) -> p g k", g=GQ), ACT.Copy).then_inc(*scal.step("mix", f"Y{q}"))
                    if q == NQ - 1:
                        act.wait_ge(*scal.after("mix", b, f"Y{q}"))
                        for t in R(T):
                            act.dma_start(ys_d[:, t, :].rearrange("(g h) c -> h g c", h=HG),
                                          u8[t * HG:(t + 1) * HG, :, :]).then_inc(y_out, 16)
                    gate(10 + q)
                act.wait_ge(y_out, 16 * T * (b + 1))
                act.dma_start(yz[:], ys_d.rearrange("(m p) s c -> p m s c", p=P)).then_inc(yz_in, 16)
                load_xs(x_d, (b + 1) % NB * TB)
                for m in R(KC):
                    act.wait_ge(*vec.after("mix", b, f"cen{m}"))
                    s.activation(sq[:, m, :], yc[:, m, :], ACT.Square).then_inc(*scal.step("mix", f"sq{m}"))
                gate(14)
                act.wait_ge(*tensor.after("mix", b, "ln2"))
                s.activation(dt_[0][:], bank[plan["mix", "ln2"]][:], ACT.Sqrt, bias=eps1[:, 0:1])\
                    .then_inc(*scal.step("mix", "lsd"))
                act.wait_ge(yz_in, 16 * (b + 1))
                for m in R(KS):
                    s.activation(tr[m][:].rearrange("p (c s) -> p c s", s=T),
                                 yz[:, m, :, :].rearrange("p s c -> p c s"), ACT.Gelu_apprx_tanh)\
                        .then_inc(*scal.step("mix", f"ge{m}"))
                gate(15)
                for m in R(KC):
                    act.wait_ge(*vec.after("mix", b, f"nm{m}"))
                    act.wait_ge(*vec.after("mix", b, f"ysl{m}"))
                    s.activation(tr[m][:], yc[:, m, :], ACT.Silu, scale=cvec[:, 1, m:m + 1], bias=cvec[:, 2, m:m + 1])\
                        .then_inc(*scal.step("mix", f"si{m}"))
                norm_stats("mix", b, 64 * (b + 2))
                for i in R(TT):
                    act.wait_ge(x2_out[i], 16 * 2 * b)
                    act.dma_start(xr[i][:], x_d[bass.ds(b * TB + i * P, P), 0:HALF]).then_inc(xr_in[i], 16)
                for p in R(KD // 2):
                    for m in (2 * p, 2 * p + 1):
                        act.wait_ge(*tensor.after("mix", b, f"zb{m}"))
                        act.wait_ge(*vec.after("mix", b, f"ms{m - 2}" if p else f"ynl{m}"))
                        s.activation(tr[m % 2][:], bank[plan["mix", f"zb{m}"]][:], ACT.Sigmoid)\
                            .then_inc(*scal.step("mix", f"zb{m}"))
                    for k in (2 * p, 2 * p + 1):
                        h_tile("mix", b, k, 2 + k % 2, 0,
                               vec.after("mix", b, f"hl{k - 2}" if p else f"ynl{2 + k}"))
                for f in R(2):
                    for i in R(TT):
                        act.wait_ge(*vec.after("mix", b, f"ob{f}{i}"))
                        act.dma_start(x2_d[bass.ds(b * TB + i * P, P), f * HALF:(f + 1) * HALF], xr[i][:])\
                            .then_inc(x2_out[i], 16)
                    if f == 0:
                        for i in R(TT):
                            act.wait_ge(x2_out[i], 16 * (2 * b + 1))
                            act.dma_start(xr[i][:], x_d[bass.ds(b * TB + i * P, P), HALF:]).then_inc(xr_in[i], 16)

            act.wait_ge(*tensor.after("mix", NB - 1, f"h{KD - 1}"))
            for i in R(TT):
                act.wait_ge(x2_out[i], 16 * 2)
            load_xs(x2_d, 0)
            norm_stats("mid", 0, 64 * (NB + 2))
            for k in R(KD):
                h_tile("mid", 0, k, k % 4, 1, vec.after("mid", 0, f"hl{k - 4}") if k >= 4 else
                       vec.after("mix", NB - 1, f"hl{KD - 1}"))
            for i in R(TT):
                act.wait_ge(x2_out[i], 16 * 2 * NB)
            act.dma_start(fgb[:], final_g.partition_broadcast(P)).then_inc(fg_in, 16)

            with act.Fori(0, NB) as b:
                act.wait_ge(final_out, 64 * b)
                act.dma_start(x3[:], x2_d[bass.ds(b * TB, TB), :].rearrange("(i p) d -> p i d", p=P))\
                    .then_inc(x3_in, 16)
                load_xs(x2_d, ((b + 1) % NB) * TB)
                with act.Fori(0, FI) as it:
                    for j in R(2):
                        act.wait_ge(*tensor.after("ffn", b, f"fg{j}", it))
                        act.wait_ge(*vec.before("ffn", b, f"fm{j}", it))
                        s.activation(tr[j][:], bank[plan["ffn", f"fg{j}"]][:], ACT.Silu)\
                            .then_inc(*scal.step("ffn", f"fs{j}"))
                norm_stats("ffn", b, 64 * (b + NB + 3))
                for k in R(KD):
                    h_tile("ffn", b, k, k % 4, 1, vec.after("ffn", b, f"hl{k - 4}") if k >= 4 else
                           vec.after("ffn", b, "fm1", FI - 1))
                for i in R(TT):
                    act.wait_ge(*vec.after("ffn", b, f"pb1{i}"))
                    act.wait_ge(*scal.after("ffn", b, f"fq{i - 1}" if i else "nsd"))
                    s.activation(junk[:], x3[:, i, :], ACT.Square, accum_out=ss[:, i:i + 1])\
                        .then_inc(*scal.step("ffn", f"fq{i}"))
                act.wait_ge(*vec.after("ffn", b, "fms"))
                s.activation(sd[:], ss[:], ACT.Sqrt).then_inc(*scal.step("ffn", "fsd"))
                for i in R(TT):
                    act.wait_ge(*vec.after("ffn", b, f"fx{i}"))
                    act.dma_start(out_d[bass.ds(b * TB + i * P, P), :], x3[:, i, :]).then_inc(final_out, 16)
            act.wait_ge(final_out, 64 * NB)

        @block.tensor
        def _(pe):
            t = nc.tensor
            pe.wait_ge(consts, 9)
            pe.wait_ge(small_in, mark["small"])
            for n in R(2):
                for j in R(4):
                    ins = t.transpose(bank[n][:, j * P:(j + 1) * P], cx[:, n, j, :], ident[:])
                ins.then_inc(*tensor.step("pro", f"ct{n}"))
            pe.wait_ge(pro_v, mark["wm"])
            pe.wait_ge(pro_v, mark["cc"])
            for n in R(8):
                for j in R(4):
                    ins = t.transpose(bank[n][:, j * P:(j + 1) * P],
                                      wm[:, 4 * n + j, :, :].rearrange("p s h -> p (s h)"), ident[:])
                ins.then_inc(*tensor.step("pro", f"wt{n}"))
            pe.wait_ge(pro_v, mark["vm"])
            for n in R(8):
                pe.wait_ge(*scal.after("pro", 0, f"wt{n}"))
                for j in R(4):
                    g = 4 * n + j
                    ins = t.matmul(bank[n][0:HG, j * P:(j + 1) * P], b1[:, g, :],
                                   vm[:, g, 0:T, :].rearrange("p s h -> p (s h)"), start=True, stop=True)
                ins.then_inc(*tensor.step("pro", f"kk{n}"))
            pe.wait_ge(pro_v, mark["cbc"])
            pe.wait_ge(*scal.after("pro", 0, "kk7"))
            for n in R(24):
                pe.wait_ge(ada_in[n % 2], 16 * (n // 2 + 1))
                if n >= 2:
                    pe.wait_ge(ada_done, n - 1)
                dst, slab = bank[2 + n % 2], ada[n % 2]
                if n // 4 in (2, 5):
                    for k in R(KD):
                        ins = t.matmul(dst[:, 0:256], cbc[:, k, :], slab[:, k, :], start=(k == 0), stop=(k == KD - 1))
                else:
                    for j in R(2):
                        for k in R(KD):
                            ins = t.matmul(dst[:, j:j + 1], slab[:, k, j * P:(j + 1) * P], cact[:, 1, k:k + 1],
                                           start=(k == 0), stop=(k == KD - 1))
                ins.then_inc(*tensor.step("pro", f"ada{n}"))
            pe.wait_ge(ada_done, 24)

            def transposes(phase, b, k, free=True):
                if free:
                    pe.wait_ge(*bank_free(phase, b, f"h{k}"))
                if k == 0:
                    pe.wait_ge(*vec.after(phase, b, f"nx{TT - 1}"))
                for i in R(TT):
                    ins = t.transpose(bank[plan[phase, f"h{k}"]][:, i * P:(i + 1) * P], xs[:, i, k * P:(k + 1) * P],
                                      ident[:])
                ins.then_inc(*tensor.step(phase, f"h{k}"))

            for k in R(KD):
                if k >= 4:
                    pe.wait_ge(*scal.after("pro", 0, f"h{k - 4}"))
                transposes("pro", 0, k, free=False)
            pe.wait_ge(*vec.after("pro", 0, f"hl{KD - 1}"))

            def three(dst, wh, wl, xh, xl, first, last):
                t.matmul(dst, wh, xh, start=first, stop=False)
                t.matmul(dst, wh, xl, start=False, stop=False)
                return t.matmul(dst, wl, xh, start=False, stop=last)

            with pe.Fori(0, NB) as b:
                chunk = [0]

                def next_chunk():
                    chunk[0] += 1
                    pe.wait_ge(split_done, RAW + b * NMIX + chunk[0])
                    return (chunk[0] - 1) % SPL

                def layer(name, ws, first_col, width, kt, xh, xl):
                    pe.wait_ge(*bank_free("mix", b, name))
                    hi = w_hi[ws][:].rearrange("p (k n) -> p k n", n=width)
                    lo = w_lo[ws][:].rearrange("p (k n) -> p k n", n=width)
                    for k in R(kt):
                        ins = three(bank[plan["mix", name]][:], hi[:, k, first_col:first_col + P],
                                    lo[:, k, first_col:first_col + P], xh[:, k, :], xl[:, k, :], k == 0, k == kt - 1)
                    ins.then_inc(*tensor.step("mix", name))

                def gates(*tiles):
                    for i in tiles:
                        layer(f"gl{i}", next_chunk(), 0, P, KD, h_hi, h_lo)

                ssm_use = [0]

                def next_ssm():
                    n = ssm_use[0]
                    ssm_use[0] += 1
                    pe.wait_ge(ssm_in[n % 3], 16 * (4 * b + n // 3 + 1))
                    return ssm_m[n % 3]

                for m in R(KS):
                    layer(f"us{m}", next_chunk(), 0, P, KD, h_hi, h_lo)
                for m in R(KC):
                    layer(f"ua{m}", next_chunk(), 0, P, KD, h_hi, h_lo)
                    layer(f"ug{m}", next_chunk(), 0, P, KD, h_hi, h_lo)
                pe.wait_ge(u8_in, 16 * T * (b + 1))
                for q in R(NQ):
                    mat = next_ssm()[:].rearrange("p (g n) -> p g n", g=GQ)
                    pe.wait_ge(*bank_free("mix", b, f"S{q}"))
                    for j in R(GQ):
                        ins = t.matmul(bank[plan["mix", f"S{q}"]][:, j * NC:(j + 1) * NC], mat[:, j, :],
                                       u8[:, q * GQ + j, :], start=True, stop=True)
                    ins.then_inc(*tensor.step("mix", f"S{q}"))
                gates(0, 1)

                def turned(name, q, lo):
                    pe.wait_ge(*bank_free("mix", b, name))
                    t.matmul(bank[plan["mix", name]][:], turn[:], wst[:, q * GQ:(q + 1) * GQ, lo:lo + NC],
                             start=True, stop=True).then_inc(*tensor.step("mix", name))

                for q in R(NQ):
                    pe.wait_ge(*scal.after("mix", b, f"S{q}"))
                    turned(f"R{q}", q, 1)
                gates(2, 3, 4, 5)
                pe.wait_ge(*vec.after("mix", b, f"sc{G - 1}"))
                for q in R(NQ):
                    turned(f"D{q}", q, 0)
                pe.wait_ge(*bank_free("mix", b, "dc"))
                t.matmul(bank[plan["mix", "dc"]][:, 0:G], turn[:], wst[:, :, NC], start=True, stop=True)\
                    .then_inc(*tensor.step("mix", "dc"))
                gates(6, 7, 8, 9)
                for q in R(NQ):
                    pe.wait_ge(*vec.after("mix", b, f"Ds{q}"))
                    pe.wait_ge(*bank_free("mix", b, f"Y{q}"))
                    for half in R(2):
                        mat = next_ssm()[:].rearrange("p (g a n) -> p g a n", g=GQ // 2, a=2)
                        for j in R(GQ // 2):
                            g = q * GQ + half * (GQ // 2) + j
                            dst = bank[plan["mix", f"Y{q}"]][:, (g % GQ) * NC:(g % GQ + 1) * NC]
                            t.matmul(dst, mat[:, j, 0, :], wst[:, g, 0:NC], start=True, stop=False)
                            ins = t.matmul(dst, mat[:, j, 1, :], u8[:, g, :], start=False, stop=True)
                    ins.then_inc(*tensor.step("mix", f"Y{q}"))
                    gates(10 + q)

                def mean(name, src):
                    pe.wait_ge(*bank_free("mix", b, name))
                    for m in R(KC):
                        ins = t.matmul(bank[plan["mix", name]][:], mean_w[:], src[:, m, :], start=(m == 0),
                                       stop=(m == KC - 1))
                    ins.then_inc(*tensor.step("mix", name))

                pe.wait_ge(*vec.after("mix", b, f"c{TAPS - 1}_{KC - 1}"))
                mean("ln1", yc)
                gates(14)
                pe.wait_ge(*scal.after("mix", b, f"sq{KC - 1}"))
                mean("ln2", sq)
                gates(15)
                for p in R(KD // 2):
                    if p == 0:
                        pe.wait_ge(*vec.after("mix", b, f"ynl{KC - 1}"))
                    for name, xh, xl in (("cp", yn_hi, yn_lo), ("za", ys_hi, ys_lo), ("zb", ys_hi, ys_lo)):
                        slot = next_chunk()
                        for j in R(2):
                            layer(f"{name}{2 * p + j}", slot, j * P, 2 * P, KC, xh, xl)
                    for k in (2 * p, 2 * p + 1):
                        transposes("mix", b, k)

                def out_half(phase, b, f, kt, xh, xl, pre, step, between=None):
                    for j in R(kt // 2):
                        slot = next_chunk()
                        for kk in R(2):
                            k = 2 * j + kk
                            for i in R(TT):
                                if k == 0:
                                    pe.wait_ge(*bank_free(phase, b, f"{pre}{f}{i}"))
                                dst = bank[plan[phase, f"{pre}{f}{i}"]][:]
                                cols = slice(i * P, (i + 1) * P)
                                wcols = slice(kk * HALF, (kk + 1) * HALF)
                                t.matmul(dst, xh[:, k, cols], w_hi[slot][:, wcols], start=(k == 0), stop=False)
                                t.matmul(dst, xl[:, k, cols], w_hi[slot][:, wcols], start=False, stop=False)
                                ins = t.matmul(dst, xh[:, k, cols], w_lo[slot][:, wcols], start=False,
                                               stop=(k == kt - 1))
                                if k == kt - 1:
                                    ins.then_inc(*tensor.step(phase, f"{pre}{f}{i}"))
                        if j < kt // 2 - 1:
                            ins.then_inc(*tensor.step(phase, step(f, j)))
                        if between:
                            between(f, j)

                pe.wait_ge(*vec.after("mix", b, f"ml{KD - 1}"))
                for f in R(2):
                    out_half("mix", b, f, KD, m_hi, m_lo, "o", lambda f, j: f"oc{f}{j}")
                pe.wait_ge(*vec.after("mix", b, f"hl{KD - 1}"))
                assert chunk[0] == NMIX

            for k in R(KD):
                if k < 4:
                    pe.wait_ge(*bank_free("mid", 0, f"h{k}") if k >= 4 else vec.after("mix", NB - 1, f"oa0{k}"))
                    transposes("mid", 0, k, free=False)
                else:
                    transposes("mid", 0, k)
            pe.wait_ge(*vec.after("mid", 0, f"hl{KD - 1}"))

            with pe.Fori(0, NB) as b:
                with pe.Fori(0, FI) as it:
                    for n, name in enumerate(pe_loop):
                        pe.wait_ge(split_done, RAW + NB * NMIX + b * NFFN + it * 4 + n + 1)
                        pe.wait_ge(*bank_free("ffn", b, name, it))
                        ws = n % SPL
                        for k in R(KD):
                            cols = slice(k * P, (k + 1) * P)
                            ins = three(bank[plan["ffn", name]][:], w_hi[ws][:, cols], w_lo[ws][:, cols],
                                        h_hi[:, k, :], h_lo[:, k, :], k == 0, k == KD - 1)
                        ins.then_inc(*tensor.step("ffn", name))
                chunk = [2 * KF]

                def next_chunk():
                    chunk[0] += 1
                    pe.wait_ge(split_done, RAW + NB * NMIX + b * NFFN + chunk[0])
                    return (chunk[0] - 1) % SPL

                def next_h(f, j):
                    if f == 0 and 1 <= j <= KD:
                        transposes("ffn", b, j - 1)

                pe.wait_ge(*vec.after("ffn", b, "fl1", FI - 1))
                for f in R(2):
                    for j in R(KF // 2):
                        slot = next_chunk()
                        for kk in R(2):
                            k = 2 * j + kk
                            for i in R(TT):
                                if k == 0:
                                    pe.wait_ge(*bank_free("ffn", b, f"p{f}{i}"))
                                dst = bank[plan["ffn", f"p{f}{i}"]][:]
                                cols = slice(i * P, (i + 1) * P)
                                wcols = slice(kk * HALF, (kk + 1) * HALF)
                                t.matmul(dst, hid_hi[:, k, cols], w_hi[slot][:, wcols], start=(k == 0), stop=False)
                                t.matmul(dst, hid_lo[:, k, cols], w_hi[slot][:, wcols], start=False, stop=False)
                                ins = t.matmul(dst, hid_hi[:, k, cols], w_lo[slot][:, wcols], start=False,
                                               stop=(k == KF - 1))
                                if k == KF - 1:
                                    ins.then_inc(*tensor.step("ffn", f"p{f}{i}"))
                        if j < KF // 2 - 1:
                            ins.then_inc(*tensor.step("ffn", f"fc{f}_{j}"))
                        next_h(f, j)
                pe.wait_ge(*vec.after("ffn", b, f"hl{KD - 1}"))
                assert chunk[0] == NFFN

        @block.gpsimd
        def _(pool):
            g = nc.gpsimd
            g.memset(ident[:], 0.0).then_inc(consts, 1)
            g.memset(turn[:], 0.0).then_inc(consts, 1)
            pool.wait_ge(consts, 2)
            g.affine_select(out=ident[:], in_=ident[:], compare_op=ALU.not_equal, fill=1.0, base=0,
                            pattern=[[-1, P]], channel_multiplier=1).then_inc(consts, 1)
            g.affine_select(out=turn[:], in_=turn[:], compare_op=ALU.not_equal, fill=1.0, base=-NST,
                            pattern=[[-1, P]], channel_multiplier=1).then_inc(consts, 1)
            pool.wait_ge(consts, 4)
            g.affine_select(out=turn[:], in_=turn[:], compare_op=ALU.not_equal, fill=-1.0, base=NST,
                            pattern=[[-1, P]], channel_multiplier=1).then_inc(consts, 1)
            g.iota(iota_i[:], pattern=[[1, NC + 1]], base=0, channel_multiplier=0).then_inc(consts, 1)
            g.memset(sign[:], 1.0).then_inc(split_done, 1)
            g.memset(nsign[:], -1.0).then_inc(split_done, 1)
            g.memset(zero1[:], 0.0).then_inc(split_done, 1)
            g.memset(eps1[:], EPS)
            g.memset(mean_w[:], 1.0 / CW)
            g.memset(carry[:], 0.0)
            g.memset(zrow[:], 0.0)
            g.memset(uc[:, :, 0:HALO], 0.0).then_inc(consts, 1)
            pool.wait_ge(consts, 7)
            g.memset(sign[0:NST, :], -1.0)
            g.memset(nsign[0:NST, :], 1.0).then_inc(consts, 1)
            g.tensor_copy(iota_f[:], iota_i[:]).then_inc(consts, 1)

            zeros = zero1[:, 0:1].broadcast_to([P, CH])

            with pool.Fori(0, NB) as b:
                for n in R(NMIX):
                    first = b * NMIX
                    pool.wait_ge(raw_in[n % RAW], 16 * (b * (NMIX // RAW) + n // RAW + 1))
                    if n >= SPL:
                        pool.wait_ge(*chunk_used("mix", b, n - SPL + 1))
                    else:
                        s_, v_ = tensor.before("mix", b, chunk_no["mix", NMIX - SPL + n + 1], None)
                        pool.wait_ge(s_, v_)
                    src, hi, lo = raw[n % RAW], w_hi[n % SPL], w_lo[n % SPL]
                    g.tensor_tensor(hi[:], src[:], zeros, ALU.add).then_inc(hi_done, 1)
                    pool.wait_ge(hi_done, first + n + 1)
                    g.tensor_tensor(lo[:], src[:], hi[:].bitcast(F32), ALU.subtract).then_inc(split_done, 1)
            with pool.Fori(0, NB) as b:
                for n in R(NFFN):
                    first = NB * NMIX + b * NFFN
                    pool.wait_ge(raw_in[n % RAW], 16 * (NB * NMIX // RAW + b * (NFFN // RAW) + n // RAW + 1))
                    m = n - SPL + 1
                    if m <= 0:
                        s_, v_ = tensor.before("ffn", b, chunk_no["ffn", NFFN + m], None)
                    elif m <= 2 * KF:
                        s_, v_ = tensor.after("ffn", b, pe_loop[(m - 1) % 4], (m - 1) // 4)
                    else:
                        s_, v_ = chunk_used("ffn", b, m)
                    pool.wait_ge(s_, v_)
                    src, hi, lo = raw[n % RAW], w_hi[n % SPL], w_lo[n % SPL]
                    g.tensor_tensor(hi[:], src[:], zeros, ALU.add).then_inc(hi_done, 1)
                    pool.wait_ge(hi_done, first + n + 1)
                    g.tensor_tensor(lo[:], src[:], hi[:].bitcast(F32), ALU.subtract).then_inc(split_done, 1)

        @block.sync
        def _(sp):
            for n in R(24):
                if n >= 2:
                    sp.wait_ge(*tensor.after("pro", 0, f"ada{n - 2}"))
                sp.dma_start(ada[n % 2][:], ada_d[:, :, n * 256:(n + 1) * 256]).then_inc(ada_in[n % 2], 16)
            sp.wait_ge(mat_out, 16 * (2 + 2 * T - 1))
            sp.wait_ge(*tensor.after("pro", 0, "ada23"))
            sp.wait_ge(ada_done, 24)

            def load(n, key, number):
                dst = raw[n % RAW]
                sp.wait_ge(split_done, number + 1)
                if key[0] == "in":
                    d, src = dst[:].rearrange("p (k n) -> p k n", n=P), win_d[:, :, key[1]:key[1] + P]
                elif key[0] in ("proj", "glu"):
                    d = dst[:].rearrange("p (k n) -> p k n", n=2 * P)
                    src = (proj_d if key[0] == "proj" else glu_d)[:, :, key[1]:key[1] + 2 * P]
                elif key[0] == "out":
                    d = dst[:].rearrange("p (k n) -> p k n", n=HALF)
                    src = wout_d[:, 2 * key[2]:2 * key[2] + 2, key[1] * HALF:(key[1] + 1) * HALF]
                elif key[0] == "fin":
                    d, src = dst[:].rearrange("p (k n) -> p k n", n=P), fin_d[:, :, key[1]:key[1] + P]
                else:
                    d = dst[:].rearrange("p (k n) -> p k n", n=HALF)
                    src = fout_d[:, 2 * key[2]:2 * key[2] + 2, key[1] * HALF:(key[1] + 1) * HALF]
                sp.dma_start(d, src).then_inc(raw_in[n % RAW], 16)

            with sp.Fori(0, NB) as b:
                ssm_user = [f"S{q}" for q in R(NQ)] + [f"Y{q}" for q in R(NQ) for _ in R(2)]

                def load_ssm(n):
                    if n >= 3:
                        sp.wait_ge(*tensor.after("mix", b, ssm_user[n - 3]))
                    else:
                        sp.wait_ge(*tensor.start("mix", b))
                    if n < NQ:
                        src = wt_d[:, n * GQ:(n + 1) * GQ, :].rearrange("p g n -> p (g n)")
                    else:
                        m = n - NQ
                        src = vk_d[:, m * GQ // 2:(m + 1) * GQ // 2, :, :].rearrange("p g a n -> p (g a n)")
                    sp.dma_start(ssm_m[n % 3][:], src).then_inc(ssm_in[n % 3], 16)

                ahead = {8: [0, 1, 2], 13: [3], 15: [4, 5], 22: [6], 24: [7, 8], 25: [9, 10], 26: [11]}
                for n, key in enumerate(MIX_CHUNKS):
                    for m in ahead.get(n, []):
                        load_ssm(m)
                    load(n, key, b * NMIX + n)
            with sp.Fori(0, NB) as b:
                base = NB * NMIX + b * NFFN
                for n in R(2 * KF):
                    m, up = n // 2, n % 2
                    load(n, ("fin", up * FF + m * P), base + n)
                for n in R(2 * KF, NFFN):
                    f, j = divmod(n - 2 * KF, KF // 2)
                    load(n, ("fout", f, j), base + n)

        for s_ in (tensor, scal, vec):
            s_.finished()


INPUTS = ["x", "c", "w_ada", "b_ada", "norm1_g", "w_in", "conv_w", "conv_b", "conv_ln_g", "conv_ln_b",
          "conv_proj", "ssm_a_re", "ssm_a_im", "ssm_b_re", "ssm_b_im", "ssm_c_re", "ssm_c_im",
          "ssm_d", "ssm_log_dt", "ssm_glu", "w_out", "norm2_g", "w_ffn_in", "w_ffn_out", "final_g"]


def kernel(**inputs):
    import concourse.bacc as bacc
    from concourse.bass_utils import run_bass_kernel_spmd

    nc = bacc.Bacc("TRN2", target_bir_lowering=False, num_devices=1, dynamic_dma_scratch_size=1024)
    arrays, args = {}, []
    for name in INPUTS:
        a = np.ascontiguousarray(inputs[name])
        arrays[f"in_{name}"] = a
        args.append(nc.dram_tensor(f"in_{name}", a.shape, mybir.dt.from_np(a.dtype), kind="ExternalInput").ap())
    shape = inputs["x"].shape
    args.append(nc.dram_tensor("out_0", shape, F32, kind="ExternalOutput").ap())
    build(nc, *args)
    result = run_bass_kernel_spmd(nc, [arrays], core_ids=[0])
    return result.results[0]["out_0"]
```

```python
from contextlib import ExitStack

import numpy as np

import concourse.bass as bass
from concourse import mybir

ALU = mybir.AluOpType
ACT = mybir.ActivationFunctionType
F32 = mybir.dt.float32
F32R = mybir.dt.float32r
BF16 = mybir.dt.bfloat16
I32 = mybir.dt.int32

P = 128
EPS = 1e-6


class Steps:

    def __init__(self, sem, phases):
        self.sem, self.at, self.base, self.per, self.names = sem, {}, {}, {}, {}
        total = 0
        for phase, times, segments in phases:
            n = 0
            names = []
            for seg, rep in segments:
                for j, name in enumerate(seg):
                    assert (phase, name) not in self.at, name
                    self.at[phase, name] = (n + j + 1, len(seg))
                names += seg
                n += len(seg) * rep
            self.base[phase], self.per[phase], self.names[phase] = total, n, names
            total += n * times
        self.next = {phase: 0 for phase, _, _ in phases}

    def step(self, phase, name):
        want = self.names[phase][self.next[phase]]
        assert want == name, f"{phase}: {name} where {want} stands"
        self.next[phase] += 1
        return self.sem, 1

    def after(self, phase, b, name, it=0):
        at, width = self.at[phase, name]
        return self.sem, self.base[phase] + at + b * self.per[phase] + it * width

    def before(self, phase, b, name, it=0):
        at, width = self.at[phase, name]
        round_ = self.per[phase] if it is None else width
        v = self.base[phase] + at - round_
        assert v >= 0, (phase, name, v)
        return self.sem, v + b * self.per[phase] + (0 if it is None else it * width)

    def start(self, phase, b):
        return self.sem, self.base[phase] + b * self.per[phase]

    def finished(self):
        for phase, n in self.next.items():
            assert n == len(self.names[phase]), (phase, self.names[phase][n])


def build(nc, x, c, w_ada, b_ada, norm1_g, w_in, conv_w, conv_b, conv_ln_g, conv_ln_b, conv_proj,
          ssm_a_re, ssm_a_im, ssm_b_re, ssm_b_im, ssm_c_re, ssm_c_im, ssm_d, ssm_log_dt, ssm_glu,
          w_out, norm2_g, w_ffn_in, w_ffn_out, final_g, out):
    SEQ, D = x.shape[1], x.shape[2]
    TAPS, CW = conv_w.shape[1], conv_w.shape[2]
    G, NST, HG = ssm_b_re.shape[1:]
    FF = w_ffn_out.shape[1]
    SW = G * HG
    TB = 512
    NB = SEQ // TB
    TT = TB // P
    KD = D // P
    KC = CW // P
    KS = SW // P
    KF = FF // P
    T = P // HG
    NC = TB // T
    GQ = 512 // NC
    NQ = G // GQ
    GT = P // HG
    HALO = TAPS - 1
    CH = 1024
    HALF = D // 2
    ADA = 3
    SLABS = [("pe", k, h, r) for k in range(5) for h in range(2) for r in range(2)]
    for n, at in enumerate((2, 7, 12, 17)):
        SLABS.insert(at, ("pool", 5, n // 2, n % 2))
    last_slab = lambda kind: SLABS.index(("pe", kind, 1, 1))
    first_gate = last_slab(1) + 1
    RAW, SPL = 3, 2
    assert 2 * NST == P and KC == 4 and KS == 4 and KD == 8 and NQ == 4 and x.shape[0] == 1
    assert KF % 2 == 0 and GT == T

    o_ssm, o_gl = 2 * CW, 2 * CW + SW
    MIX_CHUNKS = [("in", o_ssm + m * P) for m in range(KS)]
    for m in range(KC):
        MIX_CHUNKS += [("in", m * P), ("in", CW + m * P)]
    MIX_CHUNKS += [("in", o_gl + i * P) for i in range(2 * KD)]
    for p in range(KD // 2):
        MIX_CHUNKS += [("glu", 2 * p * P), ("glu", D + 2 * p * P)]
    MIX_CHUNKS += [("proj", 2 * p * P) for p in range(KD // 2)]
    MIX_CHUNKS += [("out", h, j) for h in range(2) for j in range(KD // 2)]
    NMIX = len(MIX_CHUNKS)
    FI = KF // 2
    NFFN = 2 * KF + 2 * (KF // 2)
    assert NMIX % (RAW * SPL) == 0 and NFFN % (RAW * SPL) == 0

    x2_d = nc.dram_tensor("x2_scratch", (SEQ, D), F32).ap()
    us_d = nc.dram_tensor("us_scratch", (SW, T, NC), F32).ap()
    ys_d = nc.dram_tensor("ys_scratch", (SW, T, NC), F32).ap()
    wt_d = nc.dram_tensor("wt_scratch", (P, G, P), F32).ap()
    vk_d = nc.dram_tensor("vk_scratch", (P, G, 2, P), F32).ap()

    x_d, out_d = x[0], out[0]
    win_d = w_in[0].rearrange("(k p) n -> p k n", p=P)
    proj_d = conv_proj[0].rearrange("(k p) n -> p k n", p=P)
    glu_d = ssm_glu[0].rearrange("(k p) n -> p k n", p=P)
    wout_d = w_out[0].rearrange("(k p) n -> p k n", p=P)
    fin_d = w_ffn_in[0].rearrange("(k p) n -> p k n", p=P)
    fout_d = w_ffn_out[0].rearrange("(k p) n -> p k n", p=P)
    ada_d = w_ada[0].rearrange("(k p) n -> p k n", p=P)

    with ExitStack() as ctx:
        cursor = [(nc.sbuf_base + 63) // 64 * 64]

        def place(name, shape, dtype=F32, at=None):
            size = int(np.prod(shape[1:])) * (2 if dtype == BF16 else 4)
            off = cursor[0] if at is None else at
            t = nc.alloc_sbuf_tensor_at(name, list(shape), dtype, offset=off)
            if at is None:
                cursor[0] = (off + size + 63) // 64 * 64
            return t

        raw_at = cursor[0]
        raw = [place(f"raw{s}", [P, CH]) for s in range(RAW)]
        w_hi = [place(f"w_hi{s}", [P, CH], F32R) for s in range(SPL)]
        w_lo = [place(f"w_lo{s}", [P, CH], F32R) for s in range(SPL)]
        h_at = cursor[0]
        h_hi = place("h_hi", [P, KD, TB], F32R)
        h_lo = place("h_lo", [P, KD, TB], F32R)
        tr_at = cursor[0]
        tr = [place(f"tr{s}", [P, TB]) for s in range(4)]
        dt_at = cursor[0]
        dt_ = [place(f"dt{s}", [P, TB]) for s in range(4)]
        junk = place("junk", [P, D], BF16)
        g2b = place("g2b", [P, D])
        ident = place("ident", [P, P])
        turn = place("turn", [P, P])
        mean_w = place("mean_w", [P, P])
        zero1 = place("zero1", [P, 1])
        eps1 = place("eps1", [P, 1])
        half_pi = place("half_pi", [P, 1])
        sign = place("sign", [P, 1])
        nsign = place("nsign", [P, 1])
        mod = place("mod", [P, 4 * KD])
        vt = place("vt", [P, 6 * KD + 3 * KD + 3 * KC])
        bmod, c_in, ng = vt[:, 0:6 * KD], vt[:, 6 * KD:7 * KD], vt[:, 7 * KD:9 * KD]
        cvec = vt[:, 9 * KD:].rearrange("p (a k) -> p a k", a=3)
        scale = [place(f"scale{n}", [P, KD]) for n in range(2)]
        ss = place("ss", [P, TT])
        sd = place("sd", [P, TT])
        rs = place("rs", [P, TT])
        over = cursor[0]
        g1b = place("g1b", [P, D])
        uc = place("uc", [P, KC, HALO + TB])
        cwt = place("cwt", [P, KC, TAPS])
        carry = place("carry", [P, G])
        ctmp = place("ctmp", [P, G])
        mag_t = place("mag_t", [P, G])
        cos_t = place("cos_t", [P, NC + 1, G])
        sin_t = place("sin_t", [P, NC + 1, G])
        kept = cursor[0]
        ssm_m = [place(f"ssm_m{s}", [P, CH]) for s in range(3)]
        xr = [place(f"xr{s}", [P, HALF]) for s in range(4)]
        yn_at = cursor[0]
        yn_hi = place("yn_hi", [P, KC, TB], F32R)
        ync_at = cursor[0]
        yn_lo = place("yn_lo", [P, KC, TB], F32R)
        ys_hi = place("ys_hi", [P, KS, TB], F32R)
        yz_at = cursor[0]
        ys_lo = place("ys_lo", [P, KS, TB], F32R)
        mc_at = cursor[0]
        m_hi = place("m_hi", [P, KD, TB], F32R)
        ms_at = cursor[0]
        m_lo = place("m_lo", [P, KD, TB], F32R)
        end_kept = cursor[0]
        xs = place("xs", [P, TT, D])
        uz = place("uz", [P, KS, T, NC], at=yn_at)
        sq = place("sq", [P, KC, TB], at=yn_at)
        yc = place("yc", [P, KC, TB], at=ync_at)
        yz = place("yz", [P, KS, T, NC], at=yz_at)
        sg_c = place("sg_c", [P, KD, TB], at=mc_at)
        sg_s = place("sg_s", [P, KD, TB], at=ms_at)
        cursor[0] = end_kept
        u8 = place("u8", [P, G, NC])
        wst = place("wst", [P, G, NC + 1])
        cursor[0] = over
        hid_hi = place("hid_hi", [P, KF, TB], F32R)
        hid_lo = place("hid_lo", [P, KF, TB], F32R)
        x3 = place("x3", [P, TT, D])
        fgb = place("fgb", [P, D])
        assert cursor[0] <= end_kept
        cursor[0] = kept
        vm = place("vm", [P, G, T + 1, HG])
        wm = place("wm", [P, G, T, HG])
        bx1 = place("bx1", [P, G, HG])
        bx2 = place("bx2", [P, G, HG])
        b1 = place("b1", [P, G, HG])
        b2 = place("b2", [P, G, HG])
        c1 = place("c1", [P, G, HG])
        c2 = place("c2", [P, G, HG])
        cx = place("cx", [P, 2, 4, P])
        ptmp_at = cursor[0]
        ptmp = place("ptmp", [P, G, HG])
        modrow = place("modrow", [4, HALF], at=ptmp_at)
        jexp = place("jexp", [P, T + 1, G])
        jer = place("jer", [P, T + 1, G])
        jei = place("jei", [P, T + 1, G])
        sv = place("sv", [P, 12, G])
        iota_i = place("iota_i", [P, NC + 1], I32)
        iota_f = place("iota_f", [P, NC + 1])
        cact = place("cact", [P, KD])
        dvec = place("dvec", [HG, G])
        cbc = place("cbc", [P, KD, P])
        ones = place("ones", [P, P])
        zc = place("zc", [P, KD, 7])
        ddiag = place("ddiag", [HG, G, HG])
        nat_v = place("nat_v", [6 * KD + 3 * KD + 3 * KC, P])
        nat_a = place("nat_a", [2 * G, P])
        nat_w = place("nat_w", [KC * TAPS, P])
        kst_at = end_kept - (T - 1) * G * HG * 4
        assert cursor[0] <= kst_at, (cursor[0], kst_at)
        kst = place("kst", [HG, G, 2 * T - 1, HG], at=kst_at)
        ada = [place(f"ada{s}", [P, KD // 2, HALF], at=raw_at + s * KD * HALF * 2) for s in range(ADA)]
        acc = place("acc", [P, 2, HALF], at=raw_at + ADA * KD * HALF * 2)
        bg = place("bg", [P, 2, D], at=dt_at)
        cursor[0] = h_at
        karg = place("karg", [P, 2, NC + 1, G])
        ktmp = place("ktmp", [P, NC + 1, G])
        jarg = place("jarg", [P, 2, T + 1, G])
        jtmp = place("jtmp", [P, T + 1, G])
        assert cursor[0] <= tr_at

        bank = [ctx.enter_context(nc.psum_tensor(f"bank{i}", [P, 512], F32)) for i in range(8)]
        Z, Q = [0, 1, 2, 3], [4, 5, 6, 7]

        def sem(name):
            return ctx.enter_context(nc.semaphore(name))

        R = range
        norm_act = ["ns0", "ns1", "ns2", "ns3", "nsd"]
        norm_dve = ["nms", "nr", "nx0", "nx1", "nx2", "nx3"]
        h_steps = [f"h{k}" for k in R(KD)]
        hh = lambda k: [f"hh{k}", f"hl{k}"]
        h_dve = [n for k in R(KD) for n in hh(k)]

        GL = [0, 2, 5, 7]
        pair = lambda p: (2 * p, 2 * p + 1)
        gl = lambda lo, hi: [f"gl{i}" for i in R(lo, hi)]
        pe_mix = [f"us{m}" for m in R(KS)] + [f"u{a}{m}" for m in R(KC) for a in "ag"]
        pe_mix += [f"S{q}" for q in R(NQ)] + gl(0, GL[1]) + [f"R{q}" for q in R(NQ)]
        pe_mix += gl(GL[1], GL[2]) + [f"D{q}" for q in R(NQ)] + ["dc"] + gl(GL[2], GL[3])
        for q in R(NQ):
            pe_mix += [f"Y{q}", f"gl{GL[3] + q}"]
        pe_mix += gl(GL[3] + NQ, 2 * KD)
        for p in R(KD // 2):
            pe_mix += [f"{a}{m}" for a in ("za", "zb") for m in pair(p)]
            pe_mix += [["ln1"], ["ln2"], [], []][p]
        for p in R(KD // 2):
            pe_mix += [f"h{k}" for k in pair(p)] + [f"cp{m}" for m in pair(p)]
        for f in R(2):
            pe_mix += [f"oc{f}{j}" for j in R(KD // 2 - 1)] + [f"o{f}{i}" for i in R(TT)]
        pe_loop = ["fg0", "fu0", "fg1", "fu1"]
        pe_out = []
        for f in R(2):
            for j in R(KF // 2 - 1):
                pe_out += [f"fc{f}_{j}"] + ([f"h{j - 1}"] if f == 0 and 1 <= j <= KD else [])
            pe_out += [f"p{f}{i}" for i in R(TT)]
        ada_steps = lambda lo, hi: [f"ada{n}" for n in R(lo, hi) if SLABS[n][0] == "pe"]
        pe_pro = ["v0", "v1", "v2"] + ada_steps(0, first_gate) + ["mt", "ct0", "ct1"] + h_steps
        pe_pro += ada_steps(first_gate, last_slab(3) + 1) + [f"wt{n}" for n in R(8)]
        pe_pro += ada_steps(last_slab(3) + 1, len(SLABS)) + ["mt2", "sg0", "sg1"]
        pe_pro += [f"kk{n}" for n in R(8)]
        tensor = Steps(sem("tensor_done"), [
            ("pro", 1, [(pe_pro, 1)]), ("mix", NB, [(pe_mix, 1)]), ("mid", 1, [(h_steps, 1)]),
            ("ffn", NB, [(pe_loop, FI), (pe_out, 1)])])

        act_mix = [f"us{m}" for m in R(KS)] + [f"ug{m}" for m in R(KC)] + [f"S{q}" for q in R(NQ)]
        act_mix += gl(0, GL[3])
        for q in R(NQ):
            act_mix += [f"Y{q}", f"gl{GL[3] + q}"]
        act_mix += gl(GL[3] + NQ, 2 * KD - 2) + [f"ge{m}" for m in R(KS)] + gl(2 * KD - 2, 2 * KD)
        act_mix += ["zb0", "zb1"] + [f"sq{m}" for m in R(KC)] + ["zb2", "zb3", "lsd"] + norm_act
        act_mix += ["si0", "si1", "zb4", "zb5", "si2", "si3", "zb6", "zb7"] + h_steps
        act_loop = ["fs0", "fs1"]
        act_out = norm_act + h_steps + [f"fq{i}" for i in R(TT)] + ["fsd"]
        act_pro = ["cs", "dt", "ej", "m8", "sj", "cj", "sk", "ck"] + norm_act + h_steps
        act_pro += [f"wt{n}" for n in R(8)] + [f"kk{n}" for n in R(8)]
        scal = Steps(sem("scalar_done"), [
            ("pro", 1, [(act_pro, 1)]), ("mix", NB, [(act_mix, 1)]), ("mid", 1, [(norm_act + h_steps, 1)]),
            ("ffn", NB, [(act_loop, FI), (act_out, 1)])])

        CUT = [0, 7, 8, 26, TAPS]
        taps = lambda n: [f"c{t}_{m}" for t in R(CUT[n], CUT[n + 1]) for m in R(KC)]
        dve_mix = [f"u{m}" for m in R(KC)] + taps(0)
        for q in R(NQ):
            dve_mix += [f"Rt{q}", f"Rc{q}"]
        dve_mix += [f"Rs{q}" for q in R(NQ)] + ["in"] + [f"sc{g}" for g in R(G)]
        dve_mix += taps(1)
        for q in R(NQ):
            dve_mix += [f"Dt{q}", f"Dc{q}"]
        dve_mix += ["dc1", "dc2"] + [f"Ds{q}" for q in R(NQ)] + ["dc3"]
        zz = lambda p: [f"{a}{m}" for a in ("ms", "mt") for m in pair(p)]
        dve_mix += taps(2) + [f"{a}{m}" for m in R(KS) for a in ("ysh", "ysl")] + taps(3) + ["halo"]
        dve_mix += zz(0) + [f"cen{m}" for m in R(KC)] + zz(1) + ["rec"] + [f"nm{m}" for m in R(KC)]
        dve_mix += norm_dve + zz(2) + [f"{a}{m}" for m in R(KC) for a in ("ynh", "ynl")] + zz(3)
        for p in R(KD // 2):
            dve_mix += [n for k in pair(p) for n in hh(k)]
            dve_mix += [f"{a}{m}" for a in ("mc", "ma", "mh", "ml") for m in pair(p)]
        for f in R(2):
            dve_mix += [n for i in R(TT) for n in (f"oa{f}{i}", f"ob{f}{i}")]
        dve_loop = [f"{a}{j}" for a in ("fm", "fh", "fl") for j in R(2)]
        dve_out = norm_dve + h_dve
        for f in R(2):
            dve_out += [n for i in R(TT) for n in (f"pa{f}{i}", f"pb{f}{i}")]
        dve_out += ["fms", "fr"] + [f"fx{i}" for i in R(TT)]
        vec = Steps(sem("vector_done"), [
            ("pro", 1, [(norm_dve + h_dve, 1)]), ("mix", NB, [(dve_mix, 1)]),
            ("mid", 1, [(norm_dve + h_dve, 1)]), ("ffn", NB, [(dve_loop, FI), (dve_out, 1)])])

        def is_z(n):
            return n[0] in "uzh" or n[:2] in ("gl", "cp") or n[:2] in ("fg", "fu")

        plan = {}
        for phase, names in (("pro", h_steps), ("mix", pe_mix), ("mid", h_steps), ("ffn", pe_loop + pe_out)):
            z = 0
            for n in names:
                if n[:2] in ("oc", "fc"):
                    continue
                if is_z(n) or n[:2] in ("o0", "p1"):
                    plan[phase, n] = z % 4
                    z += 1
            assert z % 4 == 0
        for q in R(NQ):
            plan["mix", f"S{q}"] = 4 + q % 2
            plan["mix", f"R{q}"] = 6 + q % 2
            plan["mix", f"D{q}"] = 4 + q % 2
            plan["mix", f"Y{q}"] = 6 + q % 2
        plan["mix", "dc"], plan["mix", "ln1"], plan["mix", "ln2"] = 6, 4, 5
        for i in R(TT):
            plan["mix", f"o1{i}"] = plan["ffn", f"p0{i}"] = 4 + i

        def reader(phase, n):
            if n[:2] in ("us", "gl", "zb", "ug") or n[0] in "hSY":
                return scal, n
            if n == "ln2":
                return scal, "lsd"
            if n[0] in "RD":
                return vec, n[0] + "t" + n[1]
            return vec, {"ua": "u" + n[2:], "dc": "dc1", "ln": "cen3", "cp": "mc" + n[2:], "za": "ms" + n[2:],
                         "o0": "oa" + n[1:], "o1": "oa" + n[1:], "p0": "pa" + n[1:], "p1": "pa" + n[1:],
                         "fu": "fm" + n[2:]}[n[:2]] if n[:2] != "fg" else None

        order = {"pro": h_steps, "mix": pe_mix, "mid": h_steps, "ffn": pe_loop + pe_out}

        def bank_free(phase, b, n, it=0):
            use = [m for m in order[phase] if plan.get((phase, m)) == plan[phase, n]]
            j = use.index(n)
            if j and not (n in pe_loop):
                who, step = reader(phase, use[j - 1]) if use[j - 1][:2] != "fg" else (scal, "fs" + use[j - 1][2])
                last = FI - 1 if use[j - 1] in pe_loop else 0
                return who.after(phase, b, step, last)
            if n in pe_loop:
                who, step = (scal, "fs" + n[2]) if n[:2] == "fg" else (vec, "fm" + n[2])
                return who.before(phase, b, step, it)
            who, step = reader(phase, use[-1])
            return who.before(phase, b, step, None)

        raw_in = [sem(f"raw_in{s}") for s in R(RAW)]
        hi_done = sem("hi_done")
        split_done = sem("split_done")
        ssm_in = [sem(f"ssm_in{s}") for s in R(3)]
        xs_in = sem("xs_in")
        uz_out, u8_in, y_out, yz_in = sem("uz_out"), sem("u8_in"), sem("y_out"), sem("yz_in")
        xr_in = [sem(f"xr_in{s}") for s in R(4)]
        x2_out = [sem(f"x2_out{s}") for s in R(4)]
        x3_in, final_out = sem("x3_in"), sem("final_out")
        vectors_in = sem("vectors_in")
        small_in = sem("small_in")
        bg_in = sem("bg_in")
        consts = sem("consts")
        ada_in = [sem(f"ada_in{s}") for s in R(ADA)]
        acc_done = sem("acc_done")
        acc_link = sem("acc_link")
        pro_v = sem("prologue_vector")
        mat_out = sem("mat_out")
        fg_in = sem("fg_in")
        SMALL_LOADS = 4 + 4 + 1
        mark = {}

        chunk_no = {}
        n = 0
        for s in pe_mix:
            if s[:2] in ("us", "gl", "ua", "ug", "oc") or s in ("o03", "o13") or (
                    s[:2] in ("cp", "za", "zb") and int(s[2]) % 2):
                n += 1
                chunk_no["mix", n] = s
        assert n == NMIX
        n = 2 * KF
        for s in pe_out:
            if s[:2] == "fc" or s in ("p03", "p13"):
                n += 1
                chunk_no["ffn", n] = s
        assert n == NFFN

        def chunk_used(phase, b, n, it=0):
            return tensor.after(phase, b, chunk_no[phase, n])

        block = ctx.enter_context(nc.Block())

        @block.vector
        def _(dve):
            v = nc.vector

            def link(ins, name=None):
                mark["n"] = mark.get("n", 0) + 1
                ins.then_inc(pro_v, 1)
                dve.wait_ge(pro_v, mark["n"])
                if name:
                    mark[name] = mark["n"]

            dve.wait_ge(consts, 9)
            TWO_PI = 2 * np.pi
            c1_ = float(np.float32(6.28125))
            c2_ = float(np.float32(TWO_PI - 6.28125))
            MAGIC = float(1.5 * 2 ** 23)
            PI_ = float(np.float32(3.1415925))

            def reduce_angle(dst, src, tmp):
                link(v.tensor_scalar(tmp, src, float(1 / TWO_PI), MAGIC, ALU.mult, ALU.add))
                link(v.tensor_scalar(tmp, tmp, MAGIC, None, ALU.subtract))
                link(v.scalar_tensor_tensor(out=dst, in0=tmp, scalar=-c1_, in1=src, op0=ALU.mult, op1=ALU.add))
                link(v.scalar_tensor_tensor(out=dst, in0=tmp, scalar=-c2_, in1=dst, op0=ALU.mult, op1=ALU.add))
                link(v.tensor_scalar(dst, dst, PI_, -PI_, ALU.min, ALU.max))

            def angles(table, tmp, angle, n, name):
                flat = lambda a: a.rearrange("p a b -> p (a b)")
                steps = iota_f[:, 0:n].unsqueeze(2).broadcast_to([P, n, G])
                link(v.tensor_tensor(table[:, 0, :, :], steps, angle.unsqueeze(1).broadcast_to([P, n, G]), ALU.mult))
                reduce_angle(flat(table[:, 0, :, :]), flat(table[:, 0, :, :]), flat(tmp[:, :, :]))
                x_ = flat(table[:, 0, :, :])
                link(v.scalar_tensor_tensor(out=flat(table[:, 1, :, :]), in0=x_, scalar=-1.0, in1=x_,
                                            op0=ALU.mult, op1=ALU.min), name)

            def wait_self(phase, b, name, it=0):
                dve.wait_ge(*vec.after(phase, b, name, it))

            def split(hi, lo, src, steps, phase, b, it=0):
                v.tensor_copy(hi, src).then_inc(*vec.step(phase, steps[0]))
                wait_self(phase, b, steps[0], it)
                v.tensor_tensor(lo, src, hi.bitcast(F32), ALU.subtract).then_inc(*vec.step(phase, steps[1]))

            def norm_scale(phase, b):
                dve.wait_ge(*scal.after(phase, b, "ns3"))
                v.tensor_scalar(ss[:], ss[:], 1.0 / D, EPS, ALU.mult, ALU.add).then_inc(*vec.step(phase, "nms"))
                dve.wait_ge(*scal.after(phase, b, "nsd"))
                v.reciprocal(rs[:], sd[:]).then_inc(*vec.step(phase, "nr"))
                wait_self(phase, b, "nr")
                for i in R(TT):
                    v.tensor_scalar(xs[:, i, :], xs[:, i, :], rs[:, i:i + 1], None, ALU.mult)\
                        .then_inc(*vec.step(phase, f"nx{i}"))

            def h_split(phase, b, k):
                dve.wait_ge(*scal.after(phase, b, f"h{k}"))
                split(h_hi[:, k, :], h_lo[:, k, :], tr[k % 4][:], hh(k), phase, b)

            def scale_of(which):
                link(v.tensor_scalar(scale[which][:], mod[:, (2 * which + 1) * KD:(2 * which + 2) * KD],
                                     1.0, None, ALU.add))
                link(v.tensor_tensor(scale[which][:], scale[which][:], ng[:, which * KD:(which + 1) * KD],
                                     ALU.mult), f"scale{which}")

            def shift_and_scale(which):
                dve.wait_ge(*tensor.after("pro", 0, f"ada{last_slab((1, 4)[which])}"))
                link(v.tensor_copy(modrow[:], bank[5][0:4, :]), f"modrow{which}")
                dve.wait_ge(*tensor.after("pro", 0, ("mt", "mt2")[which]))
                by_row = lambda a: a.rearrange("p (r j) -> p r j", j=4)
                link(v.tensor_tensor(by_row(mod[:, 2 * which * KD:2 * (which + 1) * KD]),
                                     bank[6][:, 0:16].rearrange("p (j r) -> p r j", j=4),
                                     by_row(bmod[:, 3 * which * KD:(3 * which + 2) * KD]), ALU.add))
                scale_of(which)

            dve.wait_ge(*tensor.after("pro", 0, "v2"))
            nv = 6 * KD + 3 * KD + 3 * KC
            link(v.tensor_copy(sv[:, 0:2, :].rearrange("p a g -> p (a g)"), bank[0][:, 0:2 * G]))
            link(v.tensor_copy(vt[:], bank[1][:, 0:nv]), "vt")
            link(v.tensor_copy(cwt[:].rearrange("p m t -> p (m t)"), bank[2][:, 0:KC * TAPS]))
            dve.wait_ge(*scal.after("pro", 0, "cs"))
            link(v.tensor_copy(zc[:, :, 3], cact[:]), "zc")
            link(v.tensor_copy(cbc[:], cact[:].unsqueeze(2).broadcast_to([P, KD, P])), "cbc")
            ar, ai, dt, th, lg, ph, t0, t1 = (sv[:, n, :] for n in R(8))
            qr, qi, nr, den = (sv[:, n, :] for n in R(8, 12))
            dve.wait_ge(*scal.after("pro", 0, "dt"))
            link(v.tensor_tensor(lg, dt, ar, ALU.mult))
            link(v.tensor_tensor(jexp[:], iota_f[:, 0:T + 1].unsqueeze(2).broadcast_to([P, T + 1, G]),
                                 lg.unsqueeze(1).broadcast_to([P, T + 1, G]), ALU.mult))
            link(v.tensor_tensor(th, dt, ai, ALU.mult))
            reduce_angle(th, th, t0)
            angles(jarg, jtmp, th, T + 1, "jargs")
            flat2 = lambda a: a[:].rearrange("p a b -> p (a b)")
            link(v.tensor_scalar(ph, th, float(T), None, ALU.mult))
            reduce_angle(ph, ph, t0)
            angles(karg, ktmp, ph, NC + 1, "kargs")
            dve.wait_ge(*scal.after("pro", 0, "cj"))
            link(v.tensor_tensor(jer[:], jexp[:], jer[:], ALU.mult))
            link(v.tensor_tensor(jei[:], jexp[:], jei[:], ALU.mult))
            e_r, e_i = jer[:, 1, :], jei[:, 1, :]
            link(v.tensor_scalar(nr, e_r, -1.0, None, ALU.add))
            link(v.tensor_tensor(t0, ar, ar, ALU.mult))
            link(v.tensor_tensor(t1, ai, ai, ALU.mult))
            link(v.tensor_tensor(den, t0, t1, ALU.add))
            link(v.reciprocal(den, den))
            link(v.tensor_tensor(t0, nr, ar, ALU.mult))
            link(v.tensor_tensor(t1, e_i, ai, ALU.mult))
            link(v.tensor_tensor(qr, t0, t1, ALU.add))
            link(v.tensor_tensor(qr, qr, den, ALU.mult))
            link(v.tensor_tensor(t0, e_i, ar, ALU.mult))
            link(v.tensor_tensor(t1, nr, ai, ALU.mult))
            link(v.tensor_tensor(qi, t0, t1, ALU.subtract))
            link(v.tensor_tensor(qi, qi, den, ALU.mult))

            def by_h(a):
                return a.unsqueeze(2).broadcast_to([P, G, HG])

            dve.wait_ge(small_in, SMALL_LOADS * 16)
            link(v.tensor_tensor(b1[:], bx1[:], by_h(qr), ALU.mult))
            link(v.tensor_tensor(ptmp[:], bx2[:], by_h(qi), ALU.mult))
            link(v.scalar_tensor_tensor(out=flat2(b1), in0=flat2(ptmp), scalar=sign[:, 0:1], in1=flat2(b1),
                                        op0=ALU.mult, op1=ALU.add))
            link(v.tensor_tensor(b2[:], bx2[:], by_h(qr), ALU.mult))
            link(v.tensor_tensor(ptmp[:], bx1[:], by_h(qi), ALU.mult))
            link(v.scalar_tensor_tensor(out=flat2(b2), in0=flat2(b2), scalar=sign[:, 0:1], in1=flat2(ptmp),
                                        op0=ALU.mult, op1=ALU.subtract))
            norm_scale("pro", 0)
            shift_and_scale(0)
            dve.wait_ge(*tensor.after("pro", 0, "ct1"))
            link(v.tensor_scalar(flat2(c1), bank[3][:], nsign[:, 0:1], None, ALU.mult))
            link(v.tensor_scalar(flat2(c2), bank[4][:], -1.0, None, ALU.mult), "cc")
            for s in R(T):
                j = T - 1 - s
                link(v.tensor_tensor(wm[:, :, s, :], b1[:], by_h(jer[:, j, :]), ALU.mult))
                link(v.tensor_tensor(ptmp[:], b2[:], by_h(jei[:, j, :]), ALU.mult))
                link(v.tensor_tensor(wm[:, :, s, :], wm[:, :, s, :], ptmp[:], ALU.add), "wm" if s == T - 1 else None)
            for k in R(KD):
                h_split("pro", 0, k)
            for j in R(T + 1):
                link(v.tensor_tensor(vm[:, :, j, :], c1[:], by_h(jer[:, j, :]), ALU.mult))
                link(v.tensor_tensor(ptmp[:], c2[:], by_h(jei[:, j, :]), ALU.mult))
                link(v.tensor_tensor(vm[:, :, j, :], vm[:, :, j, :], ptmp[:], ALU.add), "vm" if j == T else None)
            dve.wait_ge(bg_in, 32)
            for h in R(2):
                cols = slice(h * HALF, (h + 1) * HALF)
                dve.wait_ge(*tensor.after("pro", 0, f"ada{SLABS.index(('pe', 2, h, 1))}"))
                link(v.tensor_tensor(g1b[:, cols], bank[(4, 7)[h]][:], bg[:, 0, cols], ALU.add), f"g1b{h}")
            shift_and_scale(1)
            for h in R(2):
                cols = slice(h * HALF, (h + 1) * HALF)
                dve.wait_ge(*tensor.after("pro", 0, f"sg{h}"))
                link(v.tensor_tensor(g2b[:, cols], bank[6 + h][:], bg[:, 1, cols], ALU.add), "g2b")
            link(v.tensor_tensor(ddiag[:], ident[0:HG, 0:HG].unsqueeze(1).broadcast_to([HG, G, HG]),
                                 dvec[:].unsqueeze(2).broadcast_to([HG, G, HG]), ALU.mult))
            dve.wait_ge(*scal.after("pro", 0, "kk7"))
            link(v.tensor_tensor(kst[:, :, T - 1, :], kst[:, :, T - 1, :], ddiag[:], ALU.add), "kst")

            with dve.Fori(0, NB) as b:
                for m in R(KC):
                    dve.wait_ge(*scal.after("mix", b, f"ug{m}"))
                    v.tensor_tensor(uc[:, m, HALO:], bank[plan["mix", f"ua{m}"]][:], tr[m][:], ALU.mult)\
                        .then_inc(*vec.step("mix", f"u{m}"))

                def conv(part):
                    for t in R(CUT[part], CUT[part + 1]):
                        for m in R(KC):
                            src = uc[:, m, t:t + TB]
                            w = cwt[:, m, t:t + 1]
                            if t == 0:
                                wait_self("mix", b, f"u{m}")
                                ins = v.tensor_scalar(yc[:, m, :], src, w, cvec[:, 0, m:m + 1], ALU.mult, ALU.add)
                            else:
                                wait_self("mix", b, f"c{t - 1}_{m}")
                                ins = v.scalar_tensor_tensor(out=yc[:, m, :], in0=src, scalar=w, in1=yc[:, m, :],
                                                             op0=ALU.mult, op1=ALU.add)
                            ins.then_inc(*vec.step("mix", f"c{t}_{m}"))

                def quarter(a, q, lo, hi_):
                    return a[:, q * GQ:(q + 1) * GQ, lo:hi_]

                def table(t, q, lo, hi_):
                    return t[:, lo:hi_, q * GQ:(q + 1) * GQ].rearrange("p k g -> p g k")

                def by_g(a):
                    return a.rearrange("p (g k) -> p g k", g=GQ)

                conv(0)
                for q in R(NQ):
                    dve.wait_ge(*tensor.after("mix", b, f"R{q}"))
                    v.tensor_tensor(by_g(dt_[q][:]), by_g(bank[plan["mix", f"R{q}"]][:]), table(sin_t, q, 1, NC + 1),
                                    ALU.mult).then_inc(*vec.step("mix", f"Rt{q}"))
                    v.tensor_tensor(quarter(wst, q, 1, NC + 1), quarter(wst, q, 1, NC + 1), table(cos_t, q, 1, NC + 1),
                                    ALU.mult).then_inc(*vec.step("mix", f"Rc{q}"))
                for q in R(NQ):
                    wait_self("mix", b, f"Rc{q}")
                    v.tensor_tensor(quarter(wst, q, 1, NC + 1), quarter(wst, q, 1, NC + 1), by_g(dt_[q][:]),
                                    ALU.add).then_inc(*vec.step("mix", f"Rs{q}"))
                v.tensor_copy(wst[:, :, 0], carry[:]).then_inc(*vec.step("mix", "in"))
                for g in R(G):
                    if g == 0:
                        wait_self("mix", b, "in")
                    v.tensor_tensor_scan(wst[:, g, 1:], mag_t[:, g:g + 1].broadcast_to([P, NC]), wst[:, g, 1:],
                                         carry[:, g:g + 1], ALU.mult, ALU.add).then_inc(*vec.step("mix", f"sc{g}"))
                conv(1)
                for q in R(NQ):
                    dve.wait_ge(*tensor.after("mix", b, f"D{q}"))
                    v.tensor_tensor(by_g(dt_[q][:]), by_g(bank[plan["mix", f"D{q}"]][:]), table(sin_t, q, 0, NC),
                                    ALU.mult).then_inc(*vec.step("mix", f"Dt{q}"))
                    v.tensor_tensor(quarter(wst, q, 0, NC), quarter(wst, q, 0, NC), table(cos_t, q, 0, NC),
                                    ALU.mult).then_inc(*vec.step("mix", f"Dc{q}"))
                dve.wait_ge(*tensor.after("mix", b, "dc"))
                v.tensor_tensor(ctmp[:], bank[plan["mix", "dc"]][:, 0:G], sin_t[:, NC, :], ALU.mult)\
                    .then_inc(*vec.step("mix", "dc1"))
                v.tensor_tensor(carry[:], wst[:, :, NC], cos_t[:, NC, :], ALU.mult).then_inc(*vec.step("mix", "dc2"))
                for q in R(NQ):
                    wait_self("mix", b, f"Dc{q}")
                    v.tensor_tensor(quarter(wst, q, 0, NC), quarter(wst, q, 0, NC), by_g(dt_[q][:]),
                                    ALU.subtract).then_inc(*vec.step("mix", f"Ds{q}"))
                wait_self("mix", b, "dc2")
                v.tensor_tensor(carry[:], carry[:], ctmp[:], ALU.subtract).then_inc(*vec.step("mix", "dc3"))
                conv(2)
                for m in R(KS):
                    dve.wait_ge(*scal.after("mix", b, f"ge{KS - 1}"))
                    split(ys_hi[:, m, :], ys_lo[:, m, :], tr[m][:], (f"ysh{m}", f"ysl{m}"), "mix", b)
                conv(3)
                v.tensor_copy(uc[:, :, 0:HALO], uc[:, :, TB:]).then_inc(*vec.step("mix", "halo"))

                def gated_ssm(p):
                    for m in pair(p):
                        dve.wait_ge(*scal.after("mix", b, f"zb{m}"))
                        if p:
                            wait_self("mix", b, f"mt{m - 2}")
                        v.tensor_tensor(dt_[m % 2][:], bank[plan["mix", f"za{m}"]][:], tr[m % 2][:], ALU.mult)\
                            .then_inc(*vec.step("mix", f"ms{m}"))
                    for m in pair(p):
                        wait_self("mix", b, f"ms{m}")
                        v.tensor_tensor(sg_s[:, m, :], dt_[m % 2][:], sg_s[:, m, :], ALU.mult)\
                            .then_inc(*vec.step("mix", f"mt{m}"))

                gated_ssm(0)
                dve.wait_ge(*tensor.after("mix", b, "ln1"))
                for m in R(KC):
                    v.tensor_tensor(yc[:, m, :], yc[:, m, :], bank[plan["mix", "ln1"]][:], ALU.subtract)\
                        .then_inc(*vec.step("mix", f"cen{m}"))
                gated_ssm(1)
                dve.wait_ge(*scal.after("mix", b, "lsd"))
                v.reciprocal(dt_[3][:], dt_[2][:]).then_inc(*vec.step("mix", "rec"))
                wait_self("mix", b, "rec")
                for m in R(KC):
                    v.tensor_tensor(yc[:, m, :], yc[:, m, :], dt_[3][:], ALU.mult).then_inc(*vec.step("mix", f"nm{m}"))
                norm_scale("mix", b)
                gated_ssm(2)
                for m in R(KC):
                    dve.wait_ge(*scal.after("mix", b, f"si{m}"))
                    split(yn_hi[:, m, :], yn_lo[:, m, :], tr[2 + m % 2][:], (f"ynh{m}", f"ynl{m}"), "mix", b)
                gated_ssm(3)
                for p in R(KD // 2):
                    for k in pair(p):
                        h_split("mix", b, k)
                    for m in pair(p):
                        dve.wait_ge(*tensor.after("mix", b, f"cp{m}"))
                        if p:
                            wait_self("mix", b, f"ml{m - 2}")
                        v.tensor_tensor(dt_[m % 2][:], bank[plan["mix", f"cp{m}"]][:], sg_c[:, m, :], ALU.mult)\
                            .then_inc(*vec.step("mix", f"mc{m}"))
                    for m in pair(p):
                        wait_self("mix", b, f"mc{m}")
                        v.tensor_tensor(dt_[m % 2][:], dt_[m % 2][:], sg_s[:, m, :], ALU.add)\
                            .then_inc(*vec.step("mix", f"ma{m}"))
                    for m in pair(p):
                        wait_self("mix", b, f"ma{m}")
                        v.tensor_copy(m_hi[:, m, :], dt_[m % 2][:]).then_inc(*vec.step("mix", f"mh{m}"))
                    for m in pair(p):
                        wait_self("mix", b, f"mh{m}")
                        v.tensor_tensor(m_lo[:, m, :], dt_[m % 2][:], m_hi[:, m, :].bitcast(F32), ALU.subtract)\
                            .then_inc(*vec.step("mix", f"ml{m}"))
                for f in R(2):
                    for i in R(TT):
                        dve.wait_ge(*tensor.after("mix", b, f"o{f}{i}"))
                        v.tensor_tensor(dt_[i][:], bank[plan["mix", f"o{f}{i}"]][:], g1b[:, f * HALF:(f + 1) * HALF],
                                        ALU.mult).then_inc(*vec.step("mix", f"oa{f}{i}"))
                        dve.wait_ge(xr_in[i], 16 * (2 * b + f + 1))
                        wait_self("mix", b, f"oa{f}{i}")
                        v.tensor_tensor(xr[i][:], xr[i][:], dt_[i][:], ALU.add).then_inc(*vec.step("mix", f"ob{f}{i}"))

            norm_scale("mid", 0)
            for k in R(KD):
                h_split("mid", 0, k)

            with dve.Fori(0, NB) as b:
                with dve.Fori(0, FI) as it:
                    for j in R(2):
                        dve.wait_ge(*scal.after("ffn", b, f"fs{j}", it))
                        dve.wait_ge(*tensor.after("ffn", b, f"fu{j}", it))
                        dve.wait_ge(*vec.before("ffn", b, f"fl{j}", it))
                        v.tensor_tensor(dt_[j][:], bank[plan["ffn", f"fu{j}"]][:], tr[j][:], ALU.mult)\
                            .then_inc(*vec.step("ffn", f"fm{j}"))
                    hid = lambda t, j: t[:, bass.ds(2 * it + j, 1), :]
                    one = lambda a: a.unsqueeze(1)
                    for j in R(2):
                        wait_self("ffn", b, f"fm{j}", it)
                        v.tensor_copy(hid(hid_hi, j), one(dt_[j][:])).then_inc(*vec.step("ffn", f"fh{j}"))
                    for j in R(2):
                        wait_self("ffn", b, f"fh{j}", it)
                        v.tensor_tensor(hid(hid_lo, j), one(dt_[j][:]), hid(hid_hi, j).bitcast(F32), ALU.subtract)\
                            .then_inc(*vec.step("ffn", f"fl{j}"))
                norm_scale("ffn", b)
                for k in R(KD):
                    h_split("ffn", b, k)
                for f in R(2):
                    for i in R(TT):
                        dve.wait_ge(*tensor.after("ffn", b, f"p{f}{i}"))
                        v.tensor_tensor(dt_[i][:], bank[plan["ffn", f"p{f}{i}"]][:], g2b[:, f * HALF:(f + 1) * HALF],
                                        ALU.mult).then_inc(*vec.step("ffn", f"pa{f}{i}"))
                        if f == i == 0:
                            dve.wait_ge(x3_in, 16 * (b + 1))
                        wait_self("ffn", b, f"pa{f}{i}")
                        part = x3[:, i, f * HALF:(f + 1) * HALF]
                        v.tensor_tensor(part, part, dt_[i][:], ALU.add).then_inc(*vec.step("ffn", f"pb{f}{i}"))
                dve.wait_ge(*scal.after("ffn", b, f"fq{TT - 1}"))
                v.tensor_scalar(ss[:], ss[:], 1.0 / D, EPS, ALU.mult, ALU.add).then_inc(*vec.step("ffn", "fms"))
                dve.wait_ge(*scal.after("ffn", b, "fsd"))
                v.reciprocal(rs[:], sd[:]).then_inc(*vec.step("ffn", "fr"))
                wait_self("ffn", b, "fr")
                dve.wait_ge(fg_in, 16)
                for i in R(TT):
                    v.scalar_tensor_tensor(out=x3[:, i, :], in0=x3[:, i, :], scalar=rs[:, i:i + 1], in1=fgb[:],
                                           op0=ALU.mult, op1=ALU.mult).then_inc(*vec.step("ffn", f"fx{i}"))

        @block.scalar
        def _(act):
            s = nc.scalar

            def load_vectors():
                for row, src in ((0, b_ada[0]), (6 * KD, c[0]), (7 * KD, norm1_g[0]), (8 * KD, norm2_g[0]),
                                 (9 * KD, conv_b[0]), (9 * KD + KC, conv_ln_g[0]), (9 * KD + 2 * KC, conv_ln_b[0])):
                    n = src.shape[0] // P
                    yield act.dma_start(nat_v[row:row + n, :], src.rearrange("(k p) -> k p", p=P))
                for n, src in enumerate((ssm_a_re[0], ssm_a_im[0])):
                    for half in R(2):
                        yield act.dma_start(nat_a[n * G:(n + 1) * G, half * NST:(half + 1) * NST], src)
                yield act.dma_start(sv[:, 2, :], ssm_log_dt[0].partition_broadcast(P))
                for m in R(KC):
                    yield act.dma_start(nat_w[m * TAPS:(m + 1) * TAPS, :], conv_w[0][:, m * P:(m + 1) * P])

            def load_small():
                for n, (re, im) in enumerate(((ssm_c_re, ssm_c_im), (ssm_c_im, ssm_c_re))):
                    flat = lambda a: a[0].rearrange("g h p -> (g h) p").rearrange("(t q) p -> q t p", q=P)
                    yield act.dma_start(cx[:, n, :, 0:NST], flat(re))
                    yield act.dma_start(cx[:, n, :, NST:], flat(im))
                for half in R(2):
                    rows = slice(half * NST, (half + 1) * NST)
                    for dst, src in ((bx1, (ssm_b_re, ssm_b_im)[half]), (bx2, (ssm_b_im, ssm_b_re)[half])):
                        yield act.dma_start(dst[rows, :, :], src[0].rearrange("g p h -> p g h"))
                with nc.allow_non_contiguous_dma(reason="the skip's diagonal, 512 values"):
                    yield act.dma_start(dvec[:], ssm_d[0].rearrange("(g h) -> h g", h=HG))

            mark["vectors"] = mark["small"] = 0
            for ins in load_vectors():
                ins.then_inc(vectors_in, 16)
                mark["vectors"] += 16

            def load_xs(src, row):
                for i in R(TT):
                    act.dma_start(xs[:, i, :], src[bass.ds(row + i * P, P), :]).then_inc(xs_in, 16)

            def norm_stats(phase, b, n_loads):
                act.wait_ge(xs_in, n_loads)
                for i in R(TT):
                    if i:
                        act.wait_ge(*scal.after(phase, b, f"ns{i - 1}"))
                    s.activation(junk[:], xs[:, i, :], ACT.Square, accum_out=ss[:, i:i + 1])\
                        .then_inc(*scal.step(phase, f"ns{i}"))
                act.wait_ge(*vec.after(phase, b, "nms"))
                s.activation(sd[:], ss[:], ACT.Sqrt).then_inc(*scal.step(phase, "nsd"))

            def h_tile(phase, b, k, slot, which, free):
                act.wait_ge(*tensor.after(phase, b, f"h{k}"))
                if free:
                    act.wait_ge(*free)
                s.activation(tr[slot][:], bank[plan[phase, f"h{k}"]][:], ACT.Identity, scale=scale[which][:, k:k + 1],
                             bias=mod[:, 2 * which * KD + k:2 * which * KD + k + 1]).then_inc(*scal.step(phase, f"h{k}"))

            for ins in load_small():
                ins.then_inc(small_in, 16)
                mark["small"] += 16
            assert mark["small"] == SMALL_LOADS * 16
            act.wait_ge(consts, 9)
            act.wait_ge(pro_v, mark["vt"])
            s.activation(cact[:], c_in, ACT.Silu).then_inc(*scal.step("pro", "cs"))
            act.wait_ge(vectors_in, mark["vectors"])
            s.activation(sv[:, 2, :], sv[:, 2, :], ACT.Exp).then_inc(*scal.step("pro", "dt"))
            load_xs(x_d, 0)
            for n, off in enumerate((2 * D, 5 * D)):
                act.dma_start(bg[:, n, :], b_ada[0][off:off + D].partition_broadcast(P)).then_inc(bg_in, 16)
            act.wait_ge(pro_v, mark["jargs"])
            s.activation(jexp[:], jexp[:], ACT.Exp).then_inc(*scal.step("pro", "ej"))
            s.activation(mag_t[:], sv[:, 4, :], ACT.Exp, scale=float(T)).then_inc(*scal.step("pro", "m8"))
            s.activation(jei[:], jarg[:, 0, :, :], ACT.Sin).then_inc(*scal.step("pro", "sj"))
            s.activation(jer[:], jarg[:, 1, :, :], ACT.Sin, bias=half_pi[:, 0:1]).then_inc(*scal.step("pro", "cj"))
            act.wait_ge(pro_v, mark["kargs"])
            s.activation(sin_t[:], karg[:, 0, :, :], ACT.Sin).then_inc(*scal.step("pro", "sk"))
            s.activation(cos_t[:], karg[:, 1, :, :], ACT.Sin, bias=half_pi[:, 0:1]).then_inc(*scal.step("pro", "ck"))
            norm_stats("pro", 0, 64)
            act.wait_ge(pro_v, mark["scale0"])
            act.wait_ge(*scal.after("pro", 0, "ck"))
            for k in R(KD):
                h_tile("pro", 0, k, k % 4, 0, vec.after("pro", 0, f"hl{k - 4}") if k >= 4 else None)
            for n in R(8):
                act.wait_ge(*tensor.after("pro", 0, f"wt{n}"))
                s.activation(wm[:, 4 * n:4 * n + 4, :, :].rearrange("p g s h -> p (g s h)"), bank[n % 4][:], ACT.Copy)\
                    .then_inc(*scal.step("pro", f"wt{n}"))
            for n in R(8):
                act.wait_ge(*tensor.after("pro", 0, f"kk{n}"))
                s.activation(kst[:, 4 * n:4 * n + 4, T - 1:, :],
                             bank[n % 4][0:HG, :].rearrange("p (g s h) -> p g s h", g=4, s=T), ACT.Copy).then_inc(*scal.step("pro", f"kk{n}"))
            act.wait_ge(*scal.after("pro", 0, "wt7"))
            act.dma_start(wt_d, wm[:].rearrange("p g s h -> p g (s h)")).then_inc(mat_out, 16)
            act.wait_ge(pro_v, mark["vm"])
            act.dma_start(vk_d[:, :, 0, :], vm[:, :, 1:, :].rearrange("p g s h -> p g (s h)")).then_inc(mat_out, 16)
            act.wait_ge(pro_v, mark["kst"])
            act.wait_ge(acc_done, 5)
            for t in R(T):
                act.dma_start(vk_d[t * HG:(t + 1) * HG, :, 1, :],
                              kst[:, :, T - 1 - t:2 * T - 1 - t, :].rearrange("p g s h -> p g (s h)"))\
                    .then_inc(mat_out, 16)

            with act.Fori(0, NB) as b:
                act.wait_ge(mat_out, 16 * (2 + T))
                for m in R(KS):
                    act.wait_ge(*tensor.after("mix", b, f"us{m}"))
                    s.activation(uz[:, m, :, :].rearrange("p s c -> p c s"),
                                 bank[plan["mix", f"us{m}"]][:].rearrange("p (c s) -> p c s", s=T), ACT.Copy)\
                        .then_inc(*scal.step("mix", f"us{m}"))
                    act.wait_ge(*scal.after("mix", b, f"us{m}"))
                    act.dma_start(us_d[m * P:(m + 1) * P], uz[:, m, :, :]).then_inc(uz_out, 16)
                act.wait_ge(uz_out, 64 * (b + 1))
                for t in R(T):
                    act.dma_start(u8[t * HG:(t + 1) * HG, :, :], us_d[:, t, :].rearrange("(g h) c -> h g c", h=HG))\
                        .then_inc(u8_in, 16)
                for m in R(KC):
                    act.wait_ge(*tensor.after("mix", b, f"ug{m}"))
                    s.activation(tr[m][:], bank[plan["mix", f"ug{m}"]][:], ACT.Sigmoid)\
                        .then_inc(*scal.step("mix", f"ug{m}"))
                for q in R(NQ):
                    act.wait_ge(*tensor.after("mix", b, f"S{q}"))
                    s.activation(wst[:, q * GQ:(q + 1) * GQ, 1:], bank[plan["mix", f"S{q}"]][:]
                                 .rearrange("p (g k) -> p g k", g=GQ), ACT.Copy).then_inc(*scal.step("mix", f"S{q}"))

                def gate(i):
                    act.wait_ge(*tensor.after("mix", b, f"gl{i}"))
                    dst = (sg_c if i < KD else sg_s)[:, i % KD, :]
                    s.activation(dst, bank[plan["mix", f"gl{i}"]][:], ACT.Sigmoid).then_inc(*scal.step("mix", f"gl{i}"))

                for i in R(GL[3]):
                    gate(i)
                for q in R(NQ):
                    act.wait_ge(*tensor.after("mix", b, f"Y{q}"))
                    s.activation(u8[:, q * GQ:(q + 1) * GQ, :], bank[plan["mix", f"Y{q}"]][:]
                                 .rearrange("p (g k) -> p g k", g=GQ), ACT.Copy).then_inc(*scal.step("mix", f"Y{q}"))
                    if q == NQ - 1:
                        act.wait_ge(*scal.after("mix", b, f"Y{q}"))
                        for t in R(T):
                            act.dma_start(ys_d[:, t, :].rearrange("(g h) c -> h g c", h=HG),
                                          u8[t * HG:(t + 1) * HG, :, :]).then_inc(y_out, 16)
                    gate(GL[3] + q)
                act.wait_ge(y_out, 16 * T * (b + 1))
                act.dma_start(yz[:], ys_d.rearrange("(m p) s c -> p m s c", p=P)).then_inc(yz_in, 16)
                load_xs(x_d, (b + 1) % NB * TB)
                for i in R(TT):
                    act.wait_ge(x2_out[i], 1 + 16 * 2 * b)
                    act.dma_start(xr[i][:], x_d[bass.ds(b * TB + i * P, P), 0:HALF]).then_inc(xr_in[i], 16)
                for i in R(GL[3] + NQ, 2 * KD - 2):
                    gate(i)
                act.wait_ge(yz_in, 16 * (b + 1))
                for m in R(KS):
                    s.activation(tr[m][:].rearrange("p (c s) -> p c s", s=T),
                                 yz[:, m, :, :].rearrange("p s c -> p c s"), ACT.Gelu_apprx_tanh)\
                        .then_inc(*scal.step("mix", f"ge{m}"))
                gate(2 * KD - 2)
                gate(2 * KD - 1)

                def gate_b(p):
                    for m in pair(p):
                        act.wait_ge(*tensor.after("mix", b, f"zb{m}"))
                        act.wait_ge(*vec.after("mix", b, f"ms{m - 2}" if p else f"ysl{m}"))
                        s.activation(tr[m % 2][:], bank[plan["mix", f"zb{m}"]][:], ACT.Sigmoid)\
                            .then_inc(*scal.step("mix", f"zb{m}"))

                gate_b(0)
                for m in R(KC):
                    act.wait_ge(*vec.after("mix", b, f"cen{m}"))
                    s.activation(sq[:, m, :], yc[:, m, :], ACT.Square).then_inc(*scal.step("mix", f"sq{m}"))
                gate_b(1)
                act.wait_ge(*tensor.after("mix", b, "ln2"))
                s.activation(dt_[2][:], bank[plan["mix", "ln2"]][:], ACT.Sqrt, bias=eps1[:, 0:1])\
                    .then_inc(*scal.step("mix", "lsd"))
                norm_stats("mix", b, 64 * (b + 2))
                for m in R(KC):
                    act.wait_ge(*vec.after("mix", b, f"nm{m}"))
                    act.wait_ge(*vec.after("mix", b, f"ysl{2 + m}" if m < 2 else f"ynl{m - 2}"))
                    s.activation(tr[2 + m % 2][:], yc[:, m, :], ACT.Silu, scale=cvec[:, 1, m:m + 1],
                                 bias=cvec[:, 2, m:m + 1]).then_inc(*scal.step("mix", f"si{m}"))
                    if m == 1:
                        gate_b(2)
                gate_b(3)
                for k in R(KD):
                    h_tile("mix", b, k, k % 4, 0,
                           vec.after("mix", b, f"hl{k - 4}" if k >= 4 else f"ms{6 + k}" if k < 2 else f"ynl{k}"))
                for f in R(2):
                    for i in R(TT):
                        act.wait_ge(*vec.after("mix", b, f"ob{f}{i}"))
                        act.dma_start(x2_d[bass.ds(b * TB + i * P, P), f * HALF:(f + 1) * HALF], xr[i][:])\
                            .then_inc(x2_out[i], 16)
                    if f == 0:
                        for i in R(TT):
                            act.wait_ge(x2_out[i], 1 + 16 * (2 * b + 1))
                            act.dma_start(xr[i][:], x_d[bass.ds(b * TB + i * P, P), HALF:]).then_inc(xr_in[i], 16)

            act.wait_ge(*tensor.after("mix", NB - 1, f"h{KD - 1}"))
            for i in R(TT):
                act.wait_ge(x2_out[i], 1 + 16 * 2)
            load_xs(x2_d, 0)
            norm_stats("mid", 0, 64 * (NB + 2))
            for k in R(KD):
                h_tile("mid", 0, k, k % 4, 1, vec.after("mid", 0, f"hl{k - 4}") if k >= 4 else
                       vec.after("mix", NB - 1, f"hl{KD - 1}"))
            for i in R(TT):
                act.wait_ge(x2_out[i], 1 + 16 * 2 * NB)
            act.dma_start(fgb[:], final_g.partition_broadcast(P)).then_inc(fg_in, 16)

            with act.Fori(0, NB) as b:
                act.wait_ge(final_out, 1 + 64 * b)
                act.dma_start(x3[:], x2_d[bass.ds(b * TB, TB), :].rearrange("(i p) d -> p i d", p=P))\
                    .then_inc(x3_in, 16)
                load_xs(x2_d, ((b + 1) % NB) * TB)
                with act.Fori(0, FI) as it:
                    for j in R(2):
                        act.wait_ge(*tensor.after("ffn", b, f"fg{j}", it))
                        act.wait_ge(*vec.before("ffn", b, f"fm{j}", it))
                        s.activation(tr[j][:], bank[plan["ffn", f"fg{j}"]][:], ACT.Silu)\
                            .then_inc(*scal.step("ffn", f"fs{j}"))
                norm_stats("ffn", b, 64 * (b + NB + 3))
                for k in R(KD):
                    h_tile("ffn", b, k, k % 4, 1, vec.after("ffn", b, f"hl{k - 4}") if k >= 4 else
                           vec.after("ffn", b, "fm1", FI - 1))
                for i in R(TT):
                    act.wait_ge(*vec.after("ffn", b, f"pb1{i}"))
                    act.wait_ge(*scal.after("ffn", b, f"fq{i - 1}" if i else "nsd"))
                    s.activation(junk[:], x3[:, i, :], ACT.Square, accum_out=ss[:, i:i + 1])\
                        .then_inc(*scal.step("ffn", f"fq{i}"))
                act.wait_ge(*vec.after("ffn", b, "fms"))
                s.activation(sd[:], ss[:], ACT.Sqrt).then_inc(*scal.step("ffn", "fsd"))
                for i in R(TT):
                    act.wait_ge(*vec.after("ffn", b, f"fx{i}"))
                    act.dma_start(out_d[bass.ds(b * TB + i * P, P), :], x3[:, i, :]).then_inc(final_out, 16)
            act.wait_ge(final_out, 1 + 64 * NB)

        @block.tensor
        def _(pe):
            t = nc.tensor
            pe.wait_ge(consts, 9)
            pe.wait_ge(vectors_in, mark["vectors"])
            for n, src in enumerate((nat_a, nat_v, nat_w)):
                rows = src.shape[0]
                t.transpose(bank[n][:, 0:rows], src[:], ident[0:rows, 0:rows]).then_inc(*tensor.step("pro", f"v{n}"))

            def modulation(lo, hi):
                for n in R(lo, hi):
                    who, kind, half, rows = SLABS[n]
                    if who != "pe":
                        continue
                    pe.wait_ge(ada_in[n % ADA], 16 * (n // ADA + 1))
                    for j in R(KD // 2):
                        k = rows * KD // 2 + j
                        if kind == 2:
                            ins = t.matmul(bank[(4, 7)[half]][:], cbc[:, k, :], ada[n % ADA][:, j, :],
                                           start=(k == 0), stop=(k == KD - 1))
                        else:
                            r = 2 * (kind % 3) + half
                            ins = t.matmul(bank[5][0:4, :], zc[:, k, 3 - r:7 - r], ada[n % ADA][:, j, :],
                                           start=(r == 0 and k == 0), stop=(r == 3 and k == KD - 1))
                    ins.then_inc(*tensor.step("pro", f"ada{n}"))

            def transposes(phase, b, k, free=True):
                if free:
                    pe.wait_ge(*bank_free(phase, b, f"h{k}"))
                if k == 0:
                    pe.wait_ge(*vec.after(phase, b, f"nx{TT - 1}"))
                for i in R(TT):
                    ins = t.transpose(bank[plan[phase, f"h{k}"]][:, i * P:(i + 1) * P], xs[:, i, k * P:(k + 1) * P],
                                      ident[:])
                ins.then_inc(*tensor.step(phase, f"h{k}"))

            pe.wait_ge(pro_v, mark["zc"])
            modulation(0, first_gate)

            def modulation_by_feature(which):
                pe.wait_ge(pro_v, mark[f"modrow{which}"])
                for j in R(4):
                    ins = t.transpose(bank[6][:, 4 * j:4 * j + 4], modrow[:, j * P:(j + 1) * P], ident[0:4, 0:4])
                ins.then_inc(*tensor.step("pro", ("mt", "mt2")[which]))

            modulation_by_feature(0)
            pe.wait_ge(small_in, mark["small"])
            for n in R(2):
                for j in R(4):
                    ins = t.transpose(bank[3 + n][:, j * P:(j + 1) * P], cx[:, n, j, :], ident[:])
                ins.then_inc(*tensor.step("pro", f"ct{n}"))
            pe.wait_ge(pro_v, mark["cc"])
            for k in R(KD):
                if k >= 4:
                    pe.wait_ge(*scal.after("pro", 0, f"h{k - 4}"))
                transposes("pro", 0, k, free=False)
            pe.wait_ge(pro_v, mark["cbc"])
            modulation(first_gate, last_slab(3) + 1)
            pe.wait_ge(pro_v, mark["wm"])
            for n in R(8):
                pe.wait_ge(*scal.after("pro", 0, f"wt{n - 4}" if n >= 4 else f"h{4 + n}"))
                for j in R(4):
                    ins = t.transpose(bank[n % 4][:, j * P:(j + 1) * P],
                                      wm[:, 4 * n + j, :, :].rearrange("p s h -> p (s h)"), ident[:])
                ins.then_inc(*tensor.step("pro", f"wt{n}"))
            modulation(last_slab(3) + 1, len(SLABS))
            modulation_by_feature(1)
            pe.wait_ge(acc_done, 4)
            pe.wait_ge(pro_v, mark["scale1"])
            for h in R(2):
                t.matmul(bank[6 + h][:], ones[:], acc[:, h, :], start=True, stop=True)\
                    .then_inc(*tensor.step("pro", f"sg{h}"))
            pe.wait_ge(pro_v, mark["vm"])
            for n in R(8):
                pe.wait_ge(*scal.after("pro", 0, f"kk{n - 4}" if n >= 4 else f"wt{4 + n}"))
                for j in R(4):
                    g = 4 * n + j
                    ins = t.matmul(bank[n % 4][0:HG, j * P:(j + 1) * P], b1[:, g, :],
                                   vm[:, g, 0:T, :].rearrange("p s h -> p (s h)"), start=True, stop=True)
                ins.then_inc(*tensor.step("pro", f"kk{n}"))
            pe.wait_ge(*scal.after("pro", 0, "kk7"))
            pe.wait_ge(*vec.after("pro", 0, f"hl{KD - 1}"))

            def three(dst, wh, wl, xh, xl, first, last):
                t.matmul(dst, wh, xh, start=first, stop=False)
                t.matmul(dst, wh, xl, start=False, stop=False)
                return t.matmul(dst, wl, xh, start=False, stop=last)

            with pe.Fori(0, NB) as b:
                chunk = [0]

                def next_chunk():
                    chunk[0] += 1
                    pe.wait_ge(split_done, RAW + b * NMIX + chunk[0])
                    return (chunk[0] - 1) % SPL

                def layer(name, ws, first_col, width, kt, xh, xl):
                    pe.wait_ge(*bank_free("mix", b, name))
                    hi = w_hi[ws][:].rearrange("p (k n) -> p k n", n=width)
                    lo = w_lo[ws][:].rearrange("p (k n) -> p k n", n=width)
                    for k in R(kt):
                        ins = three(bank[plan["mix", name]][:], hi[:, k, first_col:first_col + P],
                                    lo[:, k, first_col:first_col + P], xh[:, k, :], xl[:, k, :], k == 0, k == kt - 1)
                    ins.then_inc(*tensor.step("mix", name))

                def gates(*tiles):
                    for i in tiles:
                        layer(f"gl{i}", next_chunk(), 0, P, KD, h_hi, h_lo)

                ssm_use = [0]

                def next_ssm():
                    n = ssm_use[0]
                    ssm_use[0] += 1
                    pe.wait_ge(ssm_in[n % 3], 16 * (4 * b + n // 3 + 1))
                    return ssm_m[n % 3]

                for m in R(KS):
                    layer(f"us{m}", next_chunk(), 0, P, KD, h_hi, h_lo)
                for m in R(KC):
                    layer(f"ua{m}", next_chunk(), 0, P, KD, h_hi, h_lo)
                    layer(f"ug{m}", next_chunk(), 0, P, KD, h_hi, h_lo)
                pe.wait_ge(pro_v, mark["g2b"])
                pe.wait_ge(u8_in, 16 * T * (b + 1))
                for q in R(NQ):
                    mat = next_ssm()[:].rearrange("p (g n) -> p g n", g=GQ)
                    pe.wait_ge(*bank_free("mix", b, f"S{q}"))
                    for j in R(GQ):
                        ins = t.matmul(bank[plan["mix", f"S{q}"]][:, j * NC:(j + 1) * NC], mat[:, j, :],
                                       u8[:, q * GQ + j, :], start=True, stop=True)
                    ins.then_inc(*tensor.step("mix", f"S{q}"))
                gates(*R(0, GL[1]))

                def turned(name, q, lo):
                    pe.wait_ge(*bank_free("mix", b, name))
                    t.matmul(bank[plan["mix", name]][:], turn[:], wst[:, q * GQ:(q + 1) * GQ, lo:lo + NC],
                             start=True, stop=True).then_inc(*tensor.step("mix", name))

                for q in R(NQ):
                    pe.wait_ge(*scal.after("mix", b, f"S{q}"))
                    turned(f"R{q}", q, 1)
                gates(*R(GL[1], GL[2]))
                pe.wait_ge(*vec.after("mix", b, f"sc{G - 1}"))
                for q in R(NQ):
                    turned(f"D{q}", q, 0)
                pe.wait_ge(*bank_free("mix", b, "dc"))
                t.matmul(bank[plan["mix", "dc"]][:, 0:G], turn[:], wst[:, :, NC], start=True, stop=True)\
                    .then_inc(*tensor.step("mix", "dc"))
                gates(*R(GL[2], GL[3]))
                for q in R(NQ):
                    pe.wait_ge(*vec.after("mix", b, f"Ds{q}"))
                    pe.wait_ge(*bank_free("mix", b, f"Y{q}"))
                    for half in R(2):
                        mat = next_ssm()[:].rearrange("p (g a n) -> p g a n", g=GQ // 2, a=2)
                        for j in R(GQ // 2):
                            g = q * GQ + half * (GQ // 2) + j
                            dst = bank[plan["mix", f"Y{q}"]][:, (g % GQ) * NC:(g % GQ + 1) * NC]
                            t.matmul(dst, mat[:, j, 0, :], wst[:, g, 0:NC], start=True, stop=False)
                            ins = t.matmul(dst, mat[:, j, 1, :], u8[:, g, :], start=False, stop=True)
                    ins.then_inc(*tensor.step("mix", f"Y{q}"))
                    gates(GL[3] + q)
                gates(*R(GL[3] + NQ, 2 * KD))

                def two_tiles(name, p, xh, xl):
                    slot = next_chunk()
                    for j in R(2):
                        layer(f"{name}{2 * p + j}", slot, j * P, 2 * P, KC, xh, xl)

                def mean(name, src):
                    pe.wait_ge(*bank_free("mix", b, name))
                    for m in R(KC):
                        ins = t.matmul(bank[plan["mix", name]][:], mean_w[:], src[:, m, :], start=(m == 0),
                                       stop=(m == KC - 1))
                    ins.then_inc(*tensor.step("mix", name))

                pe.wait_ge(*vec.after("mix", b, f"ysl{KS - 1}"))
                for p in R(KD // 2):
                    two_tiles("za", p, ys_hi, ys_lo)
                    two_tiles("zb", p, ys_hi, ys_lo)
                    if p == 0:
                        pe.wait_ge(*vec.after("mix", b, f"c{TAPS - 1}_{KC - 1}"))
                        mean("ln1", yc)
                    if p == 1:
                        pe.wait_ge(*scal.after("mix", b, f"sq{KC - 1}"))
                        mean("ln2", sq)
                for p in R(KD // 2):
                    for k in pair(p):
                        transposes("mix", b, k)
                    if p == 0:
                        pe.wait_ge(*vec.after("mix", b, f"ynl{KC - 1}"))
                    two_tiles("cp", p, yn_hi, yn_lo)

                def out_half(phase, b, f, kt, xh, xl, pre, step, between=None):
                    for j in R(kt // 2):
                        slot = next_chunk()
                        for kk in R(2):
                            k = 2 * j + kk
                            for i in R(TT):
                                if k == 0:
                                    pe.wait_ge(*bank_free(phase, b, f"{pre}{f}{i}"))
                                dst = bank[plan[phase, f"{pre}{f}{i}"]][:]
                                cols = slice(i * P, (i + 1) * P)
                                wcols = slice(kk * HALF, (kk + 1) * HALF)
                                t.matmul(dst, xh[:, k, cols], w_hi[slot][:, wcols], start=(k == 0), stop=False)
                                t.matmul(dst, xl[:, k, cols], w_hi[slot][:, wcols], start=False, stop=False)
                                ins = t.matmul(dst, xh[:, k, cols], w_lo[slot][:, wcols], start=False,
                                               stop=(k == kt - 1))
                                if k == kt - 1:
                                    ins.then_inc(*tensor.step(phase, f"{pre}{f}{i}"))
                        if j < kt // 2 - 1:
                            ins.then_inc(*tensor.step(phase, step(f, j)))
                        if between:
                            between(f, j)

                pe.wait_ge(*vec.after("mix", b, f"ml{KD - 1}"))
                for f in R(2):
                    out_half("mix", b, f, KD, m_hi, m_lo, "o", lambda f, j: f"oc{f}{j}")
                pe.wait_ge(*vec.after("mix", b, f"hl{KD - 1}"))
                assert chunk[0] == NMIX

            for k in R(KD):
                if k < 4:
                    pe.wait_ge(*vec.after("mix", NB - 1, f"oa0{k}"))
                    transposes("mid", 0, k, free=False)
                else:
                    transposes("mid", 0, k)
            pe.wait_ge(*vec.after("mid", 0, f"hl{KD - 1}"))

            with pe.Fori(0, NB) as b:
                with pe.Fori(0, FI) as it:
                    for n, name in enumerate(pe_loop):
                        pe.wait_ge(split_done, RAW + NB * NMIX + b * NFFN + it * 4 + n + 1)
                        pe.wait_ge(*bank_free("ffn", b, name, it))
                        ws = n % SPL
                        for k in R(KD):
                            cols = slice(k * P, (k + 1) * P)
                            ins = three(bank[plan["ffn", name]][:], w_hi[ws][:, cols], w_lo[ws][:, cols],
                                        h_hi[:, k, :], h_lo[:, k, :], k == 0, k == KD - 1)
                        ins.then_inc(*tensor.step("ffn", name))
                chunk = [2 * KF]

                def next_chunk():
                    chunk[0] += 1
                    pe.wait_ge(split_done, RAW + NB * NMIX + b * NFFN + chunk[0])
                    return (chunk[0] - 1) % SPL

                def next_h(f, j):
                    if f == 0 and 1 <= j <= KD:
                        transposes("ffn", b, j - 1)

                pe.wait_ge(*vec.after("ffn", b, "fl1", FI - 1))
                for f in R(2):
                    for j in R(KF // 2):
                        slot = next_chunk()
                        for kk in R(2):
                            k = 2 * j + kk
                            for i in R(TT):
                                if k == 0:
                                    pe.wait_ge(*bank_free("ffn", b, f"p{f}{i}"))
                                dst = bank[plan["ffn", f"p{f}{i}"]][:]
                                cols = slice(i * P, (i + 1) * P)
                                wcols = slice(kk * HALF, (kk + 1) * HALF)
                                t.matmul(dst, hid_hi[:, k, cols], w_hi[slot][:, wcols], start=(k == 0), stop=False)
                                t.matmul(dst, hid_lo[:, k, cols], w_hi[slot][:, wcols], start=False, stop=False)
                                ins = t.matmul(dst, hid_hi[:, k, cols], w_lo[slot][:, wcols], start=False,
                                               stop=(k == KF - 1))
                                if k == KF - 1:
                                    ins.then_inc(*tensor.step("ffn", f"p{f}{i}"))
                        if j < KF // 2 - 1:
                            ins.then_inc(*tensor.step("ffn", f"fc{f}_{j}"))
                        next_h(f, j)
                pe.wait_ge(*vec.after("ffn", b, f"hl{KD - 1}"))
                assert chunk[0] == NFFN

        @block.gpsimd
        def _(pool):
            g = nc.gpsimd
            g.memset(ident[:], 0.0).then_inc(consts, 1)
            g.memset(turn[:], 0.0).then_inc(consts, 1)
            pool.wait_ge(consts, 2)
            g.affine_select(out=ident[:], in_=ident[:], compare_op=ALU.not_equal, fill=1.0, base=0,
                            pattern=[[-1, P]], channel_multiplier=1).then_inc(consts, 1)
            g.affine_select(out=turn[:], in_=turn[:], compare_op=ALU.not_equal, fill=1.0, base=-NST,
                            pattern=[[-1, P]], channel_multiplier=1).then_inc(consts, 1)
            pool.wait_ge(consts, 4)
            g.affine_select(out=turn[:], in_=turn[:], compare_op=ALU.not_equal, fill=-1.0, base=NST,
                            pattern=[[-1, P]], channel_multiplier=1).then_inc(consts, 1)
            g.iota(iota_i[:], pattern=[[1, NC + 1]], base=0, channel_multiplier=0).then_inc(consts, 1)
            g.memset(sign[:], 1.0).then_inc(split_done, 1)
            g.memset(nsign[:], -1.0).then_inc(split_done, 1)
            g.memset(zero1[:], 0.0).then_inc(split_done, 1)
            g.memset(eps1[:], EPS).then_inc(x2_out[0], 1)
            g.memset(half_pi[:], float(np.pi / 2)).then_inc(x2_out[1], 1)
            g.memset(mean_w[:], 1.0 / CW).then_inc(x2_out[2], 1)
            g.memset(carry[:], 0.0).then_inc(x2_out[3], 1)
            g.memset(ones[:], 1.0).then_inc(final_out, 1)
            g.memset(zc[:], 0.0)
            g.memset(uc[:, :, 0:HALO], 0.0).then_inc(consts, 1)
            pool.wait_ge(consts, 7)
            g.memset(sign[0:NST, :], -1.0)
            g.memset(nsign[0:NST, :], 1.0).then_inc(consts, 1)
            g.tensor_copy(iota_f[:], iota_i[:]).then_inc(consts, 1)

            pool.wait_ge(*scal.after("pro", 0, "cs"))
            pool.wait_ge(consts, 9)
            mine = [n for n in R(len(SLABS)) if SLABS[n][0] == "pool"]
            ops = 0

            def add(out, a, b_):
                pool.wait_ge(acc_link, ops)
                return g.tensor_tensor(out, a, b_, ALU.add)

            for i, n in enumerate(mine):
                _, kind, half, rows = SLABS[n]
                slab, a = ada[n % ADA], acc[:, half, :]
                pool.wait_ge(ada_in[n % ADA], 16 * (n // ADA + 1))
                g.tensor_tensor(slab[:], slab[:], cact[:, rows * KD // 2:(rows + 1) * KD // 2].unsqueeze(2)
                                .broadcast_to([P, KD // 2, HALF]), ALU.mult).then_inc(acc_link, 1)
                ops += 1
                for j in R(1 if rows == 0 else 0, KD // 2):
                    ins = add(a, slab[:, j - 1, :] if j == 1 and rows == 0 else a, slab[:, j, :])
                    if j < KD // 2 - 1:
                        ins.then_inc(acc_link, 1)
                        ops += 1
                ins.then_inc(acc_done, 1)
                pool.wait_ge(acc_done, i + 1)
            pool.wait_ge(*tensor.after("pro", 0, f"h{KD - 1}"))
            g.memset(kst[:, :, 0:T - 1, :], 0.0).then_inc(acc_done, 1)

            zeros = zero1[:, 0:1].broadcast_to([P, CH])

            with pool.Fori(0, NB) as b:
                for n in R(NMIX):
                    first = b * NMIX
                    pool.wait_ge(raw_in[n % RAW], 16 * (b * (NMIX // RAW) + n // RAW + 1))
                    if n >= SPL:
                        pool.wait_ge(*chunk_used("mix", b, n - SPL + 1))
                    else:
                        s_, v_ = tensor.before("mix", b, chunk_no["mix", NMIX - SPL + n + 1], None)
                        pool.wait_ge(s_, v_)
                    src, hi, lo = raw[n % RAW], w_hi[n % SPL], w_lo[n % SPL]
                    g.tensor_tensor(hi[:], src[:], zeros, ALU.add).then_inc(hi_done, 1)
                    pool.wait_ge(hi_done, first + n + 1)
                    g.tensor_tensor(lo[:], src[:], hi[:].bitcast(F32), ALU.subtract).then_inc(split_done, 1)
            with pool.Fori(0, NB) as b:
                for n in R(NFFN):
                    first = NB * NMIX + b * NFFN
                    pool.wait_ge(raw_in[n % RAW], 16 * (NB * NMIX // RAW + b * (NFFN // RAW) + n // RAW + 1))
                    m = n - SPL + 1
                    if m <= 0:
                        s_, v_ = tensor.before("ffn", b, chunk_no["ffn", NFFN + m], None)
                    elif m <= 2 * KF:
                        s_, v_ = tensor.after("ffn", b, pe_loop[(m - 1) % 4], (m - 1) // 4)
                    else:
                        s_, v_ = chunk_used("ffn", b, m)
                    pool.wait_ge(s_, v_)
                    src, hi, lo = raw[n % RAW], w_hi[n % SPL], w_lo[n % SPL]
                    g.tensor_tensor(hi[:], src[:], zeros, ALU.add).then_inc(hi_done, 1)
                    pool.wait_ge(hi_done, first + n + 1)
                    g.tensor_tensor(lo[:], src[:], hi[:].bitcast(F32), ALU.subtract).then_inc(split_done, 1)

        @block.sync
        def _(sp):
            of_pool_so_far = 0
            for n, (who, kind, half, rows) in enumerate(SLABS):
                if n >= ADA and SLABS[n - ADA][0] == "pe":
                    sp.wait_ge(*tensor.after("pro", 0, f"ada{n - ADA}"))
                elif n >= ADA:
                    of_pool_so_far += 1
                    sp.wait_ge(acc_done, of_pool_so_far)
                col = kind * D + half * HALF
                sp.dma_start(ada[n % ADA][:], ada_d[:, rows * KD // 2:(rows + 1) * KD // 2, col:col + HALF])\
                    .then_inc(ada_in[n % ADA], 16)
            sp.wait_ge(*tensor.after("pro", 0, "sg1"))

            def load(n, key, number):
                dst = raw[n % RAW]
                sp.wait_ge(split_done, number + 1)
                if key[0] == "in":
                    d, src = dst[:].rearrange("p (k n) -> p k n", n=P), win_d[:, :, key[1]:key[1] + P]
                elif key[0] in ("proj", "glu"):
                    d = dst[:].rearrange("p (k n) -> p k n", n=2 * P)
                    src = (proj_d if key[0] == "proj" else glu_d)[:, :, key[1]:key[1] + 2 * P]
                elif key[0] == "out":
                    d = dst[:].rearrange("p (k n) -> p k n", n=HALF)
                    src = wout_d[:, 2 * key[2]:2 * key[2] + 2, key[1] * HALF:(key[1] + 1) * HALF]
                elif key[0] == "fin":
                    d, src = dst[:].rearrange("p (k n) -> p k n", n=P), fin_d[:, :, key[1]:key[1] + P]
                else:
                    d = dst[:].rearrange("p (k n) -> p k n", n=HALF)
                    src = fout_d[:, 2 * key[2]:2 * key[2] + 2, key[1] * HALF:(key[1] + 1) * HALF]
                sp.dma_start(d, src).then_inc(raw_in[n % RAW], 16)

            with sp.Fori(0, NB) as b:
                ssm_user = [f"S{q}" for q in R(NQ)] + [f"Y{q}" for q in R(NQ) for _ in R(2)]

                def load_ssm(n):
                    if n >= 3:
                        sp.wait_ge(*tensor.after("mix", b, ssm_user[n - 3]))
                    else:
                        sp.wait_ge(*tensor.start("mix", b))
                    if n < NQ:
                        src = wt_d[:, n * GQ:(n + 1) * GQ, :].rearrange("p g n -> p (g n)")
                    else:
                        m = n - NQ
                        src = vk_d[:, m * GQ // 2:(m + 1) * GQ // 2, :, :].rearrange("p g a n -> p (g a n)")
                    sp.dma_start(ssm_m[n % 3][:], src).then_inc(ssm_in[n % 3], 16)

                ahead = {8: [0, 1, 2], 13: [3, 4, 5], 20: [6, 7], 21: [8, 9], 22: [10, 11]}
                for n, key in enumerate(MIX_CHUNKS):
                    if n == min(ahead):
                        sp.wait_ge(mat_out, 16 * (2 + T))
                    for m in ahead.get(n, []):
                        load_ssm(m)
                    load(n, key, b * NMIX + n)
            with sp.Fori(0, NB) as b:
                base = NB * NMIX + b * NFFN
                for n in R(2 * KF):
                    m, up = n // 2, n % 2
                    load(n, ("fin", up * FF + m * P), base + n)
                for n in R(2 * KF, NFFN):
                    f, j = divmod(n - 2 * KF, KF // 2)
                    load(n, ("fout", f, j), base + n)

        for s_ in (tensor, scal, vec):
            s_.finished()


INPUTS = ["x", "c", "w_ada", "b_ada", "norm1_g", "w_in", "conv_w", "conv_b", "conv_ln_g", "conv_ln_b",
          "conv_proj", "ssm_a_re", "ssm_a_im", "ssm_b_re", "ssm_b_im", "ssm_c_re", "ssm_c_im",
          "ssm_d", "ssm_log_dt", "ssm_glu", "w_out", "norm2_g", "w_ffn_in", "w_ffn_out", "final_g"]


def kernel(**inputs):
    import concourse.bacc as bacc
    from concourse.bass_utils import run_bass_kernel_spmd

    nc = bacc.Bacc("TRN2", target_bir_lowering=False, num_devices=1, dynamic_dma_scratch_size=1024)
    arrays, args = {}, []
    for name in INPUTS:
        a = np.ascontiguousarray(inputs[name])
        arrays[f"in_{name}"] = a
        args.append(nc.dram_tensor(f"in_{name}", a.shape, mybir.dt.from_np(a.dtype), kind="ExternalInput").ap())
    shape = inputs["x"].shape
    args.append(nc.dram_tensor("out_0", shape, F32, kind="ExternalOutput").ap())
    build(nc, *args)
    result = run_bass_kernel_spmd(nc, [arrays], core_ids=[0])
    return result.results[0]["out_0"]
```

```python
from contextlib import ExitStack

import numpy as np

import concourse.bass as bass
from concourse import mybir

ALU = mybir.AluOpType
ACT = mybir.ActivationFunctionType
F32 = mybir.dt.float32
F32R = mybir.dt.float32r
BF16 = mybir.dt.bfloat16
I32 = mybir.dt.int32

P = 128
EPS = 1e-6


class Steps:

    def __init__(self, sem, phases):
        self.sem, self.at, self.base, self.per, self.names = sem, {}, {}, {}, {}
        total = 0
        for phase, times, segments in phases:
            n = 0
            names = []
            for seg, rep in segments:
                for j, name in enumerate(seg):
                    assert (phase, name) not in self.at, name
                    self.at[phase, name] = (n + j + 1, len(seg))
                names += seg
                n += len(seg) * rep
            self.base[phase], self.per[phase], self.names[phase] = total, n, names
            total += n * times
        self.next = {phase: 0 for phase, _, _ in phases}

    def step(self, phase, name):
        want = self.names[phase][self.next[phase]]
        assert want == name, f"{phase}: {name} where {want} stands"
        self.next[phase] += 1
        return self.sem, 1

    def again(self, phase):
        self.finished()
        self.next[phase] = 0

    def after(self, phase, b, name, it=0):
        at, width = self.at[phase, name]
        return self.sem, self.base[phase] + at + b * self.per[phase] + it * width

    def before(self, phase, b, name, it=0):
        at, width = self.at[phase, name]
        round_ = self.per[phase] if it is None else width
        v = self.base[phase] + at - round_
        assert v >= 0, (phase, name, v)
        return self.sem, v + b * self.per[phase] + (0 if it is None else it * width)

    def start(self, phase, b):
        return self.sem, self.base[phase] + b * self.per[phase]

    def finished(self):
        for phase, n in self.next.items():
            assert n in (0, len(self.names[phase])), (phase, self.names[phase][n])


def build(nc, x, c, w_ada, b_ada, norm1_g, w_in, conv_w, conv_b, conv_ln_g, conv_ln_b, conv_proj,
          ssm_a_re, ssm_a_im, ssm_b_re, ssm_b_im, ssm_c_re, ssm_c_im, ssm_d, ssm_log_dt, ssm_glu,
          w_out, norm2_g, w_ffn_in, w_ffn_out, final_g, out):
    SEQ, D = x.shape[1], x.shape[2]
    TAPS, CW = conv_w.shape[1], conv_w.shape[2]
    G, NST, HG = ssm_b_re.shape[1:]
    FF = w_ffn_out.shape[1]
    SW = G * HG
    TB = 512
    NB = SEQ // TB
    TT = TB // P
    KD = D // P
    KC = CW // P
    KS = SW // P
    KF = FF // P
    T = P // HG
    NC = TB // T
    GQ = 512 // NC
    NQ = G // GQ
    GT = P // HG
    HALO = TAPS - 1
    CH = 1024
    HALF = D // 2
    ADA = 3
    SLABS = [("pe", k, h, r) for k in range(5) for h in range(2) for r in range(2)]
    for n, at in enumerate((2, 7, 12, 17)):
        SLABS.insert(at, ("pool", 5, n // 2, n % 2))
    last_slab = lambda kind: SLABS.index(("pe", kind, 1, 1))
    first_gate = last_slab(1) + 1
    RAW, SPL = 3, 2
    assert 2 * NST == P and KC == 4 and KS == 4 and KD == 8 and NQ == 4 and x.shape[0] == 1
    assert KF % 2 == 0 and GT == T

    o_ssm, o_gl = 2 * CW, 2 * CW + SW
    MIX_CHUNKS = [("in", o_ssm + m * P) for m in range(KS)]
    for m in range(KC):
        MIX_CHUNKS += [("in", m * P), ("in", CW + m * P)]
    MIX_CHUNKS += [("in", o_gl + i * P) for i in range(2 * KD)]
    for p in range(KD // 2):
        MIX_CHUNKS += [("glu", 2 * p * P), ("glu", D + 2 * p * P)]
    MIX_CHUNKS += [("proj", 2 * p * P) for p in range(KD // 2)]
    MIX_CHUNKS += [("out", h, j) for h in range(2) for j in range(KD // 2)]
    NMIX = len(MIX_CHUNKS)
    FI = KF // 2
    NFFN = 2 * KF + 2 * (KF // 2)
    assert NMIX % (RAW * SPL) == 0 and NFFN % (RAW * SPL) == 0

    x2_d = nc.dram_tensor("x2_scratch", (SEQ, D), F32).ap()
    us_d = nc.dram_tensor("us_scratch", (SW, T, NC), F32).ap()
    ys_d = nc.dram_tensor("ys_scratch", (SW, T, NC), F32).ap()
    wt_d = nc.dram_tensor("wt_scratch", (P, G, P), F32).ap()
    vk_d = nc.dram_tensor("vk_scratch", (P, G, 2, P), F32).ap()

    x_d, out_d = x[0], out[0]
    win_d = w_in[0].rearrange("(k p) n -> p k n", p=P)
    proj_d = conv_proj[0].rearrange("(k p) n -> p k n", p=P)
    glu_d = ssm_glu[0].rearrange("(k p) n -> p k n", p=P)
    wout_d = w_out[0].rearrange("(k p) n -> p k n", p=P)
    fin_d = w_ffn_in[0].rearrange("(k p) n -> p k n", p=P)
    fout_d = w_ffn_out[0].rearrange("(k p) n -> p k n", p=P)
    ada_d = w_ada[0].rearrange("(k p) n -> p k n", p=P)

    with ExitStack() as ctx:
        cursor = [(nc.sbuf_base + 63) // 64 * 64]

        def place(name, shape, dtype=F32, at=None):
            size = int(np.prod(shape[1:])) * (2 if dtype == BF16 else 4)
            off = cursor[0] if at is None else at
            t = nc.alloc_sbuf_tensor_at(name, list(shape), dtype, offset=off)
            if at is None:
                cursor[0] = (off + size + 63) // 64 * 64
            return t

        raw_at = cursor[0]
        raw = [place(f"raw{s}", [P, CH]) for s in range(RAW)]
        w_hi = [place(f"w_hi{s}", [P, CH], F32R) for s in range(SPL)]
        w_lo = [place(f"w_lo{s}", [P, CH], F32R) for s in range(SPL)]
        h_at = cursor[0]
        h_hi = place("h_hi", [P, KD, TB], F32R)
        h_lo = place("h_lo", [P, KD, TB], F32R)
        tr_at = cursor[0]
        tr = [place(f"tr{s}", [P, TB]) for s in range(4)]
        dt_at = cursor[0]
        dt_ = [place(f"dt{s}", [P, TB]) for s in range(4)]
        junk = place("junk", [P, D], BF16)
        g2b = place("g2b", [P, D])
        ident = place("ident", [P, P])
        mean_w = place("mean_w", [P, P])
        zero1 = place("zero1", [P, 1])
        eps1 = place("eps1", [P, 1])
        half_pi = place("half_pi", [P, 1])
        sign = place("sign", [P, 1])
        nsign = place("nsign", [P, 1])
        mod = place("mod", [P, 4 * KD])
        vt = place("vt", [P, 6 * KD + 3 * KD + 3 * KC])
        bmod, c_in, ng = vt[:, 0:6 * KD], vt[:, 6 * KD:7 * KD], vt[:, 7 * KD:9 * KD]
        cvec = vt[:, 9 * KD:].rearrange("p (a k) -> p a k", a=3)
        scale = [place(f"scale{n}", [P, KD]) for n in range(2)]
        ss = place("ss", [P, TT])
        sd = place("sd", [P, TT])
        rs = place("rs", [P, TT])
        over = cursor[0]
        g1b = place("g1b", [P, D])
        uc = place("uc", [P, KC, HALO + TB])
        cwt = place("cwt", [P, KC, TAPS])
        carry = place("carry", [P, G])
        ctmp = place("ctmp", [P, G])
        mag_t = place("mag_t", [P, G])
        cos_t = place("cos_t", [P, NC + 1, G])
        sin_t = place("sin_t", [P, NC + 1, G])
        kept = cursor[0]
        ssm_m = [place(f"ssm_m{s}", [P, CH]) for s in range(3)]
        xr = [place(f"xr{s}", [P, HALF]) for s in range(4)]
        yn_at = cursor[0]
        yn_hi = place("yn_hi", [P, KC, TB], F32R)
        ync_at = cursor[0]
        yn_lo = place("yn_lo", [P, KC, TB], F32R)
        ys_hi = place("ys_hi", [P, KS, TB], F32R)
        yz_at = cursor[0]
        ys_lo = place("ys_lo", [P, KS, TB], F32R)
        mc_at = cursor[0]
        m_hi = place("m_hi", [P, KD, TB], F32R)
        ms_at = cursor[0]
        m_lo = place("m_lo", [P, KD, TB], F32R)
        end_kept = cursor[0]
        xs = place("xs", [P, TT, D])
        uz = place("uz", [P, KS, T, NC], at=yn_at)
        sq = place("sq", [P, KC, TB], at=yn_at)
        yc = place("yc", [P, KC, TB], at=ync_at)
        yz = place("yz", [P, KS, T, NC], at=yz_at)
        sg_c = place("sg_c", [P, KD, TB], at=mc_at)
        sg_s = place("sg_s", [P, KD, TB], at=ms_at)
        cursor[0] = end_kept
        u8 = place("u8", [P, G, NC])
        wst = place("wst", [P, G, NC + 1])
        cursor[0] = over
        hid_hi = place("hid_hi", [P, KF, TB], F32R)
        hid_lo = place("hid_lo", [P, KF, TB], F32R)
        x3 = place("x3", [P, TT, D])
        fgb = place("fgb", [P, D])
        assert cursor[0] <= end_kept
        cursor[0] = kept
        vm = place("vm", [P, G, T + 1, HG])
        wm = place("wm", [P, G, T, HG])
        bx1 = place("bx1", [P, G, HG])
        bx2 = place("bx2", [P, G, HG])
        b1 = place("b1", [P, G, HG])
        b2 = place("b2", [P, G, HG])
        c1 = place("c1", [P, G, HG])
        c2 = place("c2", [P, G, HG])
        cx = place("cx", [P, 2, 4, P])
        ptmp_at = cursor[0]
        ptmp = place("ptmp", [P, G, HG])
        modrow = place("modrow", [4, HALF], at=ptmp_at)
        jexp = place("jexp", [P, T + 1, G])
        jer = place("jer", [P, T + 1, G])
        jei = place("jei", [P, T + 1, G])
        sv = place("sv", [P, 12, G])
        iota_i = place("iota_i", [P, NC + 1], I32)
        iota_f = place("iota_f", [P, NC + 1])
        cact = place("cact", [P, KD])
        dvec = place("dvec", [HG, G])
        cbc = place("cbc", [P, KD, P])
        ones = place("ones", [P, P])
        zc = place("zc", [P, KD, 7])
        ddiag = place("ddiag", [HG, G, HG])
        nat_v = place("nat_v", [6 * KD + 3 * KD + 3 * KC, P])
        nat_a = place("nat_a", [2 * G, P])
        nat_w = place("nat_w", [KC * TAPS, P])
        kst_at = end_kept - (T - 1) * G * HG * 4
        assert cursor[0] <= kst_at, (cursor[0], kst_at)
        kst = place("kst", [HG, G, 2 * T - 1, HG], at=kst_at)
        ada = [place(f"ada{s}", [P, KD // 2, HALF], at=raw_at + s * KD * HALF * 2) for s in range(ADA)]
        acc = place("acc", [P, 2, HALF], at=raw_at + ADA * KD * HALF * 2)
        bg = place("bg", [P, 2, D], at=dt_at)
        cursor[0] = h_at
        karg = place("karg", [P, 2, NC + 1, G])
        ktmp = place("ktmp", [P, NC + 1, G])
        jarg = place("jarg", [P, 2, T + 1, G])
        jtmp = place("jtmp", [P, T + 1, G])
        assert cursor[0] <= tr_at

        bank = [ctx.enter_context(nc.psum_tensor(f"bank{i}", [P, 512], F32)) for i in range(8)]
        Z, Q = [0, 1, 2, 3], [4, 5, 6, 7]

        def sem(name):
            return ctx.enter_context(nc.semaphore(name))

        R = range
        norm_act = ["ns0", "ns1", "ns2", "ns3", "nsd"]
        norm_dve = ["nms", "nr", "nx0", "nx1", "nx2", "nx3"]
        h_steps = [f"h{k}" for k in R(KD)]
        h_act = [n for k in R(KD) for n in (f"hh{k}", f"h{k}")]
        h_dve = [f"hl{k}" for k in R(KD)]

        GX, GY = 4, 7
        pair = lambda p: (2 * p, 2 * p + 1)
        gl = lambda lo, hi: [f"gl{i}" for i in R(lo, hi)]
        pe_mix = [f"us{m}" for m in R(KS)] + [f"u{a}{m}" for m in R(KC) for a in "ag"]
        pe_mix += [f"S{q}" for q in R(NQ)] + gl(0, GY)
        for q in R(NQ):
            pe_mix += [f"Y{q}", f"gl{GY + q}"]
        pe_mix += gl(GY + NQ, 2 * KD)
        for p in R(KD // 2):
            pe_mix += [f"{a}{m}" for a in ("za", "zb") for m in pair(p)]
            pe_mix += [["ln1"], ["ln2"], [], []][p]
        for p in R(KD // 2):
            pe_mix += [f"h{k}" for k in pair(p)] + [f"cp{m}" for m in pair(p)]
        for f in R(2):
            pe_mix += [f"oc{f}{j}" for j in R(KD // 2 - 1)] + [f"o{f}{i}" for i in R(TT)]
        pe_loop = ["fg0", "fu0", "fg1", "fu1"]
        pe_out = []
        for f in R(2):
            for j in R(KF // 2 - 1):
                pe_out += [f"fc{f}_{j}"] + ([f"h{j - 1}"] if f == 0 and 1 <= j <= KD else [])
            pe_out += [f"p{f}{i}" for i in R(TT)]
        ada_steps = lambda lo, hi: [f"ada{n}" for n in R(lo, hi) if SLABS[n][0] == "pe"]
        pe_pro = ["v0", "v1", "v2"] + ada_steps(0, first_gate) + ["mt", "ct0", "ct1"] + h_steps
        pe_pro += ada_steps(first_gate, last_slab(3) + 1) + [f"wt{n}" for n in R(8)]
        pe_pro += ada_steps(last_slab(3) + 1, len(SLABS)) + ["mt2", "sg0", "sg1"]
        pe_pro += [f"kk{n}" for n in R(8)]
        tensor = Steps(sem("tensor_done"), [
            ("pro", 1, [(pe_pro, 1)]), ("mix", NB, [(pe_mix, 1)]),
            ("ffn", NB, [(pe_loop, FI), (pe_out, 1)])])

        act_mix = [f"us{m}" for m in R(KS)] + [f"ug{m}" for m in R(KC)] + [f"S{q}" for q in R(NQ)]
        act_mix += gl(0, GY)
        for q in R(NQ):
            act_mix += [f"Y{q}", f"gl{GY + q}"]
        act_mix += gl(GY + NQ, 2 * KD - 2) + [f"{a}{m}" for m in R(KS) for a in ("gh", "ge")]
        act_mix += gl(2 * KD - 2, 2 * KD)
        act_mix += ["zb0", "zb1"] + [f"sq{m}" for m in R(KC)] + ["zb2", "zb3", "lsd"] + norm_act
        act_mix += ["zb4", "zb5"] + [f"{a}{m}" for m in R(KC) for a in ("sh", "si")] + ["zb6", "zb7"] + h_act
        act_loop = ["fs0", "fs1"]
        act_out = norm_act + h_act + [f"fq{i}" for i in R(TT)] + ["fsd"]
        act_pro = ["cs", "dt", "ej", "m8", "sj", "cj", "sk", "ck"] + norm_act + h_act
        act_pro += [f"wt{n}" for n in R(8)] + [f"kk{n}" for n in R(8)]
        scal = Steps(sem("scalar_done"), [
            ("pro", 1, [(act_pro, 1)]), ("mix", NB, [(act_mix, 1)]), ("ffn", NB, [(act_out, 1)])])
        silu = Steps(sem("silu_done"), [("start", 1, [(["a", "b"], 1)]), ("ffn", NB, [(act_loop, FI)])])

        CUT = [[0, 13, 15, TAPS, TAPS], [0, 13, 15, TAPS, TAPS], [0, 12, 14, TAPS, TAPS], [0, 3, 6, TAPS, TAPS]]

        def conv_steps(part, tiles):
            longest = max(CUT[m][part + 1] - CUT[m][part] for m in tiles)
            return [(CUT[m][part] + n, m) for n in R(longest) for m in tiles if CUT[m][part] + n < CUT[m][part + 1]]

        taps = lambda part: [f"c{t}_{m}" for t, m in conv_steps(part, R(KC))]
        dve_mix = []
        for m in R(KC):
            dve_mix += [f"u{m}"] + [f"c{t}_{m}" for t, _ in conv_steps(0, [m])]
        for q in R(NQ):
            dve_mix += [f"Rt{q}", f"Rc{q}"]
        dve_mix += [f"Rs{q}" for q in R(NQ)] + ["in"] + [f"sc{g}" for g in R(G)] + ["last"]
        dve_mix += taps(1)
        for q in R(NQ):
            dve_mix += [f"Dt{q}", f"Dc{q}"]
        dve_mix += ["dc1", "dc2"] + [f"Ds{q}" for q in R(NQ)] + ["dc3"]
        zz = lambda p: [f"{a}{m}" for a in ("ms", "mt") for m in pair(p)]
        dve_mix += taps(2) + [f"ysl{m}" for m in R(KS)] + taps(3) + ["halo"]
        dve_mix += ["s11", "s12", "s13"] + zz(0) + [f"cen{m}" for m in R(KC)]
        dve_mix += ["s21", "s22", "s23"] + zz(1) + ["rec"] + [f"nm{m}" for m in R(KC)]
        dve_mix += norm_dve[:2] + zz(2) + norm_dve[2:] + [f"ynl{m}" for m in R(KC)] + zz(3)
        for p in R(KD // 2):
            dve_mix += [f"hl{k}" for k in pair(p)]
            dve_mix += [f"{a}{m}" for a in ("mc", "ma", "mh", "ml") for m in pair(p)]
        for f in R(2):
            dve_mix += [n for i in R(TT) for n in (f"oa{f}{i}", f"ob{f}{i}")]
        dve_loop = [f"{a}{j}" for a in ("fm", "fh", "fl") for j in R(2)]
        dve_out = norm_dve + h_dve
        for f in R(2):
            dve_out += [f"p{a}{f}{i}" for a in "ab" for i in R(TT)]
        dve_out += ["fms", "fr"] + [f"fx{i}" for i in R(TT)]
        vec = Steps(sem("vector_done"), [
            ("start", 1, [(list("abcdefgh"), 1)]), ("pro", 1, [(norm_dve + h_dve, 1)]),
            ("mix", NB, [(dve_mix, 1)]), ("ffn", NB, [(dve_out, 1)])])
        hidden = Steps(sem("hidden_done"), [
            ("start", 1, [(list("abcdef"), 1)]), ("ffn", NB, [(dve_loop, FI)])])

        def is_z(n):
            return n[0] in "uzh" or n[:2] in ("gl", "cp") or n[:2] in ("fg", "fu")

        plan = {}
        for phase, names in (("pro", h_steps), ("mix", pe_mix), ("ffn", pe_loop + pe_out)):
            z = 0
            for n in names:
                if n[:2] in ("oc", "fc"):
                    continue
                if is_z(n) or n[:2] == "o0":
                    plan[phase, n] = z % 4
                    z += 1
            assert z % 4 == 0
        for q in R(NQ):
            plan["mix", f"S{q}"] = plan["mix", f"Y{q}"] = 4 + q
        plan["mix", "ln1"], plan["mix", "ln2"] = 4, 5
        for i in R(TT):
            plan["mix", f"o1{i}"] = plan["ffn", f"p0{i}"] = plan["ffn", f"p1{i}"] = 4 + i

        def reader(phase, n):
            if n in pe_loop:
                return (silu, "fs" + n[2]) if n[:2] == "fg" else (hidden, "fm" + n[2])
            if n[:2] in ("us", "gl", "zb", "ug") or n[0] in "hSY":
                return scal, n
            if n == "ln2":
                return scal, "lsd"
            return vec, {"ua": "u" + n[2:], "ln": "cen3", "cp": "mc" + n[2:], "za": "ms" + n[2:],
                         "o0": "oa" + n[1:], "o1": "oa" + n[1:], "p0": "pa" + n[1:], "p1": "pa" + n[1:]}[n[:2]]

        order = {"pro": h_steps, "mix": pe_mix, "ffn": pe_loop + pe_out}

        def bank_free(phase, b, n, it=0):
            use = [m for m in order[phase] if plan.get((phase, m)) == plan[phase, n]]
            j = use.index(n)
            if j and not (n in pe_loop):
                who, step = reader(phase, use[j - 1])
                last = FI - 1 if use[j - 1] in pe_loop else 0
                return who.after(phase, b, step, last)
            if n in pe_loop:
                who, step = reader(phase, n)
                return who.before(phase, b, step, it)
            who, step = reader(phase, use[-1])
            return who.before(phase, b, step, None)

        raw_in = [sem(f"raw_in{s}") for s in R(RAW)]
        hi_done = sem("hi_done")
        split_done = sem("split_done")
        ssm_in = [sem(f"ssm_in{s}") for s in R(3)]
        turned_in = [sem(f"turned_in{q}") for q in R(NQ)]
        carry_in = sem("carry_in")
        xs_in = sem("xs_in")
        uz_out, u8_in, y_out, yz_in = sem("uz_out"), sem("u8_in"), sem("y_out"), sem("yz_in")
        xr_in = [sem(f"xr_in{s}") for s in R(4)]
        x2_out = [sem(f"x2_out{s}") for s in R(4)]
        x3_in, final_out = sem("x3_in"), sem("final_out")
        vectors_in = sem("vectors_in")
        small_in = sem("small_in")
        bg_in = sem("bg_in")
        consts = sem("consts")
        ada_in = [sem(f"ada_in{s}") for s in R(ADA)]
        acc_done = sem("acc_done")
        acc_link = sem("acc_link")
        pro_v = sem("prologue_vector")
        mat_out = sem("mat_out")
        fg_in = sem("fg_in")
        SMALL_LOADS = 4 + 4 + 1
        mark = {}

        chunk_no = {}
        n = 0
        for s in pe_mix:
            if s[:2] in ("us", "gl", "ua", "ug", "oc") or s in ("o03", "o13") or (
                    s[:2] in ("cp", "za", "zb") and int(s[2]) % 2):
                n += 1
                chunk_no["mix", n] = s
        assert n == NMIX
        n = 2 * KF
        for s in pe_out:
            if s[:2] == "fc" or s in ("p03", "p13"):
                n += 1
                chunk_no["ffn", n] = s
        assert n == NFFN

        def chunk_used(phase, b, n, it=0):
            return tensor.after(phase, b, chunk_no[phase, n])

        block = ctx.enter_context(nc.Block())

        @block.vector
        def _(dve):
            v = nc.vector

            def link(ins, name=None):
                mark["n"] = mark.get("n", 0) + 1
                ins.then_inc(pro_v, 1)
                dve.wait_ge(pro_v, mark["n"])
                if name:
                    mark[name] = mark["n"]

            dve.wait_ge(consts, 6)
            TWO_PI = 2 * np.pi
            c1_ = float(np.float32(6.28125))
            c2_ = float(np.float32(TWO_PI - 6.28125))
            MAGIC = float(1.5 * 2 ** 23)
            PI_ = float(np.float32(3.1415925))

            def reduce_angle(dst, src, tmp):
                link(v.tensor_scalar(tmp, src, float(1 / TWO_PI), MAGIC, ALU.mult, ALU.add))
                link(v.tensor_scalar(tmp, tmp, MAGIC, None, ALU.subtract))
                link(v.scalar_tensor_tensor(out=dst, in0=tmp, scalar=-c1_, in1=src, op0=ALU.mult, op1=ALU.add))
                link(v.scalar_tensor_tensor(out=dst, in0=tmp, scalar=-c2_, in1=dst, op0=ALU.mult, op1=ALU.add))
                link(v.tensor_scalar(dst, dst, PI_, -PI_, ALU.min, ALU.max))

            def angles(table, tmp, angle, n, name):
                flat = lambda a: a.rearrange("p a b -> p (a b)")
                steps = iota_f[:, 0:n].unsqueeze(2).broadcast_to([P, n, G])
                link(v.tensor_tensor(table[:, 0, :, :], steps, angle.unsqueeze(1).broadcast_to([P, n, G]), ALU.mult))
                reduce_angle(flat(table[:, 0, :, :]), flat(table[:, 0, :, :]), flat(tmp[:, :, :]))
                x_ = flat(table[:, 0, :, :])
                link(v.scalar_tensor_tensor(out=flat(table[:, 1, :, :]), in0=x_, scalar=-1.0, in1=x_,
                                            op0=ALU.mult, op1=ALU.min), name)

            def wait_self(phase, b, name, it=0):
                dve.wait_ge(*vec.after(phase, b, name, it))

            def low(lo, src, hi, phase, step):
                v.tensor_tensor(lo, src, hi.bitcast(F32), ALU.subtract).then_inc(*vec.step(phase, step))

            def norm_roots(phase, b):
                dve.wait_ge(*scal.after(phase, b, "ns3"))
                v.tensor_scalar(ss[:], ss[:], 1.0 / D, EPS, ALU.mult, ALU.add).then_inc(*vec.step(phase, "nms"))
                dve.wait_ge(*scal.after(phase, b, "nsd"))
                v.reciprocal(rs[:], sd[:]).then_inc(*vec.step(phase, "nr"))

            def norm_scale(phase, b):
                wait_self(phase, b, "nr")
                for i in R(TT):
                    v.tensor_scalar(xs[:, i, :], xs[:, i, :], rs[:, i:i + 1], None, ALU.mult)\
                        .then_inc(*vec.step(phase, f"nx{i}"))

            def h_split(phase, b, k):
                dve.wait_ge(*scal.after(phase, b, f"h{k}"))
                low(h_lo[:, k, :], tr[k % 4][:], h_hi[:, k, :], phase, f"hl{k}")

            def scale_of(which):
                link(v.tensor_scalar(scale[which][:], mod[:, (2 * which + 1) * KD:(2 * which + 2) * KD],
                                     1.0, None, ALU.add))
                link(v.tensor_tensor(scale[which][:], scale[which][:], ng[:, which * KD:(which + 1) * KD],
                                     ALU.mult), f"scale{which}")

            def shift_and_scale(which):
                dve.wait_ge(*tensor.after("pro", 0, f"ada{last_slab((1, 4)[which])}"))
                link(v.tensor_copy(modrow[:], bank[5][0:4, :]), f"modrow{which}")
                dve.wait_ge(*tensor.after("pro", 0, ("mt", "mt2")[which]))
                by_row = lambda a: a.rearrange("p (r j) -> p r j", j=4)
                link(v.tensor_tensor(by_row(mod[:, 2 * which * KD:2 * (which + 1) * KD]),
                                     bank[6][:, 0:16].rearrange("p (j r) -> p r j", j=4),
                                     by_row(bmod[:, 3 * which * KD:(3 * which + 2) * KD]), ALU.add))
                scale_of(which)

            dve.wait_ge(*tensor.after("pro", 0, "v2"))
            nv = 6 * KD + 3 * KD + 3 * KC
            link(v.tensor_copy(sv[:, 0:2, :].rearrange("p a g -> p (a g)"), bank[0][:, 0:2 * G]))
            link(v.tensor_copy(vt[:], bank[1][:, 0:nv]), "vt")
            link(v.tensor_copy(cwt[:].rearrange("p m t -> p (m t)"), bank[2][:, 0:KC * TAPS]))
            dve.wait_ge(*scal.after("pro", 0, "cs"))
            link(v.tensor_copy(zc[:, :, 3], cact[:]), "zc")
            link(v.tensor_copy(cbc[:], cact[:].unsqueeze(2).broadcast_to([P, KD, P])), "cbc")
            ar, ai, dt, th, lg, ph, t0, t1 = (sv[:, n, :] for n in R(8))
            qr, qi, nr, den = (sv[:, n, :] for n in R(8, 12))
            dve.wait_ge(*scal.after("pro", 0, "dt"))
            link(v.tensor_tensor(lg, dt, ar, ALU.mult))
            link(v.tensor_tensor(jexp[:], iota_f[:, 0:T + 1].unsqueeze(2).broadcast_to([P, T + 1, G]),
                                 lg.unsqueeze(1).broadcast_to([P, T + 1, G]), ALU.mult))
            link(v.tensor_tensor(th, dt, ai, ALU.mult))
            reduce_angle(th, th, t0)
            angles(jarg, jtmp, th, T + 1, "jargs")
            flat2 = lambda a: a[:].rearrange("p a b -> p (a b)")
            link(v.tensor_scalar(ph, th, float(T), None, ALU.mult))
            reduce_angle(ph, ph, t0)
            angles(karg, ktmp, ph, NC + 1, "kargs")
            dve.wait_ge(*scal.after("pro", 0, "cj"))
            link(v.tensor_tensor(jer[:], jexp[:], jer[:], ALU.mult))
            link(v.tensor_tensor(jei[:], jexp[:], jei[:], ALU.mult))
            e_r, e_i = jer[:, 1, :], jei[:, 1, :]
            link(v.tensor_scalar(nr, e_r, -1.0, None, ALU.add))
            link(v.tensor_tensor(t0, ar, ar, ALU.mult))
            link(v.tensor_tensor(t1, ai, ai, ALU.mult))
            link(v.tensor_tensor(den, t0, t1, ALU.add))
            link(v.reciprocal(den, den))
            link(v.tensor_tensor(t0, nr, ar, ALU.mult))
            link(v.tensor_tensor(t1, e_i, ai, ALU.mult))
            link(v.tensor_tensor(qr, t0, t1, ALU.add))
            link(v.tensor_tensor(qr, qr, den, ALU.mult))
            link(v.tensor_tensor(t0, e_i, ar, ALU.mult))
            link(v.tensor_tensor(t1, nr, ai, ALU.mult))
            link(v.tensor_tensor(qi, t0, t1, ALU.subtract))
            link(v.tensor_tensor(qi, qi, den, ALU.mult))

            def by_h(a):
                return a.unsqueeze(2).broadcast_to([P, G, HG])

            dve.wait_ge(small_in, SMALL_LOADS * 16)
            link(v.tensor_tensor(b1[:], bx1[:], by_h(qr), ALU.mult))
            link(v.tensor_tensor(ptmp[:], bx2[:], by_h(qi), ALU.mult))
            link(v.scalar_tensor_tensor(out=flat2(b1), in0=flat2(ptmp), scalar=sign[:, 0:1], in1=flat2(b1),
                                        op0=ALU.mult, op1=ALU.add))
            link(v.tensor_tensor(b2[:], bx2[:], by_h(qr), ALU.mult))
            link(v.tensor_tensor(ptmp[:], bx1[:], by_h(qi), ALU.mult))
            link(v.scalar_tensor_tensor(out=flat2(b2), in0=flat2(b2), scalar=sign[:, 0:1], in1=flat2(ptmp),
                                        op0=ALU.mult, op1=ALU.subtract))
            norm_roots("pro", 0)
            norm_scale("pro", 0)
            shift_and_scale(0)
            dve.wait_ge(*tensor.after("pro", 0, "ct1"))
            link(v.tensor_scalar(flat2(c1), bank[3][:], nsign[:, 0:1], None, ALU.mult))
            link(v.tensor_scalar(flat2(c2), bank[4][:], -1.0, None, ALU.mult), "cc")
            for s in R(T):
                j = T - 1 - s
                link(v.tensor_tensor(wm[:, :, s, :], b1[:], by_h(jer[:, j, :]), ALU.mult))
                link(v.tensor_tensor(ptmp[:], b2[:], by_h(jei[:, j, :]), ALU.mult))
                link(v.tensor_tensor(wm[:, :, s, :], wm[:, :, s, :], ptmp[:], ALU.add), "wm" if s == T - 1 else None)
            for k in R(KD):
                h_split("pro", 0, k)
            for j in R(T + 1):
                link(v.tensor_tensor(vm[:, :, j, :], c1[:], by_h(jer[:, j, :]), ALU.mult))
                link(v.tensor_tensor(ptmp[:], c2[:], by_h(jei[:, j, :]), ALU.mult))
                link(v.tensor_tensor(vm[:, :, j, :], vm[:, :, j, :], ptmp[:], ALU.add), "vm" if j == T else None)
            dve.wait_ge(bg_in, 32)
            for h in R(2):
                cols = slice(h * HALF, (h + 1) * HALF)
                dve.wait_ge(*tensor.after("pro", 0, f"ada{SLABS.index(('pe', 2, h, 1))}"))
                link(v.tensor_tensor(g1b[:, cols], bank[(4, 7)[h]][:], bg[:, 0, cols], ALU.add), f"g1b{h}")
            shift_and_scale(1)
            for h in R(2):
                cols = slice(h * HALF, (h + 1) * HALF)
                dve.wait_ge(*tensor.after("pro", 0, f"sg{h}"))
                link(v.tensor_tensor(g2b[:, cols], bank[6 + h][:], bg[:, 1, cols], ALU.add), "g2b")
            link(v.tensor_tensor(ddiag[:], ident[0:HG, 0:HG].unsqueeze(1).broadcast_to([HG, G, HG]),
                                 dvec[:].unsqueeze(2).broadcast_to([HG, G, HG]), ALU.mult))
            dve.wait_ge(*scal.after("pro", 0, "kk7"))
            link(v.tensor_tensor(kst[:, :, T - 1, :], kst[:, :, T - 1, :], ddiag[:], ALU.add), "kst")

            def mixers(b):
                def conv(part, tiles=R(KC)):
                    for t, m in conv_steps(part, tiles):
                        src = uc[:, m, t:t + TB]
                        w = cwt[:, m, t:t + 1]
                        if t == 0:
                            wait_self("mix", b, f"u{m}")
                            ins = v.tensor_scalar(yc[:, m, :], src, w, cvec[:, 0, m:m + 1], ALU.mult, ALU.add)
                        else:
                            wait_self("mix", b, f"c{t - 1}_{m}")
                            ins = v.scalar_tensor_tensor(out=yc[:, m, :], in0=src, scalar=w, in1=yc[:, m, :],
                                                         op0=ALU.mult, op1=ALU.add)
                        ins.then_inc(*vec.step("mix", f"c{t}_{m}"))

                for m in R(KC):
                    dve.wait_ge(*scal.after("mix", b, f"ug{m}"))
                    v.tensor_tensor(uc[:, m, HALO:], bank[plan["mix", f"ua{m}"]][:], tr[m][:], ALU.mult)\
                        .then_inc(*vec.step("mix", f"u{m}"))
                    conv(0, [m])

                def quarter(a, q, lo, hi_):
                    return a[:, q * GQ:(q + 1) * GQ, lo:hi_]

                def table(t, q, lo, hi_):
                    return t[:, lo:hi_, q * GQ:(q + 1) * GQ].rearrange("p k g -> p g k")

                def by_g(a):
                    return a.rearrange("p (g k) -> p g k", g=GQ)

                for q in R(NQ):
                    dve.wait_ge(turned_in[q], 32 * (2 * b + 1))
                    v.tensor_tensor(by_g(dt_[q][:]), by_g(dt_[q][:]), table(sin_t, q, 1, NC + 1),
                                    ALU.mult).then_inc(*vec.step("mix", f"Rt{q}"))
                    v.tensor_tensor(quarter(wst, q, 1, NC + 1), quarter(wst, q, 1, NC + 1), table(cos_t, q, 1, NC + 1),
                                    ALU.mult).then_inc(*vec.step("mix", f"Rc{q}"))
                for q in R(NQ):
                    wait_self("mix", b, f"Rc{q}")
                    v.tensor_tensor(quarter(wst, q, 1, NC + 1), quarter(wst, q, 1, NC + 1), by_g(dt_[q][:]),
                                    ALU.add).then_inc(*vec.step("mix", f"Rs{q}"))
                v.tensor_copy(wst[:, :, 0], carry[:]).then_inc(*vec.step("mix", "in"))
                for g in R(G):
                    if g == 0:
                        wait_self("mix", b, "in")
                    v.tensor_tensor_scan(wst[:, g, 1:], mag_t[:, g:g + 1].broadcast_to([P, NC]), wst[:, g, 1:],
                                         carry[:, g:g + 1], ALU.mult, ALU.add).then_inc(*vec.step("mix", f"sc{g}"))
                wait_self("mix", b, f"sc{G - 1}")
                v.tensor_copy(carry[:], wst[:, :, NC]).then_inc(*vec.step("mix", "last"))
                conv(1)
                for q in R(NQ):
                    dve.wait_ge(turned_in[q], 32 * (2 * b + 2))
                    v.tensor_tensor(by_g(dt_[q][:]), by_g(dt_[q][:]), table(sin_t, q, 0, NC),
                                    ALU.mult).then_inc(*vec.step("mix", f"Dt{q}"))
                    v.tensor_tensor(quarter(wst, q, 0, NC), quarter(wst, q, 0, NC), table(cos_t, q, 0, NC),
                                    ALU.mult).then_inc(*vec.step("mix", f"Dc{q}"))
                dve.wait_ge(carry_in, 32 * (b + 1))
                v.tensor_tensor(ctmp[:], ctmp[:], sin_t[:, NC, :], ALU.mult)\
                    .then_inc(*vec.step("mix", "dc1"))
                v.tensor_tensor(carry[:], carry[:], cos_t[:, NC, :], ALU.mult).then_inc(*vec.step("mix", "dc2"))
                for q in R(NQ):
                    wait_self("mix", b, f"Dc{q}")
                    v.tensor_tensor(quarter(wst, q, 0, NC), quarter(wst, q, 0, NC), by_g(dt_[q][:]),
                                    ALU.subtract).then_inc(*vec.step("mix", f"Ds{q}"))
                wait_self("mix", b, "dc2")
                v.tensor_tensor(carry[:], carry[:], ctmp[:], ALU.subtract).then_inc(*vec.step("mix", "dc3"))
                conv(2)
                for m in R(KS):
                    dve.wait_ge(*scal.after("mix", b, f"ge{KS - 1}"))
                    low(ys_lo[:, m, :], tr[m][:], ys_hi[:, m, :], "mix", f"ysl{m}")
                conv(3)
                v.tensor_copy(uc[:, :, 0:HALO], uc[:, :, TB:]).then_inc(*vec.step("mix", "halo"))

                def gated_ssm(p):
                    for m in pair(p):
                        dve.wait_ge(*scal.after("mix", b, f"zb{m}"))
                        if p:
                            wait_self("mix", b, f"mt{m - 2}")
                        v.tensor_tensor(dt_[m % 2][:], bank[plan["mix", f"za{m}"]][:], tr[m % 2][:], ALU.mult)\
                            .then_inc(*vec.step("mix", f"ms{m}"))
                    for m in pair(p):
                        wait_self("mix", b, f"ms{m}")
                        v.tensor_tensor(sg_s[:, m, :], dt_[m % 2][:], sg_s[:, m, :], ALU.mult)\
                            .then_inc(*vec.step("mix", f"mt{m}"))

                def channel_sum(dst, src, name):
                    for m in R(1, KC):
                        if m > 1:
                            wait_self("mix", b, f"{name}{m - 1}")
                        v.tensor_tensor(dst, dst if m > 1 else src[:, 0, :], src[:, m, :], ALU.add)\
                            .then_inc(*vec.step("mix", f"{name}{m}"))

                wait_self("mix", b, f"c{TAPS - 1}_{KC - 1}")
                channel_sum(dt_[2][:], yc, "s1")
                gated_ssm(0)
                dve.wait_ge(*tensor.after("mix", b, "ln1"))
                for m in R(KC):
                    v.tensor_tensor(yc[:, m, :], yc[:, m, :], bank[plan["mix", "ln1"]][:], ALU.subtract)\
                        .then_inc(*vec.step("mix", f"cen{m}"))
                dve.wait_ge(*scal.after("mix", b, f"sq{KC - 1}"))
                channel_sum(dt_[3][:], sq, "s2")
                gated_ssm(1)
                dve.wait_ge(*scal.after("mix", b, "lsd"))
                v.reciprocal(dt_[3][:], dt_[2][:]).then_inc(*vec.step("mix", "rec"))
                wait_self("mix", b, "rec")
                for m in R(KC):
                    v.tensor_tensor(yc[:, m, :], yc[:, m, :], dt_[3][:], ALU.mult).then_inc(*vec.step("mix", f"nm{m}"))
                norm_roots("mix", b)
                gated_ssm(2)
                norm_scale("mix", b)
                for m in R(KC):
                    dve.wait_ge(*scal.after("mix", b, f"si{m}"))
                    low(yn_lo[:, m, :], tr[2 + m % 2][:], yn_hi[:, m, :], "mix", f"ynl{m}")
                gated_ssm(3)
                for p in R(KD // 2):
                    for k in pair(p):
                        h_split("mix", b, k)
                    for m in pair(p):
                        dve.wait_ge(*tensor.after("mix", b, f"cp{m}"))
                        wait_self("mix", b, f"ml{m - 2}" if p else f"mt{KD - 2 + m}")
                        v.tensor_tensor(dt_[m % 2][:], bank[plan["mix", f"cp{m}"]][:], sg_c[:, m, :], ALU.mult)\
                            .then_inc(*vec.step("mix", f"mc{m}"))
                    for m in pair(p):
                        wait_self("mix", b, f"mc{m}")
                        v.tensor_tensor(dt_[m % 2][:], dt_[m % 2][:], sg_s[:, m, :], ALU.add)\
                            .then_inc(*vec.step("mix", f"ma{m}"))
                    for m in pair(p):
                        wait_self("mix", b, f"ma{m}")
                        v.tensor_copy(m_hi[:, m, :], dt_[m % 2][:]).then_inc(*vec.step("mix", f"mh{m}"))
                    for m in pair(p):
                        wait_self("mix", b, f"mh{m}")
                        v.tensor_tensor(m_lo[:, m, :], dt_[m % 2][:], m_hi[:, m, :].bitcast(F32), ALU.subtract)\
                            .then_inc(*vec.step("mix", f"ml{m}"))
                for f in R(2):
                    for i in R(TT):
                        dve.wait_ge(*tensor.after("mix", b, f"o{f}{i}"))
                        v.tensor_tensor(dt_[i][:], bank[plan["mix", f"o{f}{i}"]][:], g1b[:, f * HALF:(f + 1) * HALF],
                                        ALU.mult).then_inc(*vec.step("mix", f"oa{f}{i}"))
                        dve.wait_ge(xr_in[i], 16 * (2 * b + f + 1))
                        wait_self("mix", b, f"oa{f}{i}")
                        v.tensor_tensor(xr[i][:], xr[i][:], dt_[i][:], ALU.add).then_inc(*vec.step("mix", f"ob{f}{i}"))

            with dve.Fori(0, NB - 1) as b:
                mixers(b)
            vec.again("mix")
            mixers(NB - 1)

            with dve.Fori(0, NB) as b:
                with dve.Fori(0, FI) as it:
                    dve.wait_ge(*vec.start("ffn", b))
                    for j in R(2):
                        dve.wait_ge(*silu.after("ffn", b, f"fs{j}", it))
                        dve.wait_ge(*tensor.after("ffn", b, f"fu{j}", it))
                        dve.wait_ge(*hidden.before("ffn", b, f"fl{j}", it))
                        v.tensor_tensor(dt_[j][:], bank[plan["ffn", f"fu{j}"]][:], tr[j][:], ALU.mult)\
                            .then_inc(*hidden.step("ffn", f"fm{j}"))
                    hid = lambda t, j: t[:, bass.ds(2 * it + j, 1), :]
                    one = lambda a: a.unsqueeze(1)
                    for j in R(2):
                        dve.wait_ge(*hidden.after("ffn", b, f"fm{j}", it))
                        v.tensor_copy(hid(hid_hi, j), one(dt_[j][:])).then_inc(*hidden.step("ffn", f"fh{j}"))
                    for j in R(2):
                        dve.wait_ge(*hidden.after("ffn", b, f"fh{j}", it))
                        v.tensor_tensor(hid(hid_lo, j), one(dt_[j][:]), hid(hid_hi, j).bitcast(F32), ALU.subtract)\
                            .then_inc(*hidden.step("ffn", f"fl{j}"))
                norm_roots("ffn", b)
                norm_scale("ffn", b)
                for k in R(KD):
                    h_split("ffn", b, k)
                for f in R(2):
                    for i in R(TT):
                        dve.wait_ge(*tensor.after("ffn", b, f"p{f}{i}"))
                        if f:
                            wait_self("ffn", b, f"pb0{i}")
                        v.tensor_tensor(dt_[i][:], bank[plan["ffn", f"p{f}{i}"]][:], g2b[:, f * HALF:(f + 1) * HALF],
                                        ALU.mult).then_inc(*vec.step("ffn", f"pa{f}{i}"))
                    if f == 0:
                        dve.wait_ge(x3_in, 16 * (b + 1))
                    for i in R(TT):
                        wait_self("ffn", b, f"pa{f}{i}")
                        part = x3[:, i, f * HALF:(f + 1) * HALF]
                        v.tensor_tensor(part, part, dt_[i][:], ALU.add).then_inc(*vec.step("ffn", f"pb{f}{i}"))
                dve.wait_ge(*scal.after("ffn", b, f"fq{TT - 1}"))
                v.tensor_scalar(ss[:], ss[:], 1.0 / D, EPS, ALU.mult, ALU.add).then_inc(*vec.step("ffn", "fms"))
                dve.wait_ge(*scal.after("ffn", b, "fsd"))
                v.reciprocal(rs[:], sd[:]).then_inc(*vec.step("ffn", "fr"))
                wait_self("ffn", b, "fr")
                dve.wait_ge(fg_in, 16)
                for i in R(TT):
                    v.scalar_tensor_tensor(out=x3[:, i, :], in0=x3[:, i, :], scalar=rs[:, i:i + 1], in1=fgb[:],
                                           op0=ALU.mult, op1=ALU.mult).then_inc(*vec.step("ffn", f"fx{i}"))

        @block.scalar
        def _(act):
            s = nc.scalar

            def load_vectors():
                for row, src in ((0, b_ada[0]), (6 * KD, c[0]), (7 * KD, norm1_g[0]), (8 * KD, norm2_g[0]),
                                 (9 * KD, conv_b[0]), (9 * KD + KC, conv_ln_g[0]), (9 * KD + 2 * KC, conv_ln_b[0])):
                    n = src.shape[0] // P
                    yield act.dma_start(nat_v[row:row + n, :], src.rearrange("(k p) -> k p", p=P))
                for n, src in enumerate((ssm_a_re[0], ssm_a_im[0])):
                    for half in R(2):
                        yield act.dma_start(nat_a[n * G:(n + 1) * G, half * NST:(half + 1) * NST], src)
                yield act.dma_start(sv[:, 2, :], ssm_log_dt[0].partition_broadcast(P))
                for m in R(KC):
                    yield act.dma_start(nat_w[m * TAPS:(m + 1) * TAPS, :], conv_w[0][:, m * P:(m + 1) * P])

            def load_small():
                for n, (re, im) in enumerate(((ssm_c_re, ssm_c_im), (ssm_c_im, ssm_c_re))):
                    flat = lambda a: a[0].rearrange("g h p -> (g h) p").rearrange("(t q) p -> q t p", q=P)
                    yield act.dma_start(cx[:, n, :, 0:NST], flat(re))
                    yield act.dma_start(cx[:, n, :, NST:], flat(im))
                for half in R(2):
                    rows = slice(half * NST, (half + 1) * NST)
                    for dst, src in ((bx1, (ssm_b_re, ssm_b_im)[half]), (bx2, (ssm_b_im, ssm_b_re)[half])):
                        yield act.dma_start(dst[rows, :, :], src[0].rearrange("g p h -> p g h"))
                with nc.allow_non_contiguous_dma(reason="the skip's diagonal, 512 values"):
                    yield act.dma_start(dvec[:], ssm_d[0].rearrange("(g h) -> h g", h=HG))

            mark["vectors"] = mark["small"] = 0
            for ins in load_vectors():
                ins.then_inc(vectors_in, 16)
                mark["vectors"] += 16

            def load_xs(src, row):
                for i in R(TT):
                    act.dma_start(xs[:, i, :], src[bass.ds(row + i * P, P), :]).then_inc(xs_in, 16)

            def norm_stats(phase, b, n_loads):
                act.wait_ge(xs_in, n_loads)
                for i in R(TT):
                    if i:
                        act.wait_ge(*scal.after(phase, b, f"ns{i - 1}"))
                    s.activation(junk[:], xs[:, i, :], ACT.Square, accum_out=ss[:, i:i + 1])\
                        .then_inc(*scal.step(phase, f"ns{i}"))
                act.wait_ge(*vec.after(phase, b, "nms"))
                s.activation(sd[:], ss[:], ACT.Sqrt).then_inc(*scal.step(phase, "nsd"))

            def h_tile(phase, b, k, slot, which, free):
                act.wait_ge(*tensor.after(phase, b, f"h{k}"))
                if free:
                    act.wait_ge(*free)
                for dst, step in ((h_hi[:, k, :], f"hh{k}"), (tr[slot][:], f"h{k}")):
                    s.activation(dst, bank[plan[phase, f"h{k}"]][:], ACT.Identity, scale=scale[which][:, k:k + 1],
                                 bias=mod[:, 2 * which * KD + k:2 * which * KD + k + 1])\
                        .then_inc(*scal.step(phase, step))

            for ins in load_small():
                ins.then_inc(small_in, 16)
                mark["small"] += 16
            assert mark["small"] == SMALL_LOADS * 16
            act.wait_ge(consts, 6)
            act.wait_ge(pro_v, mark["vt"])
            s.activation(cact[:], c_in, ACT.Silu).then_inc(*scal.step("pro", "cs"))
            act.wait_ge(vectors_in, mark["vectors"])
            s.activation(sv[:, 2, :], sv[:, 2, :], ACT.Exp).then_inc(*scal.step("pro", "dt"))
            load_xs(x_d, 0)
            for n, off in enumerate((2 * D, 5 * D)):
                act.dma_start(bg[:, n, :], b_ada[0][off:off + D].partition_broadcast(P)).then_inc(bg_in, 16)
            act.wait_ge(pro_v, mark["jargs"])
            s.activation(jexp[:], jexp[:], ACT.Exp).then_inc(*scal.step("pro", "ej"))
            s.activation(mag_t[:], sv[:, 4, :], ACT.Exp, scale=float(T)).then_inc(*scal.step("pro", "m8"))
            s.activation(jei[:], jarg[:, 0, :, :], ACT.Sin).then_inc(*scal.step("pro", "sj"))
            s.activation(jer[:], jarg[:, 1, :, :], ACT.Sin, bias=half_pi[:, 0:1]).then_inc(*scal.step("pro", "cj"))
            act.wait_ge(pro_v, mark["kargs"])
            s.activation(sin_t[:], karg[:, 0, :, :], ACT.Sin, scale=nsign[:, 0:1]).then_inc(*scal.step("pro", "sk"))
            s.activation(cos_t[:], karg[:, 1, :, :], ACT.Sin, bias=half_pi[:, 0:1]).then_inc(*scal.step("pro", "ck"))
            norm_stats("pro", 0, 64)
            act.wait_ge(pro_v, mark["scale0"])
            act.wait_ge(*scal.after("pro", 0, "ck"))
            for k in R(KD):
                h_tile("pro", 0, k, k % 4, 0, vec.after("pro", 0, f"hl{k - 4}") if k >= 4 else None)
            for n in R(8):
                act.wait_ge(*tensor.after("pro", 0, f"wt{n}"))
                s.activation(wm[:, 4 * n:4 * n + 4, :, :].rearrange("p g s h -> p (g s h)"), bank[n % 4][:], ACT.Copy)\
                    .then_inc(*scal.step("pro", f"wt{n}"))
            for n in R(8):
                act.wait_ge(*tensor.after("pro", 0, f"kk{n}"))
                s.activation(kst[:, 4 * n:4 * n + 4, T - 1:, :],
                             bank[n % 4][0:HG, :].rearrange("p (g s h) -> p g s h", g=4, s=T), ACT.Copy)\
                    .then_inc(*scal.step("pro", f"kk{n}"))
            act.wait_ge(*scal.after("pro", 0, "wt7"))
            act.dma_start(wt_d, wm[:].rearrange("p g s h -> p g (s h)")).then_inc(mat_out, 16)
            act.wait_ge(pro_v, mark["vm"])
            act.dma_start(vk_d[:, :, 0, :], vm[:, :, 1:, :].rearrange("p g s h -> p g (s h)")).then_inc(mat_out, 16)
            act.wait_ge(pro_v, mark["kst"])
            act.wait_ge(acc_done, 5)
            for t in R(T):
                act.dma_start(vk_d[t * HG:(t + 1) * HG, :, 1, :],
                              kst[:, :, T - 1 - t:2 * T - 1 - t, :].rearrange("p g s h -> p g (s h)"))\
                    .then_inc(mat_out, 16)

            def exchange(dst, src, landed):
                for to, half in ((0, 1), (1, 0)):
                    d, s_ = (a[i * NST:(i + 1) * NST] for a, i in ((dst, to), (src, half)))
                    if len(src.shape) == 3:
                        d = d.rearrange("p (g k) -> p g k", g=GQ)
                    act.dma_start(d, s_).then_inc(landed, 16)

            def mixers(b, next_x, row, which):
                act.wait_ge(mat_out, 16 * (2 + T))
                for m in R(KS):
                    act.wait_ge(*tensor.after("mix", b, f"us{m}"))
                    s.activation(uz[:, m, :, :].rearrange("p s c -> p c s"),
                                 bank[plan["mix", f"us{m}"]][:].rearrange("p (c s) -> p c s", s=T), ACT.Copy)\
                        .then_inc(*scal.step("mix", f"us{m}"))
                    act.wait_ge(*scal.after("mix", b, f"us{m}"))
                    act.dma_start(us_d[m * P:(m + 1) * P], uz[:, m, :, :]).then_inc(uz_out, 16)
                act.wait_ge(uz_out, 64 * (b + 1))
                for t in R(T):
                    act.dma_start(u8[t * HG:(t + 1) * HG, :, :], us_d[:, t, :].rearrange("(g h) c -> h g c", h=HG))\
                        .then_inc(u8_in, 16)
                for m in R(KC):
                    act.wait_ge(*tensor.after("mix", b, f"ug{m}"))
                    s.activation(tr[m][:], bank[plan["mix", f"ug{m}"]][:], ACT.Sigmoid)\
                        .then_inc(*scal.step("mix", f"ug{m}"))
                for q in R(NQ):
                    act.wait_ge(*tensor.after("mix", b, f"S{q}"))
                    s.activation(wst[:, q * GQ:(q + 1) * GQ, 1:], bank[plan["mix", f"S{q}"]][:]
                                 .rearrange("p (g k) -> p g k", g=GQ), ACT.Copy).then_inc(*scal.step("mix", f"S{q}"))
                    act.wait_ge(*scal.after("mix", b, f"S{q}"))
                    exchange(dt_[q][:], wst[:, q * GQ:(q + 1) * GQ, 1:], turned_in[q])

                def gate(i):
                    act.wait_ge(*tensor.after("mix", b, f"gl{i}"))
                    dst = (sg_c if i < KD else sg_s)[:, i % KD, :]
                    s.activation(dst, bank[plan["mix", f"gl{i}"]][:], ACT.Sigmoid).then_inc(*scal.step("mix", f"gl{i}"))

                for i in R(GX):
                    gate(i)
                for q in R(NQ):
                    act.wait_ge(*vec.after("mix", b, f"sc{(q + 1) * GQ - 1}"))
                    exchange(dt_[q][:], wst[:, q * GQ:(q + 1) * GQ, 0:NC], turned_in[q])
                act.wait_ge(*vec.after("mix", b, "last"))
                exchange(ctmp[:], carry[:], carry_in)
                for i in R(GX, GY):
                    gate(i)
                for q in R(NQ):
                    act.wait_ge(*tensor.after("mix", b, f"Y{q}"))
                    s.activation(u8[:, q * GQ:(q + 1) * GQ, :], bank[plan["mix", f"Y{q}"]][:]
                                 .rearrange("p (g k) -> p g k", g=GQ), ACT.Copy).then_inc(*scal.step("mix", f"Y{q}"))
                    if q == NQ - 1:
                        act.wait_ge(*scal.after("mix", b, f"Y{q}"))
                        for t in R(T):
                            act.dma_start(ys_d[:, t, :].rearrange("(g h) c -> h g c", h=HG),
                                          u8[t * HG:(t + 1) * HG, :, :]).then_inc(y_out, 16)
                    gate(GY + q)
                act.wait_ge(y_out, 16 * T * (b + 1))
                act.dma_start(yz[:], ys_d.rearrange("(m p) s c -> p m s c", p=P)).then_inc(yz_in, 16)
                load_xs(next_x, row)
                for i in R(TT):
                    act.wait_ge(x2_out[i], 1 + 16 * 2 * b)
                    act.dma_start(xr[i][:], x_d[bass.ds(b * TB + i * P, P), 0:HALF]).then_inc(xr_in[i], 16)
                for i in R(GY + NQ, 2 * KD - 2):
                    gate(i)
                act.wait_ge(yz_in, 16 * (b + 1))
                for m in R(KS):
                    for dst, step in ((ys_hi[:, m, :], f"gh{m}"), (tr[m][:], f"ge{m}")):
                        s.activation(dst.rearrange("p (c s) -> p c s", s=T),
                                     yz[:, m, :, :].rearrange("p s c -> p c s"), ACT.Gelu_apprx_tanh)\
                            .then_inc(*scal.step("mix", step))
                gate(2 * KD - 2)
                gate(2 * KD - 1)

                def gate_b(p):
                    for m in pair(p):
                        act.wait_ge(*tensor.after("mix", b, f"zb{m}"))
                        act.wait_ge(*vec.after("mix", b, f"ms{m - 2}" if p else f"ysl{m}"))
                        s.activation(tr[m % 2][:], bank[plan["mix", f"zb{m}"]][:], ACT.Sigmoid)\
                            .then_inc(*scal.step("mix", f"zb{m}"))

                gate_b(0)
                for m in R(KC):
                    act.wait_ge(*vec.after("mix", b, f"cen{m}"))
                    s.activation(sq[:, m, :], yc[:, m, :], ACT.Square).then_inc(*scal.step("mix", f"sq{m}"))
                gate_b(1)
                act.wait_ge(*tensor.after("mix", b, "ln2"))
                s.activation(dt_[2][:], bank[plan["mix", "ln2"]][:], ACT.Sqrt, bias=eps1[:, 0:1])\
                    .then_inc(*scal.step("mix", "lsd"))
                norm_stats("mix", b, 64 * (b + 2))
                gate_b(2)
                for m in R(KC):
                    act.wait_ge(*vec.after("mix", b, f"nm{m}"))
                    act.wait_ge(*vec.after("mix", b, f"ysl{2 + m}" if m < 2 else f"ynl{m - 2}"))
                    for dst, step in ((yn_hi[:, m, :], f"sh{m}"), (tr[2 + m % 2][:], f"si{m}")):
                        s.activation(dst, yc[:, m, :], ACT.Silu, scale=cvec[:, 1, m:m + 1],
                                     bias=cvec[:, 2, m:m + 1]).then_inc(*scal.step("mix", step))
                gate_b(3)
                for k in R(KD):
                    h_tile("mix", b, k, k % 4, which,
                           vec.after("mix", b, f"hl{k - 4}" if k >= 4 else f"ms{6 + k}" if k < 2 else f"ynl{k}"))
                for f in R(2):
                    for i in R(TT):
                        act.wait_ge(*vec.after("mix", b, f"ob{f}{i}"))
                        act.dma_start(x2_d[bass.ds(b * TB + i * P, P), f * HALF:(f + 1) * HALF], xr[i][:])\
                            .then_inc(x2_out[i], 16)
                    if f == 0:
                        for i in R(TT):
                            act.wait_ge(x2_out[i], 1 + 16 * (2 * b + 1))
                            act.dma_start(xr[i][:], x_d[bass.ds(b * TB + i * P, P), HALF:]).then_inc(xr_in[i], 16)

            with act.Fori(0, NB - 1) as b:
                mixers(b, x_d, (b + 1) * TB, 0)
            for i in R(TT):
                act.wait_ge(x2_out[i], 1 + 16 * 2)
            scal.again("mix")
            mixers(NB - 1, x2_d, 0, 1)
            for i in R(TT):
                act.wait_ge(x2_out[i], 1 + 16 * 2 * NB)
            act.dma_start(fgb[:], final_g.partition_broadcast(P)).then_inc(fg_in, 16)

            with act.Fori(0, NB) as b:
                act.wait_ge(final_out, 1 + 64 * b)
                act.dma_start(x3[:], x2_d[bass.ds(b * TB, TB), :].rearrange("(i p) d -> p i d", p=P))\
                    .then_inc(x3_in, 16)
                load_xs(x2_d, ((b + 1) % NB) * TB)
                with act.Fori(0, FI) as it:
                    for j in R(2):
                        act.wait_ge(*tensor.after("ffn", b, f"fg{j}", it))
                        act.wait_ge(*hidden.before("ffn", b, f"fm{j}", it))
                        s.activation(tr[j][:], bank[plan["ffn", f"fg{j}"]][:], ACT.Silu)\
                            .then_inc(*silu.step("ffn", f"fs{j}"))
                norm_stats("ffn", b, 64 * (b + NB + 2))
                for k in R(KD):
                    h_tile("ffn", b, k, k % 4, 1, vec.after("ffn", b, f"hl{k - 4}") if k >= 4 else
                           hidden.after("ffn", b, "fm1", FI - 1))
                for i in R(TT):
                    act.wait_ge(*vec.after("ffn", b, f"pb1{i}"))
                    act.wait_ge(*scal.after("ffn", b, f"fq{i - 1}" if i else "nsd"))
                    s.activation(junk[:], x3[:, i, :], ACT.Square, accum_out=ss[:, i:i + 1])\
                        .then_inc(*scal.step("ffn", f"fq{i}"))
                act.wait_ge(*vec.after("ffn", b, "fms"))
                s.activation(sd[:], ss[:], ACT.Sqrt).then_inc(*scal.step("ffn", "fsd"))
                for i in R(TT):
                    act.wait_ge(*vec.after("ffn", b, f"fx{i}"))
                    act.dma_start(out_d[bass.ds(b * TB + i * P, P), :], x3[:, i, :]).then_inc(final_out, 16)
            act.wait_ge(final_out, 1 + 64 * NB)

        @block.tensor
        def _(pe):
            t = nc.tensor
            pe.wait_ge(consts, 6)
            pe.wait_ge(vectors_in, mark["vectors"])
            for n, src in enumerate((nat_a, nat_v, nat_w)):
                rows = src.shape[0]
                t.transpose(bank[n][:, 0:rows], src[:], ident[0:rows, 0:rows]).then_inc(*tensor.step("pro", f"v{n}"))

            def modulation(lo, hi):
                for n in R(lo, hi):
                    who, kind, half, rows = SLABS[n]
                    if who != "pe":
                        continue
                    pe.wait_ge(ada_in[n % ADA], 16 * (n // ADA + 1))
                    for j in R(KD // 2):
                        k = rows * KD // 2 + j
                        if kind == 2:
                            ins = t.matmul(bank[(4, 7)[half]][:], cbc[:, k, :], ada[n % ADA][:, j, :],
                                           start=(k == 0), stop=(k == KD - 1))
                        else:
                            r = 2 * (kind % 3) + half
                            ins = t.matmul(bank[5][0:4, :], zc[:, k, 3 - r:7 - r], ada[n % ADA][:, j, :],
                                           start=(r == 0 and k == 0), stop=(r == 3 and k == KD - 1))
                    ins.then_inc(*tensor.step("pro", f"ada{n}"))

            def transposes(phase, b, k, free=True):
                if free:
                    pe.wait_ge(*bank_free(phase, b, f"h{k}"))
                if k == 0:
                    pe.wait_ge(*vec.after(phase, b, f"nx{TT - 1}"))
                for i in R(TT):
                    ins = t.transpose(bank[plan[phase, f"h{k}"]][:, i * P:(i + 1) * P], xs[:, i, k * P:(k + 1) * P],
                                      ident[:])
                ins.then_inc(*tensor.step(phase, f"h{k}"))

            pe.wait_ge(pro_v, mark["zc"])
            modulation(0, first_gate)

            def modulation_by_feature(which):
                pe.wait_ge(pro_v, mark[f"modrow{which}"])
                for j in R(4):
                    ins = t.transpose(bank[6][:, 4 * j:4 * j + 4], modrow[:, j * P:(j + 1) * P], ident[0:4, 0:4])
                ins.then_inc(*tensor.step("pro", ("mt", "mt2")[which]))

            modulation_by_feature(0)
            pe.wait_ge(small_in, mark["small"])
            for n in R(2):
                for j in R(4):
                    ins = t.transpose(bank[3 + n][:, j * P:(j + 1) * P], cx[:, n, j, :], ident[:])
                ins.then_inc(*tensor.step("pro", f"ct{n}"))
            pe.wait_ge(pro_v, mark["cc"])
            for k in R(KD):
                if k >= 4:
                    pe.wait_ge(*scal.after("pro", 0, f"h{k - 4}"))
                transposes("pro", 0, k, free=False)
            pe.wait_ge(pro_v, mark["cbc"])
            modulation(first_gate, last_slab(3) + 1)
            pe.wait_ge(pro_v, mark["wm"])
            for n in R(8):
                pe.wait_ge(*scal.after("pro", 0, f"wt{n - 4}" if n >= 4 else f"h{4 + n}"))
                for j in R(4):
                    ins = t.transpose(bank[n % 4][:, j * P:(j + 1) * P],
                                      wm[:, 4 * n + j, :, :].rearrange("p s h -> p (s h)"), ident[:])
                ins.then_inc(*tensor.step("pro", f"wt{n}"))
            modulation(last_slab(3) + 1, len(SLABS))
            modulation_by_feature(1)
            pe.wait_ge(acc_done, 4)
            pe.wait_ge(pro_v, mark["scale1"])
            for h in R(2):
                t.matmul(bank[6 + h][:], ones[:], acc[:, h, :], start=True, stop=True)\
                    .then_inc(*tensor.step("pro", f"sg{h}"))
            pe.wait_ge(pro_v, mark["vm"])
            for n in R(8):
                pe.wait_ge(*scal.after("pro", 0, f"kk{n - 4}" if n >= 4 else f"wt{4 + n}"))
                for j in R(4):
                    g = 4 * n + j
                    ins = t.matmul(bank[n % 4][0:HG, j * P:(j + 1) * P], b1[:, g, :],
                                   vm[:, g, 0:T, :].rearrange("p s h -> p (s h)"), start=True, stop=True)
                ins.then_inc(*tensor.step("pro", f"kk{n}"))
            pe.wait_ge(*scal.after("pro", 0, "kk7"))
            pe.wait_ge(*vec.after("pro", 0, f"hl{KD - 1}"))

            def three(dst, wh, wl, xh, xl, first, last):
                t.matmul(dst, wh, xh, start=first, stop=False)
                t.matmul(dst, wh, xl, start=False, stop=False)
                return t.matmul(dst, wl, xh, start=False, stop=last)

            def mixers(b):
                chunk = [0]

                def next_chunk():
                    chunk[0] += 1
                    pe.wait_ge(split_done, RAW + b * NMIX + chunk[0])
                    return (chunk[0] - 1) % SPL

                def layer(name, ws, first_col, width, kt, xh, xl):
                    pe.wait_ge(*bank_free("mix", b, name))
                    hi = w_hi[ws][:].rearrange("p (k n) -> p k n", n=width)
                    lo = w_lo[ws][:].rearrange("p (k n) -> p k n", n=width)
                    for k in R(kt):
                        ins = three(bank[plan["mix", name]][:], hi[:, k, first_col:first_col + P],
                                    lo[:, k, first_col:first_col + P], xh[:, k, :], xl[:, k, :], k == 0, k == kt - 1)
                    ins.then_inc(*tensor.step("mix", name))

                def gates(*tiles):
                    for i in tiles:
                        layer(f"gl{i}", next_chunk(), 0, P, KD, h_hi, h_lo)

                ssm_use = [0]

                def next_ssm():
                    n = ssm_use[0]
                    ssm_use[0] += 1
                    pe.wait_ge(ssm_in[n % 3], 16 * (4 * b + n // 3 + 1))
                    return ssm_m[n % 3]

                for m in R(KS):
                    layer(f"us{m}", next_chunk(), 0, P, KD, h_hi, h_lo)
                for m in R(KC):
                    layer(f"ua{m}", next_chunk(), 0, P, KD, h_hi, h_lo)
                    layer(f"ug{m}", next_chunk(), 0, P, KD, h_hi, h_lo)
                pe.wait_ge(pro_v, mark["g2b"])
                pe.wait_ge(u8_in, 16 * T * (b + 1))
                for q in R(NQ):
                    mat = next_ssm()[:].rearrange("p (g n) -> p g n", g=GQ)
                    pe.wait_ge(*bank_free("mix", b, f"S{q}"))
                    for j in R(GQ):
                        ins = t.matmul(bank[plan["mix", f"S{q}"]][:, j * NC:(j + 1) * NC], mat[:, j, :],
                                       u8[:, q * GQ + j, :], start=True, stop=True)
                    ins.then_inc(*tensor.step("mix", f"S{q}"))
                gates(*R(0, GY))
                for q in R(NQ):
                    pe.wait_ge(*vec.after("mix", b, f"Ds{q}"))
                    pe.wait_ge(*bank_free("mix", b, f"Y{q}"))
                    for half in R(2):
                        mat = next_ssm()[:].rearrange("p (g a n) -> p g a n", g=GQ // 2, a=2)
                        for j in R(GQ // 2):
                            g = q * GQ + half * (GQ // 2) + j
                            dst = bank[plan["mix", f"Y{q}"]][:, (g % GQ) * NC:(g % GQ + 1) * NC]
                            t.matmul(dst, mat[:, j, 0, :], wst[:, g, 0:NC], start=True, stop=False)
                            ins = t.matmul(dst, mat[:, j, 1, :], u8[:, g, :], start=False, stop=True)
                    ins.then_inc(*tensor.step("mix", f"Y{q}"))
                    gates(GY + q)
                gates(*R(GY + NQ, 2 * KD))

                def two_tiles(name, p, xh, xl):
                    slot = next_chunk()
                    for j in R(2):
                        layer(f"{name}{2 * p + j}", slot, j * P, 2 * P, KC, xh, xl)

                def mean(name, src):
                    pe.wait_ge(*bank_free("mix", b, name))
                    t.matmul(bank[plan["mix", name]][:], mean_w[:], src, start=True, stop=True)\
                        .then_inc(*tensor.step("mix", name))

                pe.wait_ge(*vec.after("mix", b, f"ysl{KS - 1}"))
                for p in R(KD // 2):
                    two_tiles("za", p, ys_hi, ys_lo)
                    two_tiles("zb", p, ys_hi, ys_lo)
                    if p == 0:
                        pe.wait_ge(*vec.after("mix", b, "s13"))
                        mean("ln1", dt_[2][:])
                    if p == 1:
                        pe.wait_ge(*vec.after("mix", b, "s23"))
                        mean("ln2", dt_[3][:])
                for p in R(KD // 2):
                    for k in pair(p):
                        transposes("mix", b, k)
                    if p == 0:
                        pe.wait_ge(*vec.after("mix", b, f"ynl{KC - 1}"))
                    two_tiles("cp", p, yn_hi, yn_lo)

                def out_half(phase, b, f, kt, xh, xl, pre, step):
                    for j in R(kt // 2):
                        slot = next_chunk()
                        if f == 0:
                            pe.wait_ge(*vec.after("mix", b, f"ml{2 * j + 1}"))
                        for kk in R(2):
                            k = 2 * j + kk
                            for i in R(TT):
                                if k == 0:
                                    pe.wait_ge(*bank_free(phase, b, f"{pre}{f}{i}"))
                                dst = bank[plan[phase, f"{pre}{f}{i}"]][:]
                                cols = slice(i * P, (i + 1) * P)
                                wcols = slice(kk * HALF, (kk + 1) * HALF)
                                t.matmul(dst, xh[:, k, cols], w_hi[slot][:, wcols], start=(k == 0), stop=False)
                                t.matmul(dst, xl[:, k, cols], w_hi[slot][:, wcols], start=False, stop=False)
                                ins = t.matmul(dst, xh[:, k, cols], w_lo[slot][:, wcols], start=False,
                                               stop=(k == kt - 1))
                                if k == kt - 1:
                                    ins.then_inc(*tensor.step(phase, f"{pre}{f}{i}"))
                        if j < kt // 2 - 1:
                            ins.then_inc(*tensor.step(phase, step(f, j)))

                for f in R(2):
                    out_half("mix", b, f, KD, m_hi, m_lo, "o", lambda f, j: f"oc{f}{j}")
                pe.wait_ge(*vec.after("mix", b, f"hl{KD - 1}"))
                assert chunk[0] == NMIX

            with pe.Fori(0, NB - 1) as b:
                mixers(b)
            tensor.again("mix")
            mixers(NB - 1)
            pe.wait_ge(*vec.after("mix", NB - 1, f"oa0{TT - 1}"))

            with pe.Fori(0, NB) as b:
                with pe.Fori(0, FI) as it:
                    for n, name in enumerate(pe_loop):
                        pe.wait_ge(split_done, RAW + NB * NMIX + b * NFFN + it * 4 + n + 1)
                        pe.wait_ge(*bank_free("ffn", b, name, it))
                        ws = n % SPL
                        for k in R(KD):
                            cols = slice(k * P, (k + 1) * P)
                            ins = three(bank[plan["ffn", name]][:], w_hi[ws][:, cols], w_lo[ws][:, cols],
                                        h_hi[:, k, :], h_lo[:, k, :], k == 0, k == KD - 1)
                        ins.then_inc(*tensor.step("ffn", name))
                chunk = [2 * KF]

                def next_chunk():
                    chunk[0] += 1
                    pe.wait_ge(split_done, RAW + NB * NMIX + b * NFFN + chunk[0])
                    return (chunk[0] - 1) % SPL

                def next_h(f, j):
                    if f == 0 and 1 <= j <= KD:
                        transposes("ffn", b, j - 1)

                for f in R(2):
                    for j in R(KF // 2):
                        slot = next_chunk()
                        if f == 0:
                            pe.wait_ge(*hidden.after("ffn", b, "fl1", j))
                        for kk in R(2):
                            k = 2 * j + kk
                            for i in R(TT):
                                if k == 0:
                                    pe.wait_ge(*bank_free("ffn", b, f"p{f}{i}"))
                                dst = bank[plan["ffn", f"p{f}{i}"]][:]
                                cols = slice(i * P, (i + 1) * P)
                                wcols = slice(kk * HALF, (kk + 1) * HALF)
                                t.matmul(dst, hid_hi[:, k, cols], w_hi[slot][:, wcols], start=(k == 0), stop=False)
                                t.matmul(dst, hid_lo[:, k, cols], w_hi[slot][:, wcols], start=False, stop=False)
                                ins = t.matmul(dst, hid_hi[:, k, cols], w_lo[slot][:, wcols], start=False,
                                               stop=(k == KF - 1))
                                if k == KF - 1:
                                    ins.then_inc(*tensor.step("ffn", f"p{f}{i}"))
                        if j < KF // 2 - 1:
                            ins.then_inc(*tensor.step("ffn", f"fc{f}_{j}"))
                        next_h(f, j)
                pe.wait_ge(*vec.after("ffn", b, f"hl{KD - 1}"))
                assert chunk[0] == NFFN

        @block.gpsimd
        def _(pool):
            g = nc.gpsimd
            g.memset(ident[:], 0.0).then_inc(consts, 1)
            pool.wait_ge(consts, 1)
            g.affine_select(out=ident[:], in_=ident[:], compare_op=ALU.not_equal, fill=1.0, base=0,
                            pattern=[[-1, P]], channel_multiplier=1).then_inc(consts, 1)
            g.iota(iota_i[:], pattern=[[1, NC + 1]], base=0, channel_multiplier=0).then_inc(consts, 1)
            g.memset(sign[:], 1.0).then_inc(split_done, 1)
            g.memset(nsign[:], -1.0).then_inc(split_done, 1)
            g.memset(zero1[:], 0.0).then_inc(split_done, 1)
            g.memset(eps1[:], EPS).then_inc(x2_out[0], 1)
            g.memset(half_pi[:], float(np.pi / 2)).then_inc(x2_out[1], 1)
            g.memset(mean_w[:], 1.0 / CW).then_inc(x2_out[2], 1)
            g.memset(carry[:], 0.0).then_inc(x2_out[3], 1)
            g.memset(ones[:], 1.0).then_inc(final_out, 1)
            g.memset(zc[:], 0.0).then_inc(silu.sem, 2)
            g.memset(acc[:], 0.0).then_inc(hidden.sem, 6)
            g.memset(uc[:, :, 0:HALO], 0.0).then_inc(consts, 1)
            pool.wait_ge(consts, 4)
            g.memset(sign[0:NST, :], -1.0).then_inc(vec.sem, 8)
            g.memset(nsign[0:NST, :], 1.0).then_inc(consts, 1)
            g.tensor_copy(iota_f[:], iota_i[:]).then_inc(consts, 1)

            pool.wait_ge(*scal.after("pro", 0, "cs"))
            pool.wait_ge(consts, 6)
            mine = [n for n in R(len(SLABS)) if SLABS[n][0] == "pool"]
            ops = 0

            def add(out, a, b_):
                pool.wait_ge(acc_link, ops)
                return g.tensor_tensor(out, a, b_, ALU.add)

            for i, n in enumerate(mine):
                _, kind, half, rows = SLABS[n]
                slab, a = ada[n % ADA], acc[:, half, :]
                pool.wait_ge(ada_in[n % ADA], 16 * (n // ADA + 1))
                g.tensor_tensor(slab[:], slab[:], cact[:, rows * KD // 2:(rows + 1) * KD // 2].unsqueeze(2)
                                .broadcast_to([P, KD // 2, HALF]), ALU.mult).then_inc(acc_link, 1)
                ops += 1
                for j in R(1 if rows == 0 else 0, KD // 2):
                    ins = add(a, slab[:, j - 1, :] if j == 1 and rows == 0 else a, slab[:, j, :])
                    if j < KD // 2 - 1:
                        ins.then_inc(acc_link, 1)
                        ops += 1
                ins.then_inc(acc_done, 1)
                pool.wait_ge(acc_done, i + 1)
            pool.wait_ge(*tensor.after("pro", 0, f"h{KD - 1}"))
            g.memset(kst[:, :, 0:T - 1, :], 0.0).then_inc(acc_done, 1)

            zeros = zero1[:, 0:1].broadcast_to([P, CH])

            with pool.Fori(0, NB) as b:
                for n in R(NMIX):
                    first = b * NMIX
                    pool.wait_ge(raw_in[n % RAW], 16 * (b * (NMIX // RAW) + n // RAW + 1))
                    if n >= SPL:
                        pool.wait_ge(*chunk_used("mix", b, n - SPL + 1))
                    else:
                        s_, v_ = tensor.before("mix", b, chunk_no["mix", NMIX - SPL + n + 1], None)
                        pool.wait_ge(s_, v_)
                    src, hi, lo = raw[n % RAW], w_hi[n % SPL], w_lo[n % SPL]
                    g.tensor_tensor(hi[:], src[:], zeros, ALU.add).then_inc(hi_done, 1)
                    pool.wait_ge(hi_done, first + n + 1)
                    g.tensor_tensor(lo[:], src[:], hi[:].bitcast(F32), ALU.subtract).then_inc(split_done, 1)
            with pool.Fori(0, NB) as b:
                for n in R(NFFN):
                    first = NB * NMIX + b * NFFN
                    pool.wait_ge(raw_in[n % RAW], 16 * (NB * NMIX // RAW + b * (NFFN // RAW) + n // RAW + 1))
                    m = n - SPL + 1
                    if m <= 0:
                        s_, v_ = tensor.before("ffn", b, chunk_no["ffn", NFFN + m], None)
                    elif m <= 2 * KF:
                        s_, v_ = tensor.after("ffn", b, pe_loop[(m - 1) % 4], (m - 1) // 4)
                    else:
                        s_, v_ = chunk_used("ffn", b, m)
                    pool.wait_ge(s_, v_)
                    src, hi, lo = raw[n % RAW], w_hi[n % SPL], w_lo[n % SPL]
                    g.tensor_tensor(hi[:], src[:], zeros, ALU.add).then_inc(hi_done, 1)
                    pool.wait_ge(hi_done, first + n + 1)
                    g.tensor_tensor(lo[:], src[:], hi[:].bitcast(F32), ALU.subtract).then_inc(split_done, 1)

        @block.sync
        def _(sp):
            of_pool_so_far = 0
            for n, (who, kind, half, rows) in enumerate(SLABS):
                if n >= ADA and SLABS[n - ADA][0] == "pe":
                    sp.wait_ge(*tensor.after("pro", 0, f"ada{n - ADA}"))
                elif n >= ADA:
                    of_pool_so_far += 1
                    sp.wait_ge(acc_done, of_pool_so_far)
                col = kind * D + half * HALF
                sp.dma_start(ada[n % ADA][:], ada_d[:, rows * KD // 2:(rows + 1) * KD // 2, col:col + HALF])\
                    .then_inc(ada_in[n % ADA], 16)
            sp.wait_ge(*tensor.after("pro", 0, "sg1"))

            def load(n, key, number):
                dst = raw[n % RAW]
                sp.wait_ge(split_done, number + 1)
                if key[0] == "in":
                    d, src = dst[:].rearrange("p (k n) -> p k n", n=P), win_d[:, :, key[1]:key[1] + P]
                elif key[0] in ("proj", "glu"):
                    d = dst[:].rearrange("p (k n) -> p k n", n=2 * P)
                    src = (proj_d if key[0] == "proj" else glu_d)[:, :, key[1]:key[1] + 2 * P]
                elif key[0] == "out":
                    d = dst[:].rearrange("p (k n) -> p k n", n=HALF)
                    src = wout_d[:, 2 * key[2]:2 * key[2] + 2, key[1] * HALF:(key[1] + 1) * HALF]
                elif key[0] == "fin":
                    d, src = dst[:].rearrange("p (k n) -> p k n", n=P), fin_d[:, :, key[1]:key[1] + P]
                else:
                    d = dst[:].rearrange("p (k n) -> p k n", n=HALF)
                    src = fout_d[:, 2 * key[2]:2 * key[2] + 2, key[1] * HALF:(key[1] + 1) * HALF]
                sp.dma_start(d, src).then_inc(raw_in[n % RAW], 16)

            with sp.Fori(0, NB) as b:
                ssm_user = [f"S{q}" for q in R(NQ)] + [f"Y{q}" for q in R(NQ) for _ in R(2)]

                def load_ssm(n):
                    if n >= 3:
                        sp.wait_ge(*tensor.after("mix", b, ssm_user[n - 3]))
                    else:
                        sp.wait_ge(*tensor.start("mix", b))
                    if n < NQ:
                        src = wt_d[:, n * GQ:(n + 1) * GQ, :].rearrange("p g n -> p (g n)")
                    else:
                        m = n - NQ
                        src = vk_d[:, m * GQ // 2:(m + 1) * GQ // 2, :, :].rearrange("p g a n -> p (g a n)")
                    sp.dma_start(ssm_m[n % 3][:], src).then_inc(ssm_in[n % 3], 16)

                ahead = {8: [0, 1, 2], 16: [3], 17: [4, 5, 6], 24: [7, 8], 25: [9, 10], 26: [11]}
                for n, key in enumerate(MIX_CHUNKS):
                    if n == min(ahead):
                        sp.wait_ge(mat_out, 16 * (2 + T))
                    for m in ahead.get(n, []):
                        load_ssm(m)
                    load(n, key, b * NMIX + n)
            with sp.Fori(0, NB) as b:
                base = NB * NMIX + b * NFFN
                for n in R(2 * KF):
                    m, up = n // 2, n % 2
                    load(n, ("fin", up * FF + m * P), base + n)
                for n in R(2 * KF, NFFN):
                    f, j = divmod(n - 2 * KF, KF // 2)
                    load(n, ("fout", f, j), base + n)

        for s_ in (tensor, scal, vec, silu, hidden):
            s_.finished()


INPUTS = ["x", "c", "w_ada", "b_ada", "norm1_g", "w_in", "conv_w", "conv_b", "conv_ln_g", "conv_ln_b",
          "conv_proj", "ssm_a_re", "ssm_a_im", "ssm_b_re", "ssm_b_im", "ssm_c_re", "ssm_c_im",
          "ssm_d", "ssm_log_dt", "ssm_glu", "w_out", "norm2_g", "w_ffn_in", "w_ffn_out", "final_g"]


def kernel(**inputs):
    import concourse.bacc as bacc
    from concourse.bass_utils import run_bass_kernel_spmd

    nc = bacc.Bacc("TRN2", target_bir_lowering=False, num_devices=1, dynamic_dma_scratch_size=1024)
    arrays, args = {}, []
    for name in INPUTS:
        a = np.ascontiguousarray(inputs[name])
        arrays[f"in_{name}"] = a
        args.append(nc.dram_tensor(f"in_{name}", a.shape, mybir.dt.from_np(a.dtype), kind="ExternalInput").ap())
    shape = inputs["x"].shape
    args.append(nc.dram_tensor("out_0", shape, F32, kind="ExternalOutput").ap())
    build(nc, *args)
    result = run_bass_kernel_spmd(nc, [arrays], core_ids=[0])
    return result.results[0]["out_0"]
```
